# Optimizing a Trainium2 kernel written in Bass

```python
import math
import jax, jax.numpy as jnp
from jax import lax
import numpy as np

D_MODEL = 1024
BATCH = 1
SEQ = 256
DEPTH = 2

N_MEM = 256
EPS = 1e-6
DA_HEADS = 8
DA_HEAD_DIM = 64
DA_V_DIM = 2 * DA_HEAD_DIM
DA_WIDTH = DA_HEADS * DA_V_DIM
DA_QK_COLS = DA_HEADS * 2 * DA_HEAD_DIM
DA_LAMBDA_STD = 0.1
Q_BLOCK = 128
SSM_EXPAND = 2
SSM_INNER = SSM_EXPAND * D_MODEL
SSM_HEAD_DIM = 64
SSM_HEADS = SSM_INNER // SSM_HEAD_DIM
SSM_GROUPS = 4
SSM_STATE = 128
SSM_CONV = 5
SSM_CHUNK = 128
SSM_BC_COLS = SSM_GROUPS * SSM_STATE
SSM_CONV_CH = SSM_INNER + 2 * SSM_BC_COLS
SSM_DT_COLS = 2 * SSM_HEADS
DT_MIN = 0.001
DT_MAX = 0.1
XA_HEADS = 4
XA_HEAD_DIM = D_MODEL // XA_HEADS
XA_WIDTH = XA_HEADS * XA_HEAD_DIM
N_BRANCH = 3
GATE_COLS = N_BRANCH * D_MODEL
IN_SIZES = (DA_QK_COLS, DA_QK_COLS, DA_WIDTH, SSM_INNER, SSM_CONV_CH, SSM_DT_COLS, XA_WIDTH, GATE_COLS)
IN_COLS = sum(IN_SIZES)
BRANCH_IN = DA_WIDTH + SSM_INNER + XA_WIDTH
FFN_HIDDEN = -(-8 * D_MODEL // (3 * 256)) * 256

kernel_name = "hybrid_diffattn_bimamba2_memxattn_encoder"

def rms_norm(x, g):
    xf = x.astype(jnp.float32)
    y = xf * lax.rsqrt(jnp.mean(xf * xf, axis=-1, keepdims=True) + EPS)
    return (y * g.astype(jnp.float32)).astype(x.dtype)

def split_cols(t, sizes):
    out, off = [], 0
    for s in sizes:
        out.append(t[..., off:off + s])
        off += s
    return out

def alibi_slopes(n_heads):
    start = 2.0 ** (-8.0 / n_heads)
    return np.array([start ** (i + 1) for i in range(n_heads)], dtype=np.float32)

def diff_attention(q, k, v, lam, lambda_init, sub_g):
    b, s_len, h, _, dh = q.shape
    nblk = s_len // Q_BLOCK
    slopes = jnp.asarray(alibi_slopes(h))
    kpos = jnp.arange(s_len)
    qb = jnp.moveaxis((q * (dh ** -0.5)).reshape(b, nblk, Q_BLOCK, h, 2, dh), 1, 0)
    starts = jnp.arange(nblk) * Q_BLOCK

    def block(args):
        qi, start = args
        sc = jnp.einsum('bqhcd,bkhcd->bhcqk', qi, k, preferred_element_type=jnp.float32)
        qpos = start + jnp.arange(Q_BLOCK)
        dist = jnp.abs(qpos[:, None] - kpos[None, :]).astype(jnp.float32)
        sc = sc - slopes[None, :, None, None, None] * dist
        p = jax.nn.softmax(sc, axis=-1)
        attn = p[:, :, 0] - lam * p[:, :, 1]
        return jnp.einsum('bhqk,bkhe->bqhe', attn.astype(v.dtype), v)

    o = lax.map(block, (qb, starts))
    o = jnp.moveaxis(o, 0, 1).reshape(b, s_len, h, 2 * dh)
    o = rms_norm(o, sub_g) * (1.0 - lambda_init)
    return o.reshape(b, s_len, h * 2 * dh)

def segsum_exp(a):
    n = a.shape[-1]
    cs = jnp.cumsum(a, axis=-1)
    diff = cs[..., :, None] - cs[..., None, :]
    mask = jnp.tril(jnp.ones((n, n), dtype=bool))
    return jnp.exp(jnp.where(mask, diff, -jnp.inf))

def ssd_scan(x, dt, A, Bm, Cm):
    f32 = jnp.float32
    b, l, h, p = x.shape
    g, n = Bm.shape[-2:]
    r = h // g
    c = l // SSM_CHUNK
    q_len = SSM_CHUNK
    dtf = dt.astype(f32)
    xdt = (x.astype(f32) * dtf[..., None]).reshape(b, c, q_len, g, r, p)
    a = (dtf * A.astype(f32)).reshape(b, c, q_len, g, r).transpose(0, 1, 3, 4, 2)
    Bc = Bm.astype(f32).reshape(b, c, q_len, g, n)
    Cc = Cm.astype(f32).reshape(b, c, q_len, g, n)
    a_cs = jnp.cumsum(a, axis=-1)
    cb = jnp.einsum('bclgn,bcsgn->bcgls', Cc, Bc)
    m = cb[:, :, :, None] * segsum_exp(a)
    y_diag = jnp.einsum('bcgrls,bcsgrp->bclgrp', m, xdt)
    decay_states = jnp.exp(a_cs[..., -1:] - a_cs).transpose(0, 1, 4, 2, 3)
    states = jnp.einsum('bclgn,bclgrp->bcgrpn', Bc, xdt * decay_states[..., None])
    chunk_decay = jnp.exp(a_cs[..., -1])

    def step(carry, inp):
        st, dec = inp
        return carry * dec[..., None, None] + st, carry

    init = jnp.zeros((b, g, r, p, n), f32)
    _, prev = lax.scan(step, init, (jnp.moveaxis(states, 1, 0), jnp.moveaxis(chunk_decay, 1, 0)))
    prev = jnp.moveaxis(prev, 0, 1)
    decay_out = jnp.exp(a_cs).transpose(0, 1, 4, 2, 3)
    y_off = jnp.einsum('bclgn,bcgrpn->bclgrp', Cc, prev) * decay_out[..., None]
    return (y_diag + y_off).reshape(b, l, h, p).astype(x.dtype)

def mamba2_bidir(z, xbc, dt_raw, conv_w, conv_b, dt_bias, A_log, D_skip, norm_g):
    b, l, ch = xbc.shape
    pad = SSM_CONV // 2
    xbc = lax.conv_general_dilated(xbc, conv_w[:, None, :], window_strides=(1,),
                                   padding=[(pad, pad)], dimension_numbers=('NWC', 'WIO', 'NWC'),
                                   feature_group_count=ch) + conv_b
    xbc = jax.nn.silu(xbc)
    xs, Bm, Cm = split_cols(xbc, (SSM_INNER, SSM_BC_COLS, SSM_BC_COLS))
    xs = xs.reshape(b, l, SSM_HEADS, SSM_HEAD_DIM)
    Bm = Bm.reshape(b, l, SSM_GROUPS, SSM_STATE)
    Cm = Cm.reshape(b, l, SSM_GROUPS, SSM_STATE)
    dt = jax.nn.softplus(dt_raw.reshape(b, l, 2, SSM_HEADS).astype(jnp.float32)
                         + dt_bias.astype(jnp.float32))
    A = -jnp.exp(A_log.astype(jnp.float32))
    y_f = ssd_scan(xs, dt[:, :, 0], A[0], Bm, Cm)
    fl = lambda t: jnp.flip(t, axis=1)
    y_b = fl(ssd_scan(fl(xs), fl(dt[:, :, 1]), A[1], fl(Bm), fl(Cm)))
    y = y_f + y_b + xs * D_skip[:, None]
    y = y.reshape(b, l, SSM_INNER) * jax.nn.silu(z)
    y = rms_norm(y.reshape(b, l, SSM_GROUPS, SSM_INNER // SSM_GROUPS),
                 norm_g.reshape(SSM_GROUPS, SSM_INNER // SSM_GROUPS))
    return y.reshape(b, l, SSM_INNER)

def mem_cross_attention(q, mem_n, w_kv):
    b, m, _ = mem_n.shape
    k, v = split_cols(mem_n @ w_kv, (XA_WIDTH, XA_WIDTH))
    k = k.reshape(b, m, XA_HEADS, XA_HEAD_DIM)
    v = v.reshape(b, m, XA_HEADS, XA_HEAD_DIM)
    sc = jnp.einsum('bqhd,bkhd->bhqk', q * (XA_HEAD_DIM ** -0.5), k, preferred_element_type=jnp.float32)
    p = jax.nn.softmax(sc, axis=-1)
    o = jnp.einsum('bhqk,bkhd->bqhd', p.astype(v.dtype), v)
    return o.reshape(b, q.shape[1], XA_WIDTH)

def setup_inputs(seed: int = 0) -> dict:
    key = jax.random.key(seed)
    ks = jax.random.split(key, 24)
    f32 = jnp.float32

    def nrm(k, shape, scale):
        return jax.random.normal(k, shape, f32) * scale

    def gain(k, shape):
        return 1.0 + 0.02 * jax.random.normal(k, shape, f32)

    res_scale = (2.0 * DEPTH) ** -0.5
    dt0 = jnp.exp(jax.random.uniform(ks[10], (DEPTH, 2, SSM_HEADS), f32, math.log(DT_MIN), math.log(DT_MAX)))
    dt_bias = dt0 + jnp.log(-jnp.expm1(-dt0))
    A_log = jnp.log(jax.random.uniform(ks[11], (DEPTH, 2, SSM_HEADS), f32, 1.0, 16.0))
    return {
        "x": nrm(ks[0], (BATCH, SEQ, D_MODEL), 1.0),
        "mem": nrm(ks[1], (BATCH, N_MEM, D_MODEL), 1.0),
        "mix_norm_g": gain(ks[2], (DEPTH, D_MODEL)),
        "w_in": nrm(ks[3], (DEPTH, D_MODEL, IN_COLS), D_MODEL ** -0.5),
        "da_lambda_q1": nrm(ks[4], (DEPTH, DA_HEAD_DIM), DA_LAMBDA_STD),
        "da_lambda_k1": nrm(ks[5], (DEPTH, DA_HEAD_DIM), DA_LAMBDA_STD),
        "da_lambda_q2": nrm(ks[6], (DEPTH, DA_HEAD_DIM), DA_LAMBDA_STD),
        "da_lambda_k2": nrm(ks[7], (DEPTH, DA_HEAD_DIM), DA_LAMBDA_STD),
        "da_subln_g": gain(ks[8], (DEPTH, DA_V_DIM)),
        "ssm_conv_w": nrm(ks[9], (DEPTH, SSM_CONV, SSM_CONV_CH), SSM_CONV ** -0.5),
        "ssm_conv_b": nrm(ks[12], (DEPTH, SSM_CONV_CH), 0.02),
        "ssm_dt_bias": dt_bias,
        "ssm_A_log": A_log,
        "ssm_D": gain(ks[13], (DEPTH, SSM_HEADS)),
        "ssm_norm_g": gain(ks[14], (DEPTH, SSM_INNER)),
        "mem_norm_g": gain(ks[15], (DEPTH, D_MODEL)),
        "w_mem_kv": nrm(ks[16], (DEPTH, D_MODEL, 2 * XA_WIDTH), D_MODEL ** -0.5),
        "w_branch": nrm(ks[17], (DEPTH, BRANCH_IN, D_MODEL), D_MODEL ** -0.5),
        "w_out": nrm(ks[18], (DEPTH, D_MODEL, D_MODEL), D_MODEL ** -0.5 * res_scale),
        "ffn_norm_g": gain(ks[19], (DEPTH, D_MODEL)),
        "w_ffn_in": nrm(ks[20], (DEPTH, D_MODEL, 2 * FFN_HIDDEN), D_MODEL ** -0.5),
        "w_ffn_out": nrm(ks[21], (DEPTH, FFN_HIDDEN, D_MODEL), FFN_HIDDEN ** -0.5 * res_scale),
        "final_norm_g": gain(ks[22], (D_MODEL,)),
    }

def reference(x, mem, mix_norm_g, w_in, da_lambda_q1, da_lambda_k1, da_lambda_q2, da_lambda_k2,
              da_subln_g, ssm_conv_w, ssm_conv_b, ssm_dt_bias, ssm_A_log, ssm_D, ssm_norm_g,
              mem_norm_g, w_mem_kv, w_branch, w_out, ffn_norm_g, w_ffn_in, w_ffn_out, final_norm_g):
    b, s_len, d = x.shape
    for i in range(DEPTH):
        h = rms_norm(x, mix_norm_g[i])
        proj = h @ w_in[i]
        da_q, da_k, da_v, s_z, s_xbc, s_dt, xa_q, gates = split_cols(proj, IN_SIZES)

        lambda_init = 0.8 - 0.6 * math.exp(-0.3 * i)
        lam = (jnp.exp(jnp.sum(da_lambda_q1[i] * da_lambda_k1[i]).astype(jnp.float32))
               - jnp.exp(jnp.sum(da_lambda_q2[i] * da_lambda_k2[i]).astype(jnp.float32))
               + lambda_init)
        y_da = diff_attention(da_q.reshape(b, s_len, DA_HEADS, 2, DA_HEAD_DIM),
                              da_k.reshape(b, s_len, DA_HEADS, 2, DA_HEAD_DIM),
                              da_v.reshape(b, s_len, DA_HEADS, DA_V_DIM),
                              lam, lambda_init, da_subln_g[i])

        y_ssm = mamba2_bidir(s_z, s_xbc, s_dt, ssm_conv_w[i], ssm_conv_b[i], ssm_dt_bias[i],
                             ssm_A_log[i], ssm_D[i], ssm_norm_g[i])

        y_xa = mem_cross_attention(xa_q.reshape(b, s_len, XA_HEADS, XA_HEAD_DIM),
                                   rms_norm(mem, mem_norm_g[i]), w_mem_kv[i])

        g = jax.nn.sigmoid(gates.astype(jnp.float32)).astype(x.dtype).reshape(b, s_len, N_BRANCH, d)
        wb_da, wb_ssm, wb_xa = split_cols(w_branch[i].T, (DA_WIDTH, SSM_INNER, XA_WIDTH))
        merged = (g[:, :, 0] * (y_da @ wb_da.T)
                  + g[:, :, 1] * (y_ssm @ wb_ssm.T)
                  + g[:, :, 2] * (y_xa @ wb_xa.T))
        x = x + merged @ w_out[i]

        h = rms_norm(x, ffn_norm_g[i])
        gate, up = split_cols(h @ w_ffn_in[i], (FFN_HIDDEN, FFN_HIDDEN))
        x = x + (jax.nn.silu(gate) * up) @ w_ffn_out[i]
    return rms_norm(x, final_norm_g)


_drawn_inputs = setup_inputs


def setup_inputs(seed=0):
    import zlib

    import numpy as np

    out = dict(_drawn_inputs(seed))
    spreads = {}
    factors = {'mix_norm_g': 2.933,
     'da_lambda_q1': 4.346,
     'da_lambda_q2': 2.865,
     'da_lambda_k2': 2.897,
     'da_subln_g': 8.0,
     'ssm_conv_b': 3.437,
     'ssm_D': 200.0,
     'ssm_norm_g': 5.269,
     'mem_norm_g': 8.0,
     'ffn_norm_g': 5.303,
     'final_norm_g': 22.566}
    for name, (base, spread) in spreads.items():
        noise = np.random.default_rng([zlib.crc32(name.encode()), seed]).standard_normal(out[name].shape)
        drawn = base * np.exp(spread * noise) if base else spread * noise
        out[name] = __import__('jax').numpy.asarray(drawn.astype(out[name].dtype))
    for name, factor in factors.items():
        out[name] = (out[name] * factor).astype(out[name].dtype)
    return out
```

```python
import math
from contextlib import ExitStack

import concourse.bass as bass
from concourse import mybir

F32 = mybir.dt.float32
F32R = mybir.dt.float32r
ACT = mybir.ActivationFunctionType
ALU = mybir.AluOpType
AX = mybir.AxisListType

P = 128
D = 1024
T = 256
NT = T // P
KT = D // P
DEPTH = 2
EPS = 1e-6
HEADS, HALF = 8, 4
DH = 64
XH = 4
SH, SG = 32, 4
HPG = SH // SG
INNER = 2 * D
CONV = 5
FFN = 2816
FT = FFN // P
DA_Q, DA_K, DA_V = 0, D, 2 * D
Z0 = 3 * D
XBC0 = Z0 + INNER
DT0 = XBC0 + INNER + 2 * SG * P
XQ0 = DT0 + 2 * SH
GATE0 = XQ0 + D
CONV_T = (INNER + 2 * SG * P) // P

RING = 4
LOOKAHEAD = 4
UT = 2
UC = 512


def lambda_init(layer):
    return 0.8 - 0.6 * math.exp(-0.3 * layer)


def slope(head):
    return 2.0 ** (-(head + 1))


def layer_groups():
    g = [("mk", b, 4, "T") for b in range(2)] + [("mv", b, 4, "N") for b in range(2)]
    g += [("xq", b, 4, "T") for b in range(2)]
    for half in range(2):
        g += [("q", half, 4, "T"), ("k", half, 4, "T"), ("v", half, 4, "N")]
    g += [("xbc", b, 4, "T") for b in range(CONV_T // 4)]
    g += [("dt", 0, 2, "D")]
    g += [("z", b, 4, "N") for b in range(4)]
    for branch, units in ((0, 4), (2, 4)):
        for nb in range(2):
            g += [(f"gate{branch}", nb, 4, "T"), (f"br{branch}", nb, units, "T")]
    for nb in range(2):
        g += [("gate1", nb, 4, "T"), ("br1", nb, 8, "T")]
    g += [("out", nb, 4, "T") for nb in range(2)]
    g += [("ffn", b, 4, "T") for b in range(FT // 2)]
    g += [("down", nb, FT // UT, "T") for nb in range(2)]
    return g


GROUPS = layer_groups()
FIRST_UNIT = [sum(x[2] for x in GROUPS[:i]) for i in range(len(GROUPS))]
UNITS = sum(x[2] for x in GROUPS)
NGROUPS = len(GROUPS)
UNIT_GROUP = [i for i, x in enumerate(GROUPS) for _ in range(x[2])]
assert UNITS % RING == 0 and NGROUPS % 2 == 0
GI = {(x[0], x[1]): i for i, x in enumerate(GROUPS)}
N_FFN = FT // 2
FFN_LOOP = N_FFN // 2


def layer_plan():
    after = {}

    def put(u, *step):
        after.setdefault(u, []).append(step)

    put(0, "norm_sum", 0)
    u = FIRST_UNIT[GI["q", 0]]
    for h in range(XH):
        put(u + 3 * h, "xa_scores", h)
        put(u + 3 * h + 2, "xa_turn", h)
        put(u + 3 * h + 3, "xa_values", h)
    u = FIRST_UNIT[GI["q", 1]] + 1
    for h in range(HALF):
        put(u + 3 * h, "da_scores", h)
        put(u + 3 * h + 1, "da_combine", h)
        put(u + 3 * h + 3, "da_turn", h)
        put(u + 3 * h + 4, "da_values", h)
    u = FIRST_UNIT[GI["xbc", 0]]
    put(u + 4, "da_norm", 0)
    put(u + 6, "da_out", 0)
    for h in range(HALF):
        put(u + 5 + 4 * h, "da_scores", HALF + h)
        put(u + 5 + 4 * h + 1, "da_combine", HALF + h)
        put(u + 5 + 4 * h + 3, "da_turn", HALF + h)
        put(u + 5 + 4 * h + 4, "da_values", HALF + h)
    put(u + 22, "da_norm", 1)
    put(u + 24, "da_out", 1)
    for b in range(INNER // P // 4):
        put(u + 4 * b + 6, "xs_turn", b)
    u = FIRST_UNIT[GI["z", 0]]
    put(u, "dt_sums", 0)
    quads = SG * NT * 4
    start, per = u + 3, 1.3
    for q in range(quads + 2):
        at = start + int(per * q)
        if q < quads:
            if q % 4 == 0:
                put(at, "scale", q // 4)
            put(at, "bc", q)
        if 1 <= q <= quads:
            put(at, "decay", q - 1)
        if q % 8 == 0 and q < quads:
            put(at, "cb", q // 8)
        if q >= 2:
            if q % 4 == 2:
                put(at, "off", q // 4)
            put(at, "diag", q - 2)
            if (q - 2) % 4 == 3:
                put(at, "assemble", (q - 2) // 4)
                if (q - 2) % 16 == 15:
                    put(at + 1, "ssm_norm", (q - 2) // 16)
                if q - 2 == 19:
                    put(at, "ssm_out", 0)
                if q - 2 == 31:
                    put(at + 3, "ssm_out", 1)
    put(FIRST_UNIT[GI["out", 1]] + 3, "norm_sum", 1)
    return after


AFTER = layer_plan()
SIDE_USES = [34, 27, 33, 29]
CONST_LOADS = 20


def build(nc, x, mem, mix_norm_g, w_in, lq1, lk1, lq2, lk2, subln_g, conv_w, conv_b, dt_bias, A_log, D_skip,
          ssm_norm_g, mem_norm_g, w_mem_kv, w_branch, w_out, ffn_norm_g, w_ffn_in, w_ffn_out, final_norm_g, out,
          side_uses):
    ctx = ExitStack()
    with ctx:
        def sb(name, cols, dtype=F32):
            return ctx.enter_context(nc.sbuf_tensor(name, [P, cols], dtype))

        def sem(name):
            return ctx.enter_context(nc.semaphore(name))

        xT_t = sb("xT", KT * T)
        hH_t, hL_t = sb("hH", KT * T, F32R), sb("hL", KT * T, F32R)
        actH_t, actL_t = sb("actH", 32 * T, F32R), sb("actL", 32 * T, F32R)
        raw_t = sb("w_raw", RING * UT * UC)
        wH_t, wL_t = sb("wH", RING * UT * UC, F32R), sb("wL", RING * UT * UC, F32R)
        regA, regB, scr = sb("regA", 6144), sb("regB", 6144), sb("scr", 5888)
        dts = sb("dts", 5 * P)
        aH_t, aL_t = sb("aH", P, F32R), sb("aL", P, F32R)
        par, lp = sb("par", 3 * P), sb("lp", 192)
        rows, lrow = sb("rows", 2 * 160), sb("lrow", 160)
        dist = sb("dist", NT * T)
        ident = sb("ident", P)
        upR, loR, onesR = sb("upR", P, F32R), sb("loR", P, F32R), sb("onesR", P, F32R)
        small = sb("small", 96)
        junk = sb("junk", UC)

        def v3(ap, n):
            return ap.rearrange("p (a b) -> p a b", a=n)

        xT = v3(xT_t[:, :], KT)
        hH, hL = v3(hH_t[:, :], KT), v3(hL_t[:, :], KT)
        actH, actL = v3(actH_t[:, :], 32), v3(actL_t[:, :], 32)
        raw = raw_t[:, :].rearrange("p (s k c) -> p s k c", s=RING, k=UT)
        wH = wH_t[:, :].rearrange("p (s k c) -> p s k c", s=RING, k=UT)
        wL = wL_t[:, :].rearrange("p (s k c) -> p s k c", s=RING, k=UT)
        DA_A, SSM_A, XA_A, MEM_A, MRG_A = 0, 8, 24, 22, 0
        mkT, mvN, xqT = v3(regA[:, 0:2048], KT), v3(regA[:, 2048:4096], NT), v3(regA[:, 4096:6144], KT)
        BT, CT, xsN = v3(regA[:, 0:1024], SG), v3(regA[:, 1024:2048], SG), v3(regA[:, 2048:6144], NT)
        memN, sqT, htmp = v3(regB[:, 0:2048], NT), v3(regB[:, 2048:4096], KT), v3(regB[:, 4096:6144], KT)
        qT = [v3(regB[:, 3072 * i:3072 * i + 1024], HALF) for i in range(2)]
        kT = [v3(regB[:, 3072 * i + 1024:3072 * i + 2048], HALF) for i in range(2)]
        vN = [v3(regB[:, 3072 * i + 2048:3072 * i + 3072], NT) for i in range(2)]
        zN, mrg = v3(regB[:, 0:4096], NT), v3(regB[:, 4096:6144], KT)
        std, rstd = regB[:, 2048:2304], regB[:, 2304:2560]
        sc = [scr[:, 1024 * i:1024 * (i + 1)] for i in range(2)]
        attT = v3(scr[:, 2048:2560], NT)
        yN = v3(scr[:, 2560:3584], HALF * NT)
        cin, cacc = v3(scr[:, 3584:4624], 4), v3(scr[:, 4624:5648], 4)
        E = [scr[:, 512 * i:512 * (i + 1)] for i in range(2)]
        M = [scr[:, 1024 + 512 * i:1536 + 512 * i] for i in range(2)]
        cbf, cbb, cboff = v3(scr[:, 2048:2304], 2), v3(scr[:, 2304:2560], 2), v3(scr[:, 2560:2816], 2)
        ytmp, xsd, xw, gtmp = (scr[:, 2816 + 512 * i:3328 + 512 * i] for i in range(4))
        sg = scr[:, 4864:5888]
        hid = scr[:, 0:512]
        mtmp = scr[:, 0:2048]
        xload = v3(scr[:, 0:2048], NT)
        dtv, aN, cs, eo, wgt = (dts[:, P * i:P * (i + 1)] for i in range(5))
        dt_e, dt_u, dt_x, dt_l, dt_c = (scr[:, P * i:P * (i + 1)] for i in range(5))
        up, lo, ones = (t[:, :].bitcast(F32) for t in (upR, loR, onesR))
        p_cw, p_mem, p_cb = lp[:, 0:120], lp[:, 120:128], lp[:, 128:152]
        p_mix, p_ffn, p_ssm = lp[:, 152:160], lp[:, 160:168], lp[:, 168:184]
        p_sub, p_nlam = lp[:, 184:185], lp[:, 185:186]
        r_dtb, r_A, r_D = lrow[:, 0:64], lrow[:, 64:128], lrow[:, 128:160]
        eps = small[:, 0:1]
        lam4, nlam2, sub2 = small[:, 2:6], small[:, 6:8], small[:, 8:10]
        ms, mr = small[:, 10:12], small[:, 12:14]
        mx = [small[:, 16 + 4 * i:20 + 4 * i] for i in range(2)]
        nmx = [small[:, 24 + 4 * i:28 + 4 * i] for i in range(2)]
        sm = [small[:, 32 + 4 * i:36 + 4 * i] for i in range(2)]
        rs = [small[:, 40 + 4 * i:44 + 4 * i] for i in range(2)]
        nl = [small[:, 48 + 2 * i:50 + 2 * i] for i in range(2)]
        ss, sr = small[:, 56:64], small[:, 64:72]
        s4, r4 = small[:, 72:76], small[:, 76:80]
        cstat = small[:, 80:88]

        PS = [ctx.enter_context(nc.psum_tensor(f"PS{i}", [P, 1024], F32)) for i in range(2)]
        S = [ctx.enter_context(nc.psum_tensor(f"S{i}", [P, 512], F32)) for i in range(4)]

        const_in, const_out, x_in, mem_in, stored = (sem(n) for n in (
            "const_in", "const_out", "x_in", "mem_in", "stored"))
        raw_in = [sem(f"raw_in{s}") for s in range(RING)]
        h_done = [sem(f"h_done{s}") for s in range(RING)]
        l_done = [sem(f"l_done{s}") for s in range(RING)]
        unit_used = [sem(f"unit_used{s}") for s in range(RING)]
        psum_free = [sem(f"psum_free{i}") for i in range(2)]
        side_free = [sem(f"side_free{i}") for i in range(4)]
        pool_ready, ident_ready, par_ready = sem("pool_ready"), sem("ident_ready"), sem("par_ready")
        setup_a, setup_v, setup_t = sem("setup_a"), sem("setup_v"), sem("setup_t")
        lp_ready = sem("lp_ready")
        mem_sq, mem_scaled, mem_turned, mem_g, mem_h, mem_ready, mem_std = (sem(n) for n in (
            "mem_sq", "mem_scaled", "mem_turned", "mem_g", "mem_h", "mem_ready", "mem_std"))
        x_ready, sq_done, sum_done, std_done, hn_done, hh_done, h_ready = (sem(n) for n in (
            "x_ready", "sq_done", "sum_done", "std_done", "hn_done", "hh_done", "h_ready"))
        regb_free = sem("regb_free")
        sp_pace = sem("sp_pace")
        xa_sc, xa_max, xa_exp, xa_p, xa_turned, xa_copied, xa_pv, xa_h, xa_y = (sem("xa_" + n) for n in (
            "sc", "max", "exp", "p", "turned", "copied", "pv", "h", "y"))
        da_sc, da_max, da_exp, da_att, da_turned, da_copied, da_pv, da_yc, da_st, da_sd, da_n, da_yt, da_h, da_y = (
            sem("da_" + n) for n in ("sc", "max", "exp", "att", "turned", "copied", "pv", "yc", "st", "sd", "n",
                                     "yt", "h", "y"))
        conv_done, silu_done, xs_turned, xs_ready = (sem(n) for n in (
            "conv_done", "silu_done", "xs_turned", "xs_ready"))
        dt_abs, dt_exp, dt_u1, dt_ln, a_ready, cs_done, cs_sub, cs_exp, dt_ready = (sem(n) for n in (
            "dt_abs", "dt_exp", "dt_u1", "dt_ln", "a_ready", "cs_done", "cs_sub", "cs_exp", "dt_ready"))
        cb_done, cb_ready, bc_done, diff_done, exp_done, m_done, diag_done = (sem("ssm_" + n) for n in (
            "cb", "cb_ready", "bc", "diff", "exp", "m", "diag"))
        xw_done, off_done, xsd_done, y_done, st_done, sd_done, n_done, yt_done, g_done, gh_done, ssm_y = (
            sem("ssm_" + n) for n in ("xw", "off", "xsd", "y", "st", "sd", "n", "yt", "g", "gh", "out"))
        mrg_sum, mrg_h, mrg_ready = sem("mrg_sum"), sem("mrg_h"), sem("mrg_ready")
        gate_done, up_done, hid_h, hid_ready = sem("gate_done"), sem("up_done"), sem("hid_h"), sem("hid_ready")
        fin_turned, fin_copied = sem("fin_turned"), sem("fin_copied")

        w_in_v = w_in.rearrange("l (k p) c -> l p k c", p=P)
        w_kv_v = w_mem_kv.rearrange("l (k p) c -> l p k c", p=P)
        w_br_v = w_branch.rearrange("l (k p) c -> l p k c", p=P)
        w_out_v = w_out.rearrange("l (k p) c -> l p k c", p=P)
        w_fi_v = w_ffn_in.rearrange("l (k p) (s c) -> l p k s c", p=P, s=2)
        w_fo_v = w_ffn_out.rearrange("l (k p) c -> l p k c", p=P)

        def cols(view, lay, k, col, n=UC):
            return view[lay, :, k:k + UT, col:col + n]

        def unit_loads(lay, g, c):
            kind, b, _, _ = GROUPS[g]
            k = UT * c
            if kind == "mk":
                return [cols(w_kv_v, lay, k, UC * b)]
            if kind == "mv":
                return [cols(w_kv_v, lay, k, D + UC * b)]
            if kind == "down":
                return [cols(w_fo_v, lay, k, UC * b)]
            if kind == "out":
                return [cols(w_out_v, lay, k, UC * b)]
            if kind.startswith("br"):
                first = {"br0": 0, "br1": 8, "br2": 24}[kind]
                return [cols(w_br_v, lay, first + k, UC * b)]
            col = {"xq": XQ0, "q": DA_Q, "k": DA_K, "v": DA_V, "xbc": XBC0, "z": Z0, "gate0": GATE0,
                   "gate1": GATE0 + D, "gate2": GATE0 + 2 * D}[kind]
            return [cols(w_in_v, lay, k, col + UC * b)]

        def use(lay, u):
            return lay * (UNITS // RING) + u // RING

        def used_after(lay, g):
            return lay * (NGROUPS // 2) + g // 2 + 2

        def wait_full(eng, lay, g, extra=0):
            u = FIRST_UNIT[g] + GROUPS[g][2] - 1
            eng.wait_ge(unit_used[u % RING], use(lay, u) + extra + 2)

        def wait_evacuated(eng, lay, kind, b):
            g = GI[kind, b]
            eng.wait_ge(psum_free[g % 2], used_after(lay, g))

        def each_step(unit_fn, evac_fn, step_fn, ffn_fn):
            u = 0
            while u < UNITS:
                g = UNIT_GROUP[u]
                if GROUPS[g][:2] == ("ffn", 0):
                    ffn_fn(g)
                    u += 8 * FFN_LOOP
                    continue
                c = u - FIRST_UNIT[g]
                unit_fn(u, g, c)
                if c == GROUPS[g][2] - 1:
                    evac_fn(g)
                for step in AFTER.get(u, []):
                    step_fn(*step)
                u += 1

        block = ctx.enter_context(nc.Block())

        @block.sync
        def _(sp):
            sp.dma_start(xload, x.rearrange("b (t p) d -> p (b t) d", p=P)).then_inc(x_in, 16)
            prm = v3(sqT.rearrange("p a b -> p (a b)")[:, 0:384], 3)
            for lay in range(DEPTH):
                sp.dma_start(prm[0:120, lay, :], conv_w[lay].rearrange("t (c q) -> (t c) q", q=P)
                             ).then_inc(const_in, 16)
                sp.dma_start(prm[120:128, lay, :], mem_norm_g[lay].rearrange("(c q) -> c q", q=P)
                             ).then_inc(const_in, 16)
            at = 0
            for v in (conv_b, mix_norm_g, ffn_norm_g, ssm_norm_g):
                src = v.rearrange("l (c q) -> (l c) q", q=P)
                sp.dma_start(prm[at:at + src.shape[0], 2, :], src).then_inc(const_in, 16)
                at += src.shape[0]
            sp.dma_start(prm[112:120, 2, :], final_norm_g.rearrange("(c q) -> c q", q=P)).then_inc(const_in, 16)
            sp.dma_start(prm[120:122, 2, :], subln_g).then_inc(const_in, 16)
            for lay in range(DEPTH):
                r = rows[:, 160 * lay:160 * (lay + 1)]
                sp.dma_start(r[:, 0:64], dt_bias[lay].rearrange("a b -> (a b)").partition_broadcast(P)
                             ).then_inc(const_in, 16)
                sp.dma_start(r[:, 64:128], A_log[lay].rearrange("a b -> (a b)").partition_broadcast(P)
                             ).then_inc(const_in, 16)
                sp.dma_start(r[:, 128:160], D_skip[lay].partition_broadcast(P)).then_inc(const_in, 16)
            for i, v in enumerate((lq1, lk1, lq2, lk2)):
                sp.dma_start(scr[:, 2048 + P * i:2048 + P * (i + 1)],
                             v.rearrange("l d -> (l d)").partition_broadcast(P)).then_inc(const_in, 16)

            def load(lay, u, extra=0, col=None):
                slot = u % RING
                n = use(lay, u) + extra
                g = UNIT_GROUP[u]
                c = u - FIRST_UNIT[g]
                kind, b = GROUPS[g][:2]
                sp.wait_ge(l_done[slot], n + 1)
                sp.sem_inc(sp_pace, 1)
                if kind == "ffn":
                    b = col if col is not None else b
                    dst = raw[:, slot].rearrange("p k (s c) -> p k s c", s=2)
                    for k in range(UT):
                        sp.dma_start(dst[:, k], w_fi_v[lay, :, UT * c + k, :, bass.ds(b * T, T)]
                                     ).then_inc(raw_in[slot], 16)
                elif kind == "dt":
                    dst = raw[:, slot].rearrange("p k c -> p (k c)")[:, 0:256].rearrange("p (k c) -> p k c", k=4)
                    sp.dma_start(dst, w_in_v[lay, :, 4 * c:4 * c + 4, DT0:DT0 + 64]).then_inc(raw_in[slot], 32)
                else:
                    src, = unit_loads(lay, g, c)
                    sp.dma_start(raw[:, slot], src).then_inc(raw_in[slot], 32)

            with sp.Fori(0, DEPTH) as lay:
                sp.wait_ge(regb_free, lay + 1)
                sp.dma_start(memN, mem.rearrange("b (t p) d -> p (b t) d", p=P)).then_inc(mem_in, 16)

                def ffn_loads(g):
                    u0 = FIRST_UNIT[g]
                    with sp.Fori(0, FFN_LOOP) as i:
                        for c in range(8):
                            load(lay, u0 + c, 2 * i, 2 * i + c // 4)

                each_step(lambda u, g, c: load(lay, u), lambda g: None, lambda *s: None, ffn_loads)
            sp.wait_ge(fin_copied, 4)
            sp.dma_start(out.rearrange("b (t p) d -> p (b t) d", p=P), xload).then_inc(stored, 16)
            sp.wait_ge(stored, 16)

        @block.tensor
        def _(pe):
            side = [0, 0, 0, 0]

            def take(lay, bank):
                pe.wait_ge(side_free[bank], lay * side_uses[bank] + side[bank] + 1)
                side[bank] += 1

            def mm(o, l, r, first, last):
                return nc.tensor.matmul(o, l, r, start=first, stop=last, skip_group_check=True)

            pe.wait_ge(pool_ready, 1)
            pe.wait_ge(const_in, 16 * CONST_LOADS)
            prm = v3(sqT.rearrange("p a b -> p (a b)")[:, 0:384], 3)
            for i in range(3):
                n = 122 if i == 2 else P
                ins = nc.tensor.transpose(PS[0][:, P * i:P * i + n], prm[0:n, i, :], ident[0:n, 0:n])
            ins.then_inc(setup_t, 1)
            pe.wait_ge(x_in, 16)
            for b in range(4):
                for k in range(2):
                    for t in range(NT):
                        ins = nc.tensor.transpose(S[b][:, T * k + P * t:T * k + P * (t + 1)],
                                                  xload[:, t, P * (2 * b + k):P * (2 * b + k + 1)], ident[:, :])
                ins.then_inc(setup_t, 1)
            pe.wait_ge(setup_v, 2)

            def operand(kind):
                if kind in ("mk", "mv"):
                    return actH, actL, MEM_A
                if kind.startswith("br"):
                    return actH, actL, {"br0": DA_A, "br1": SSM_A, "br2": XA_A}[kind]
                if kind == "out":
                    return actH, actL, MRG_A
                if kind == "down":
                    return actH, actL, 0
                return hH, hL, 0

            def wait_operand(lay, kind, b, c):
                if kind == "mk" and b == 0 and c == 0:
                    pe.wait_ge(mem_ready, lay + 1)
                elif kind == "xq" and b == 0 and c == 0:
                    pe.wait_ge(h_ready, 2 * lay + 1)
                elif kind == "ffn" and b == 0 and c == 0:
                    pe.wait_ge(h_ready, 2 * lay + 2)
                elif kind == "br0" and b == 0 and c == 0:
                    pe.wait_ge(da_y, 4 * lay + 4)
                elif kind == "br2" and b == 0 and c == 0:
                    pe.wait_ge(xa_y, XH * lay + XH)
                elif kind == "br1" and b == 0 and c in (0, 4):
                    pe.wait_ge(ssm_y, 8 * lay + (4 if c == 0 else 8))
                elif kind == "out" and b == 0 and c in (0, 2):
                    pe.wait_ge(mrg_ready, 2 * lay + (1 if c == 0 else 2))
                elif kind == "down" and b == 0:
                    pe.wait_ge(hid_ready, N_FFN * lay + c + 1)

            def unit(lay, u, g, c, extra_u=0, extra_g=0):
                kind, b, units, layout = GROUPS[g]
                slot, pair = u % RING, g % 2
                dst = PS[pair]
                if c == 0:
                    pe.wait_ge(psum_free[pair], lay * (NGROUPS // 2) + g // 2 + extra_g + 1)
                wait_operand(lay, kind, b, c)
                pe.wait_ge(l_done[slot], use(lay, u) + extra_u + 2)
                aH_, aL_, a0 = operand(kind)
                last_unit = c == units - 1
                if layout == "T":
                    for m in range(4):
                        for kk in range(UT):
                            k = a0 + UT * c + kk
                            w_h, w_l = wH[:, slot, kk, P * m:P * (m + 1)], wL[:, slot, kk, P * m:P * (m + 1)]
                            o = dst[:, T * m:T * (m + 1)]
                            new = c == 0 and kk == 0
                            mm(o, w_h, aH_[:, k, :], new and m % 2 == 0, False)
                            mm(o, w_h, aL_[:, k, :], False, False)
                            ins = mm(o, w_l, aH_[:, k, :], False, last_unit and kk == UT - 1)
                elif layout == "N":
                    for t in range(NT):
                        for kk in range(UT):
                            k = a0 + UT * c + kk
                            a_h, a_l = aH_[:, k, P * t:P * (t + 1)], aL_[:, k, P * t:P * (t + 1)]
                            o = dst[:, UC * t:UC * (t + 1)]
                            new = c == 0 and kk == 0
                            mm(o, a_h, wH[:, slot, kk, :], new, False)
                            mm(o, a_l, wH[:, slot, kk, :], False, False)
                            ins = mm(o, a_h, wL[:, slot, kk, :], False, last_unit and kk == UT - 1)
                else:
                    w_h = wH[:, slot].rearrange("p k c -> p (k c)")
                    w_l = wL[:, slot].rearrange("p k c -> p (k c)")
                    for t in range(NT):
                        for kk in range(4):
                            k = 4 * c + kk
                            a_h, a_l = aH_[:, k, P * t:P * (t + 1)], aL_[:, k, P * t:P * (t + 1)]
                            o = dst[:, 64 * t:64 * (t + 1)]
                            q = slice(64 * kk, 64 * (kk + 1))
                            mm(o, a_h, w_h[:, q], c == 0 and kk == 0 and t == 0, False)
                            mm(o, a_l, w_h[:, q], False, False)
                            ins = mm(o, a_h, w_l[:, q], False, last_unit and kk == 3)
                ins.then_inc(unit_used[slot], 1)

            def norm_sum(lay, which):
                take(lay, 0)
                pe.wait_ge(sq_done, which)
                for k in range(KT):
                    ins = mm(S[0][:, 0:T], ones, sqT[:, k, :], k == 0, k == KT - 1)
                ins.then_inc(sum_done, 1)

            def mem_turn(lay):
                pe.wait_ge(mem_scaled, lay + 1)
                for b in range(4):
                    take(lay, b)
                    for k in range(2):
                        for t in range(NT):
                            ins = nc.tensor.transpose(S[b][:, T * k + P * t:T * k + P * (t + 1)],
                                                      memN[:, t, P * (2 * b + k):P * (2 * b + k + 1)], ident[:, :])
                    ins.then_inc(mem_turned, 1)

            def step(lay, kind, i):
                if kind == "norm_sum":
                    norm_sum(lay, 2 * lay + i + 1)
                elif kind == "xa_scores":
                    if i == 0:
                        wait_evacuated(pe, lay, "xq", 1)
                        wait_evacuated(pe, lay, "mk", 1)
                    take(lay, i % 2)
                    for t in range(NT):
                        for k in range(2):
                            ins = mm(S[i % 2][:, T * t:T * (t + 1)], xqT[:, 2 * i + k, P * t:P * (t + 1)],
                                     mkT[:, 2 * i + k, :], k == 0, k == 1)
                    ins.then_inc(xa_sc, 1)
                elif kind == "xa_turn":
                    take(lay, 2)
                    pe.wait_ge(xa_p, XH * lay + i + 1)
                    for k in range(2):
                        for t in range(NT):
                            ins = nc.tensor.transpose(S[2][:, T * k + P * t:T * k + P * (t + 1)],
                                                      sc[i % 2][:, T * t + P * k:T * t + P * (k + 1)], ident[:, :])
                    ins.then_inc(xa_turned, 1)
                elif kind == "xa_values":
                    take(lay, 2)
                    pe.wait_ge(xa_copied, XH * lay + i + 1)
                    for e in range(2):
                        for k in range(2):
                            ins = mm(S[2][:, T * e:T * (e + 1)],
                                     mvN[:, k, T * i + P * e:T * i + P * (e + 1)], attT[:, k, :], k == 0, k == 1)
                    ins.then_inc(xa_pv, 1)
                elif kind == "da_scores":
                    half, j = i // HALF, i % HALF
                    if j == 0:
                        wait_evacuated(pe, lay, "k", half)
                        wait_evacuated(pe, lay, "v", half)
                    for m in range(2):
                        take(lay, m)
                        r = slice(DH * m, DH * (m + 1))
                        for t in range(NT):
                            ins = mm(S[m][:, T * t:T * (t + 1)], qT[half][r, j, P * t:P * (t + 1)],
                                     kT[half][r, j, :], True, True)
                    ins.then_inc(da_sc, 1)
                elif kind == "da_turn":
                    take(lay, 2)
                    pe.wait_ge(da_att, HEADS * lay + i + 1)
                    for k in range(2):
                        for t in range(NT):
                            ins = nc.tensor.transpose(S[2][:, T * k + P * t:T * k + P * (t + 1)],
                                                      sc[i % 2][:, T * t + P * k:T * t + P * (k + 1)], ident[:, :])
                    ins.then_inc(da_turned, 1)
                elif kind == "da_values":
                    half, j = i // HALF, i % HALF
                    take(lay, 2)
                    pe.wait_ge(da_copied, HEADS * lay + i + 1)
                    for t in range(NT):
                        for k in range(2):
                            ins = mm(S[2][:, P * t:P * (t + 1)], attT[:, k, P * t:P * (t + 1)],
                                     vN[half][:, k, P * j:P * (j + 1)], k == 0, k == 1)
                    ins.then_inc(da_pv, 1)
                elif kind == "da_out":
                    pe.wait_ge(da_n, 2 * lay + i + 1)
                    for r in range(2):
                        take(lay, 3)
                        for j in range(2):
                            for t in range(NT):
                                ins = nc.tensor.transpose(S[3][:, T * j + P * t:T * j + P * (t + 1)],
                                                          yN[:, NT * (2 * r + j) + t, :], ident[:, :])
                        ins.then_inc(da_yt, 1)
                elif kind == "xs_turn":
                    pe.wait_ge(silu_done, 6 * lay + i + 1)
                    for t in range(NT):
                        take(lay, 3)
                        for j in range(4):
                            ins = nc.tensor.transpose(S[3][:, P * j:P * (j + 1)], cacc[:, j, P * t:P * (t + 1)],
                                                      ident[:, :])
                        ins.then_inc(xs_turned, 1)
                elif kind == "dt_sums":
                    take(lay, 0)
                    pe.wait_ge(a_ready, lay + 1)
                    c3 = S[0][:, 0:P].rearrange("p (c j) -> p c j", c=NT)
                    aHv = aH_t[:, :].rearrange("p (c j) -> p c j", c=NT)
                    aLv = aL_t[:, :].rearrange("p (c j) -> p c j", c=NT)
                    for tri, q in ((upR, slice(0, SH)), (loR, slice(SH, 2 * SH))):
                        mm(c3[:, :, q], tri[:, :], aHv[:, :, q], True, False)
                        mm(c3[:, :, q], tri[:, :], aLv[:, :, q], False, True)
                    mm(S[0][:, P:2 * P], onesR[:, :], aH_t[:, :], True, False)
                    mm(S[0][:, P:2 * P], onesR[:, :], aL_t[:, :], False, True).then_inc(cs_done, 1)
                elif kind == "cb":
                    take(lay, 0)
                    if i == 0:
                        pe.wait_ge(silu_done, 6 * lay + 6)
                    for c in range(NT):
                        ins = mm(S[0][:, T * c:T * (c + 1)], BT[:, i, P * c:P * (c + 1)], CT[:, i, :], True, True)
                    ins.then_inc(cb_done, 1)
                elif kind == "off":
                    take(lay, 3)
                    c = i % 2
                    pe.wait_ge(xw_done, 8 * lay + i + 1)
                    pe.wait_ge(cb_ready, SG * lay + i // 2 + 1)
                    mm(S[3][:, :], cboff[:, 1 - c, :], xw, True, True).then_inc(off_done, 1)
                elif kind == "bc":
                    job, d, hf = i // 4, i // 2 % 2, i % 2
                    g, c = job // 2, job % 2
                    take(lay, i % 2)
                    for j in range(4):
                        q = 64 * c + SH * d + HPG * g + 4 * hf + j
                        o = S[i % 2][:, P * j:P * (j + 1)]
                        tri = (upR, loR)[d][:, :]
                        mm(o, aH_t[:, q:q + 1].broadcast_to([P, P]), tri, True, False)
                        ins = mm(o, aL_t[:, q:q + 1].broadcast_to([P, P]), tri, False, True)
                    ins.then_inc(bc_done, 1)
                elif kind == "diag":
                    job, d, hf = i // 4, i // 2 % 2, i % 2
                    g, c = job // 2, job % 2
                    if i % 4 == 0:
                        take(lay, 2)
                        if job == 0:
                            pe.wait_ge(xs_ready, 8 * lay + 8)
                    pe.wait_ge(m_done, 32 * lay + i + 1)
                    for j in range(4):
                        h = 4 * hf + j
                        ins = mm(S[2][:, DH * h:DH * (h + 1)], M[i % 2][:, P * j:P * (j + 1)],
                                 xsN[:, c, DH * (HPG * g + h):DH * (HPG * g + h + 1)], i % 4 == 0 and j == 0,
                                 d == 1)
                    ins.then_inc(diag_done, 1)
                elif kind == "ssm_out":
                    pe.wait_ge(n_done, 2 * lay + i + 1)
                    for g in range(2 * i, 2 * i + 2):
                        for c in range(NT):
                            take(lay, 3)
                            for j in range(4):
                                ins = nc.tensor.transpose(S[3][:, P * j:P * (j + 1)],
                                                          zN[:, c, P * (4 * g + j):P * (4 * g + j + 1)], ident[:, :])
                            ins.then_inc(yt_done, 1)

            def ffn_units(lay, g):
                u0 = FIRST_UNIT[g]
                with pe.Fori(0, FFN_LOOP) as i:
                    for c in range(8):
                        unit(lay, u0 + c, g + c // 4, c % 4, 2 * i, i)

            with pe.Fori(0, DEPTH) as lay:
                side[:] = [0, 0, 0, 0]
                mem_turn(lay)
                each_step(lambda u, g, c: unit(lay, u, g, c), lambda g: None, lambda *s: step(lay, *s),
                          lambda g: ffn_units(lay, g))
                counted = list(side)
            side[:] = [0, 0, 0, 0]
            norm_sum(DEPTH, 2 * DEPTH + 1)
            pe.wait_ge(hn_done, 2 * DEPTH + 1)
            for b in range(4):
                take(DEPTH, b)
                for t in range(NT):
                    for k in range(2):
                        ins = nc.tensor.transpose(S[b][:, T * t + P * k:T * t + P * (k + 1)],
                                                  htmp[:, 2 * b + k, P * t:P * (t + 1)], ident[:, :])
                ins.then_inc(fin_turned, 1)
            build.counted = counted

        @block.scalar
        def _(act):
            for s in range(RING):
                act.sem_inc(unit_used[s], 1)
            act.wait_ge(const_in, 16 * CONST_LOADS)
            act.wait_ge(setup_v, 1)
            nc.scalar.activation(lam4, lam4, ACT.Exp)
            r = rows[:, :].rearrange("p (l c) -> p l c", l=DEPTH)[:, :, 64:128]
            nc.scalar.activation(r, r, ACT.Exp)
            act.drain().then_inc(setup_a, 1)

            def split_h(lay, u, extra=0):
                slot = u % RING
                n = use(lay, u) + extra
                act.wait_ge(raw_in[slot], 32 * (n + 1))
                act.wait_ge(unit_used[slot], n + 1)
                if GROUPS[UNIT_GROUP[u]][0] == "dt":
                    q = slice(0, 256)
                else:
                    q = slice(0, UT * UC)
                nc.scalar.copy(wH[:, slot].rearrange("p k c -> p (k c)")[:, q],
                               raw[:, slot].rearrange("p k c -> p (k c)")[:, q]).then_inc(h_done[slot], 1)

            def evac(lay, g, extra=0):
                kind, b = GROUPS[g][:2]
                pair = g % 2
                src = PS[pair]
                if kind in ("mk", "xq", "q", "k", "mv", "v"):
                    wait_full(act, lay, g)
                    if layout_of(kind) == "T":
                        dst = {"mk": mkT, "xq": xqT}[kind][:, 4 * b:4 * b + 4, :] if kind in ("mk", "xq") else (
                            qT if kind == "q" else kT)[b]
                        nc.scalar.copy(dst, v3(src[:, :], 4)).then_inc(psum_free[pair], 1)
                    else:
                        dst = mvN[:, :, UC * b:UC * (b + 1)] if kind == "mv" else vN[b]
                        nc.scalar.copy(dst, v3(src[:, :], NT)).then_inc(psum_free[pair], 1)
                elif kind == "xbc":
                    wait_full(act, lay, g)
                    if b == 0:
                        act.wait_ge(da_copied, HEADS * lay + 1)
                    else:
                        act.wait_ge(conv_done, 6 * lay + b)
                    nc.scalar.copy(cin[:, :, 2:2 + T], v3(src[:, :], 4)).then_inc(psum_free[pair], 1)
                elif kind == "z":
                    wait_full(act, lay, g)
                    nc.scalar.activation(zN[:, :, UC * b:UC * (b + 1)], v3(src[:, :], NT),
                                         ACT.Silu).then_inc(psum_free[pair], 1)
                elif kind.startswith("gate"):
                    wait_full(act, lay, g)
                    last = [x for x in range(g) if GROUPS[x][0].startswith("br")]
                    if last:
                        act.wait_ge(psum_free[last[-1] % 2], used_after(lay, last[-1]))
                    nc.scalar.activation(sg, src[:, :], ACT.Tanh, scale=0.5).then_inc(psum_free[pair], 1)

            def layout_of(kind):
                return "N" if kind in ("mv", "v") else "T"

            def hidden_gate(lay, g, extra=0, first=False):
                pair = g % 2
                wait_full(act, lay, g, 2 * extra)
                act.wait_ge(up_done, N_FFN * lay + (g - GI["ffn", 0]) + 2 * extra + 1)
                nc.scalar.activation(sg[:, 0:512], PS[pair][:, 0:512], ACT.Silu).then_inc(gate_done, 1)

            def hidden_h(lay, g, tile, extra=0):
                act.wait_ge(up_done, N_FFN * lay + (g - GI["ffn", 0]) + 2 * extra + 2)
                nc.scalar.copy(actH_t[:, tile], hid).then_inc(hid_h, 1)

            def norm_act(lay, which):
                act.wait_ge(x_ready, which)
                nc.scalar.activation(sqT, xT, ACT.Square).then_inc(sq_done, 1)

            def norm_root(which):
                act.wait_ge(sum_done, which)
                nc.scalar.activation(std, S[0][:, 0:T], ACT.Sqrt, bias=eps, scale=1.0 / D
                                     ).then_inc(side_free[0], 1)
                act.drain().then_inc(std_done, 1)

            def norm_h(which):
                act.wait_ge(hn_done, which)
                nc.scalar.copy(hH, htmp).then_inc(hh_done, 1)

            def mem_act(lay):
                act.wait_ge(mem_in, 16 * (lay + 1))
                act.wait_ge(lp_ready, lay + 1)
                for t in range(NT):
                    nc.scalar.activation(sqT.rearrange("p a b -> p (a b)")[:, D * t:D * (t + 1)], memN[:, t, :],
                                         ACT.Square, accum_out=ms[:, t:t + 1])
                act.drain()
                nc.scalar.activation(mr, ms, ACT.Sqrt, bias=eps, scale=1.0 / D).then_inc(mem_std, 1)

            def step(lay, kind, i):
                if kind == "norm_sum":
                    if i == 1:
                        norm_act(lay, 2 * lay + 2)
                    norm_root(2 * lay + i + 1)
                    norm_h(2 * lay + i + 1)
                elif kind == "xa_scores":
                    b = i % 2
                    act.wait_ge(xa_max, XH * lay + i + 1)
                    for t in range(NT):
                        ins = nc.scalar.activation(sc[b][:, T * t:T * (t + 1)], S[b][:, T * t:T * (t + 1)], ACT.Exp,
                                                   bias=nmx[b][:, t:t + 1], scale=1.0 / 16.0,
                                                   accum_out=sm[b][:, t:t + 1])
                    ins.then_inc(side_free[b], 1)
                    act.drain().then_inc(xa_exp, 1)
                elif kind == "xa_turn":
                    act.wait_ge(xa_turned, XH * lay + i + 1)
                    nc.scalar.copy(attT, v3(S[2][:, :], 2)).then_inc(side_free[2], 1)
                    act.drain().then_inc(xa_copied, 1)
                elif kind == "xa_values":
                    act.wait_ge(xa_pv, XH * lay + i + 1)
                    nc.scalar.copy(actH[:, XA_A + 2 * i:XA_A + 2 * i + 2, :], v3(S[2][:, :], 2)).then_inc(xa_h, 1)
                elif kind == "da_scores":
                    b = i % 2
                    act.wait_ge(da_max, HEADS * lay + i + 1)
                    for q in range(4):
                        v = sc[b][:, T * q:T * (q + 1)]
                        nc.scalar.activation(v, v, ACT.Exp, bias=nmx[b][:, q:q + 1], scale=0.125,
                                             accum_out=sm[b][:, q:q + 1])
                    act.drain().then_inc(da_exp, 1)
                elif kind == "da_turn":
                    act.wait_ge(da_turned, HEADS * lay + i + 1)
                    nc.scalar.copy(attT, v3(S[2][:, :], 2)).then_inc(side_free[2], 1)
                    act.drain().then_inc(da_copied, 1)
                elif kind == "da_values":
                    j = i % HALF
                    act.wait_ge(da_pv, HEADS * lay + i + 1)
                    if j == 0 and i > 0:
                        act.wait_ge(da_yt, 4 * lay + 2)
                    nc.scalar.copy(yN[:, NT * j:NT * (j + 1), :], v3(S[2][:, 0:T], 2)).then_inc(side_free[2], 1)
                    act.drain()
                    for t in range(NT):
                        nc.scalar.activation(junk[:, P * t:P * (t + 1)], yN[:, NT * j + t, :], ACT.Square,
                                             accum_out=ss[:, NT * j + t:NT * j + t + 1])
                    act.drain().then_inc(da_st, 1)
                elif kind == "da_norm":
                    nc.scalar.activation(sr, ss, ACT.Sqrt, bias=eps, scale=1.0 / P).then_inc(da_sd, 1)
                elif kind == "da_out":
                    for r in range(2):
                        act.wait_ge(da_yt, 4 * lay + 2 * i + r + 1)
                        t0 = DA_A + HALF * i + 2 * r
                        nc.scalar.activation(actH[:, t0:t0 + 2, :], v3(S[3][:, :], 2), ACT.Copy,
                                             scale=p_sub).then_inc(da_h, 1)
                elif kind == "conv":
                    act.wait_ge(conv_done, 6 * lay + i + 1)
                    dst = cacc if i < 4 else (BT if i == 4 else CT)
                    nc.scalar.activation(dst, cacc, ACT.Silu)
                    act.drain().then_inc(silu_done, 1)
                elif kind == "xs_turn":
                    for t in range(NT):
                        act.wait_ge(xs_turned, 8 * lay + 2 * i + t + 1)
                        nc.scalar.copy(xsN[:, t, UC * i:UC * (i + 1)], S[3][:, :]).then_inc(side_free[3], 1)
                        act.drain().then_inc(xs_ready, 1)
                elif kind == "dt":
                    act.wait_ge(dt_abs, lay + 1)
                    nc.scalar.activation(dt_e, dt_e, ACT.Exp, scale=-1.0).then_inc(dt_exp, 1)
                    act.wait_ge(dt_u1, lay + 1)
                    nc.scalar.activation(dt_l, dt_u, ACT.Ln).then_inc(dt_ln, 1)
                elif kind == "dt_sums":
                    act.wait_ge(cs_sub, lay + 1)
                    nc.scalar.activation(eo, cs, ACT.Exp)
                    nc.scalar.activation(wgt, wgt, ACT.Exp).then_inc(cs_exp, 1)
                elif kind == "decay":
                    act.wait_ge(diff_done, 32 * lay + i + 1)
                    nc.scalar.activation(E[i % 2], E[i % 2], ACT.Exp).then_inc(exp_done, 1)
                elif kind == "assemble":
                    g, c = i // 2, i % 2
                    act.wait_ge(y_done, 8 * lay + i + 1)
                    nc.scalar.activation(junk[:, :], zN[:, c, UC * g:UC * (g + 1)], ACT.Square,
                                         accum_out=s4[:, i % 4:i % 4 + 1])
                    act.drain().then_inc(st_done, 1)
                elif kind == "ssm_norm":
                    nc.scalar.activation(r4, s4, ACT.Sqrt, bias=eps, scale=1.0 / 512).then_inc(sd_done, 1)
                elif kind == "ssm_out":
                    for q in range(4):
                        g, c = 2 * i + q // 2, q % 2
                        act.wait_ge(g_done, 8 * lay + 4 * i + q + 1)
                        t0 = SSM_A + 4 * g
                        nc.scalar.copy(actH[:, t0:t0 + 4, P * c:P * (c + 1)], v3(gtmp, 4)).then_inc(gh_done, 1)
                elif kind == "merged":
                    act.wait_ge(mrg_sum, 2 * lay + i + 1)
                    nc.scalar.activation(actH[:, MRG_A + 4 * i:MRG_A + 4 * i + 4, :], mrg[:, 4 * i:4 * i + 4, :],
                                         ACT.Copy, scale=0.5).then_inc(mrg_h, 1)

            with act.Fori(0, DEPTH) as lay:
                mem_act(lay)
                norm_act(lay, 2 * lay + 1)
                act.wait_ge(mem_g, lay + 1)
                nc.scalar.copy(actH[:, MEM_A:MEM_A + KT, :], v3(mtmp, KT)).then_inc(mem_h, 1)
                for u in range(LOOKAHEAD):
                    split_h(lay, u)

                def unit(u, g, c):
                    if u + LOOKAHEAD < UNITS:
                        split_h(lay, u + LOOKAHEAD)

                def group_end(g):
                    kind, b = GROUPS[g][:2]
                    if kind == "ffn":
                        hidden_gate(lay, g)
                        hidden_h(lay, g, slice(2 * b * T, (2 * b + 2) * T))
                    else:
                        evac(lay, g)
                    if kind in ("xbc", "dt"):
                        step(lay, "conv" if kind == "xbc" else "dt", b)
                    if kind == "br1":
                        step(lay, "merged", b)

                def ffn_loop(g):
                    u0 = FIRST_UNIT[g]
                    with act.Fori(0, FFN_LOOP) as i:
                        for c in range(8):
                            split_h(lay, u0 + c + LOOKAHEAD, 2 * i)
                            if c % 4 == 3:
                                hidden_gate(lay, g + c // 4, i)
                                hidden_h(lay, g + c // 4, bass.ds((4 * i + 2 * (c // 4)) * T, 2 * T), i)

                each_step(unit, group_end, lambda *s: step(lay, *s), ffn_loop)
            norm_act(DEPTH, 2 * DEPTH + 1)
            norm_root(2 * DEPTH + 1)

        @block.gpsimd
        def _(pool):
            nc.gpsimd.iota(dist[:, :], pattern=[[P, NT], [-1, T]], base=0, channel_multiplier=1,
                           allow_small_or_imprecise_dtypes=True)
            tmp = [scr[:, 2560 + P * i:2560 + P * (i + 1)] for i in range(3)]
            nc.gpsimd.memset(ident[:, :], 0.0)
            for i in range(3):
                nc.gpsimd.memset(tmp[i], 1.0)
            pool.drain()
            nc.gpsimd.affine_select(out=ident[:, :], in_=ident[:, :], compare_op=ALU.not_equal, fill=1.0, base=0,
                                    pattern=[[-1, P]], channel_multiplier=1)
            nc.gpsimd.affine_select(out=tmp[0], in_=tmp[0], compare_op=ALU.is_ge, fill=0.0, base=0,
                                    pattern=[[1, P]], channel_multiplier=-1)
            nc.gpsimd.affine_select(out=tmp[1], in_=tmp[1], compare_op=ALU.is_ge, fill=0.0, base=0,
                                    pattern=[[-1, P]], channel_multiplier=1)
            pool.drain().then_inc(pool_ready, 1)
            pool.sem_inc(l_done[RING - 1], 1)

            def split_l(lay, u, extra=0):
                slot = u % RING
                if slot != RING - 1:
                    return
                n = use(lay, u) + extra
                q = slice(0, 256 if GROUPS[UNIT_GROUP[u]][0] == "dt" else UT * UC)
                pool.wait_ge(h_done[slot], n + 1)
                nc.gpsimd.tensor_tensor(wL[:, slot].rearrange("p k c -> p (k c)")[:, q],
                                        raw[:, slot].rearrange("p k c -> p (k c)")[:, q],
                                        wH[:, slot].rearrange("p k c -> p (k c)")[:, q].bitcast(F32),
                                        ALU.subtract).then_inc(l_done[slot], 1)

            def step(lay, kind, i):
                g, c = i // 2, i % 2
                if kind == "scale":
                    if i == 0:
                        pool.wait_ge(xs_ready, 8 * lay + 8)
                        pool.wait_ge(dt_ready, lay + 1)
                    else:
                        pool.wait_ge(off_done, 8 * lay + i)
                    q = 64 * (1 - c) + SH * (1 - c) + HPG * g
                    nc.gpsimd.tensor_tensor(v3(xw, HPG), v3(xsN[:, 1 - c, UC * g:UC * (g + 1)], HPG),
                                            wgt[:, q:q + HPG].unsqueeze(2).broadcast_to([P, HPG, DH]),
                                            ALU.mult).then_inc(xw_done, 1)
                elif kind == "off":
                    if i > 0:
                        pool.wait_ge(y_done, 8 * lay + i)
                    nc.gpsimd.tensor_tensor(v3(xsd, HPG), v3(xsN[:, c, UC * g:UC * (g + 1)], HPG),
                                            r_D[:, HPG * g:HPG * (g + 1)].unsqueeze(2).broadcast_to([P, HPG, DH]),
                                            ALU.mult).then_inc(xsd_done, 1)

            with pool.Fori(0, DEPTH) as lay:
                for u in range(LOOKAHEAD):
                    split_l(lay, u)

                def ffn_loop(g):
                    u0 = FIRST_UNIT[g]
                    with pool.Fori(0, FFN_LOOP) as i:
                        for c in range(8):
                            split_l(lay, u0 + c + LOOKAHEAD, 2 * i)

                each_step(lambda u, g, c: split_l(lay, u + LOOKAHEAD) if u + LOOKAHEAD < UNITS else None,
                          lambda g: None, lambda *s: step(lay, *s), ffn_loop)

        @block.vector
        def _(dve):
            v = nc.vector
            for s in range(RING - 1):
                dve.sem_inc(l_done[s], 1)
            for i in range(2):
                dve.sem_inc(psum_free[i], 1)
            for i in range(4):
                dve.sem_inc(side_free[i], 1)
            dve.sem_inc(regb_free, 1)
            dve.sem_inc(up_done, 1)
            v.memset(eps, EPS)
            dve.wait_ge(const_in, 16 * CONST_LOADS)
            lam = scr[:, 2048:2560].rearrange("p (a q c) -> p a q c", a=2, q=2)
            lprod = v3(xT_t[:, 0:256], 2)
            v.tensor_tensor(lprod, lam[:, :, 0, :], lam[:, :, 1, :], ALU.mult)
            dve.drain()
            v.tensor_reduce(lam4, xT_t[:, 0:256].rearrange("p (a c) -> p a c", a=4), AX.X, ALU.add)
            dve.drain().then_inc(setup_v, 1)
            dve.wait_ge(pool_ready, 1)
            for i, t in enumerate((upR, loR, onesR)):
                v.tensor_copy(t[:, :], scr[:, 2560 + P * i:2560 + P * (i + 1)])
            v.tensor_scalar(xT_t[:, 256:768], dist[:, :], -1.0, None, ALU.mult)
            dve.drain()
            v.tensor_tensor(dist[:, :], dist[:, :], xT_t[:, 256:768], ALU.max)
            dve.wait_ge(setup_a, 1)
            v.tensor_tensor(nlam2, lam4[:, 2:4], lam4[:, 0:2], ALU.subtract)
            dve.drain()
            for lay in range(DEPTH):
                v.tensor_scalar(nlam2[:, lay:lay + 1], nlam2[:, lay:lay + 1], -lambda_init(lay), None, ALU.add)
            dve.wait_ge(setup_t, 1)
            v.tensor_copy(par[:, 0:378], PS[0][:, 0:378])
            dve.drain()
            for lay in range(DEPTH):
                v.tensor_scalar(sub2[:, lay:lay + 1], par[:, 376 + lay:377 + lay], 1.0 - lambda_init(lay), None,
                                ALU.mult)
            for b in range(4):
                dve.wait_ge(setup_t, 2 + b)
                v.tensor_copy(xT[:, 2 * b:2 * b + 2, :], v3(S[b][:, :], 2))
            dve.drain().then_inc(setup_v, 1)
            dve.sem_inc(x_ready, 1)

            def split_l(lay, u, extra=0):
                slot = u % RING
                if slot == RING - 1:
                    return
                n = use(lay, u) + extra
                q = slice(0, 256 if GROUPS[UNIT_GROUP[u]][0] == "dt" else UT * UC)
                dve.wait_ge(h_done[slot], n + 1)
                v.tensor_tensor(wL[:, slot].rearrange("p k c -> p (k c)")[:, q],
                                raw[:, slot].rearrange("p k c -> p (k c)")[:, q],
                                wH[:, slot].rearrange("p k c -> p (k c)")[:, q].bitcast(F32),
                                ALU.subtract).then_inc(l_done[slot], 1)

            def low(out_l, full, high, scale=None):
                if scale is None:
                    return v.tensor_tensor(out_l, full, high.bitcast(F32), ALU.subtract)
                return v.scalar_tensor_tensor(out_l, full, scale, high.bitcast(F32), ALU.mult, ALU.subtract)

            def gains(g, n, width):
                return g.unsqueeze(2).broadcast_to([P, n, width])

            def norm_gain(which, g):
                dve.wait_ge(x_ready, which)
                v.tensor_tensor(htmp, xT, gains(g, KT, T), ALU.mult)

            def norm_scale(which):
                dve.wait_ge(std_done, which)
                v.reciprocal(rstd, std)
                dve.drain()
                v.tensor_tensor(htmp, htmp, rstd.unsqueeze(1).broadcast_to([P, KT, T]), ALU.mult)
                dve.drain().then_inc(hn_done, 1)

            def norm_low(which):
                dve.wait_ge(hh_done, which)
                low(hL, htmp, hH).then_inc(h_ready, 1)

            def params(lay):
                v.tensor_copy(lp[:, 0:128], par[:, bass.ds(lay * 128, 128)])
                v.tensor_copy(p_cb, par[:, bass.ds(lay * 24 + 256, 24)])
                v.tensor_copy(p_mix, par[:, bass.ds(lay * 8 + 304, 8)])
                v.tensor_copy(p_ffn, par[:, bass.ds(lay * 8 + 320, 8)])
                v.tensor_copy(p_ssm, par[:, bass.ds(lay * 16 + 336, 16)])
                v.tensor_copy(p_sub, sub2[:, bass.ds(lay, 1)])
                v.tensor_copy(p_nlam, nlam2[:, bass.ds(lay, 1)])
                v.tensor_copy(lrow[:, :], rows[:, bass.ds(lay * 160, 160)])
                dve.drain().then_inc(lp_ready, 1)

            def mem_part(lay):
                dve.wait_ge(mem_std, lay + 1)
                v.reciprocal(mr, mr)
                dve.drain()
                for t in range(NT):
                    v.tensor_scalar(memN[:, t, :], memN[:, t, :], mr[:, t:t + 1], None, ALU.mult)
                dve.drain().then_inc(mem_scaled, 1)
                for b in range(4):
                    dve.wait_ge(mem_turned, 4 * lay + b + 1)
                    v.tensor_tensor(v3(mtmp[:, 512 * b:512 * (b + 1)], 2), v3(S[b][:, :], 2),
                                    gains(p_mem[:, 2 * b:2 * b + 2], 2, T), ALU.mult).then_inc(side_free[b], 1)
                dve.drain().then_inc(mem_g, 1)

            def evac(lay, g, extra=0):
                kind, b = GROUPS[g][:2]
                pair = g % 2
                src = PS[pair]
                tiles = slice(4 * b, 4 * b + 4) if kind != "ffn" else None
                if kind == "xbc":
                    dve.wait_ge(psum_free[pair], used_after(lay, g))
                    if b > 0:
                        if b <= 4:
                            dve.wait_ge(xs_turned, 8 * lay + 2 * b)
                        else:
                            dve.wait_ge(silu_done, 6 * lay + b)
                    for j in range(4):
                        t = 4 * b + j
                        v.tensor_scalar(cacc[:, j, :], cin[:, j, 0:T], p_cw[:, t:t + 1], p_cb[:, t:t + 1],
                                        ALU.mult, ALU.add)
                    for k in range(1, CONV):
                        dve.drain()
                        for j in range(4):
                            q = CONV_T * k + 4 * b + j
                            v.scalar_tensor_tensor(cacc[:, j, :], cin[:, j, k:k + T], p_cw[:, q:q + 1],
                                                   cacc[:, j, :], ALU.mult, ALU.add)
                    dve.drain().then_inc(conv_done, 1)
                elif kind == "dt":
                    wait_full(dve, lay, g)
                    bias = r_dtb.unsqueeze(1).broadcast_to([P, NT, 64])
                    v.tensor_tensor(v3(dt_x, NT), v3(src[:, 0:P], NT), bias, ALU.add)
                    dve.drain().then_inc(psum_free[pair], 1)
                    v.scalar_tensor_tensor(dt_e, dt_x, -1.0, dt_x, ALU.mult, ALU.max)
                    dve.drain().then_inc(dt_abs, 1)
                    dve.wait_ge(dt_exp, lay + 1)
                    v.tensor_scalar(dt_u, dt_e, 1.0, None, ALU.add)
                    dve.drain().then_inc(dt_u1, 1)
                    v.scalar_tensor_tensor(dt_c, dt_u, -1.0, dt_e, ALU.add, ALU.subtract)
                    v.reciprocal(aN, dt_u)
                    dve.drain()
                    v.tensor_tensor(dt_c, dt_c, aN, ALU.mult)
                    dve.drain()
                    dve.wait_ge(dt_ln, lay + 1)
                    v.tensor_tensor(dt_c, dt_l, dt_c, ALU.subtract)
                    dve.drain()
                    v.scalar_tensor_tensor(dtv, dt_x, 0.0, dt_c, ALU.max, ALU.add)
                    dve.drain()
                    v.scalar_tensor_tensor(v3(aN, NT), v3(dtv, NT), -1.0,
                                           r_A.unsqueeze(1).broadcast_to([P, NT, 64]), ALU.mult, ALU.mult)
                    dve.drain()
                    v.tensor_copy(aH_t[:, :], aN)
                    dve.drain()
                    low(aL_t[:, :], aN, aH_t[:, :]).then_inc(a_ready, 1)
                elif kind.startswith("br"):
                    gate = g - 1
                    dve.wait_ge(psum_free[gate % 2], used_after(lay, gate))
                    wait_full(dve, lay, g)
                    if kind == "br0":
                        v.scalar_tensor_tensor(mrg[:, tiles, :], v3(sg, 4), 1.0, v3(src[:, :], 4), ALU.add,
                                               ALU.mult)
                        dve.drain().then_inc(psum_free[pair], 1)
                    else:
                        v.scalar_tensor_tensor(v3(sg, 4), v3(sg, 4), 1.0, v3(src[:, :], 4), ALU.add, ALU.mult)
                        dve.drain()
                        v.tensor_tensor(mrg[:, tiles, :], mrg[:, tiles, :], v3(sg, 4), ALU.add)
                        dve.drain().then_inc(psum_free[pair], 1)
                    if kind == "br1":
                        dve.drain().then_inc(mrg_sum, 1)
                        dve.wait_ge(mrg_h, 2 * lay + b + 1)
                        low(actL[:, MRG_A + 4 * b:MRG_A + 4 * b + 4, :], mrg[:, tiles, :],
                            actH[:, MRG_A + 4 * b:MRG_A + 4 * b + 4, :], 0.5).then_inc(mrg_ready, 1)
                elif kind in ("out", "down"):
                    wait_full(dve, lay, g)
                    v.tensor_tensor(xT[:, tiles, :], xT[:, tiles, :], v3(src[:, :], 4), ALU.add
                                    ).then_inc(psum_free[pair], 1)
                    if b == 1:
                        dve.drain().then_inc(x_ready, 1)
                        if kind == "out":
                            dve.drain().then_inc(regb_free, 1)

            def hidden(lay, g, tile, extra=0):
                pair = g % 2
                n = N_FFN * lay + (g - GI["ffn", 0]) + 2 * extra
                dve.wait_ge(gate_done, n + 1)
                v.tensor_tensor(hid, sg[:, 0:512], PS[pair][:, 512:1024], ALU.mult).then_inc(psum_free[pair], 1)
                dve.drain().then_inc(up_done, 1)
                dve.wait_ge(hid_h, n + 1)
                low(actL_t[:, tile], hid, actH_t[:, tile]).then_inc(hid_ready, 1)
                dve.drain()

            def step(lay, kind, i):
                if kind == "norm_sum":
                    if i == 1:
                        norm_gain(2 * lay + 2, p_ffn)
                    norm_scale(2 * lay + i + 1)
                    norm_low(2 * lay + i + 1)
                elif kind == "xa_scores":
                    b = i % 2
                    dve.wait_ge(xa_sc, XH * lay + i + 1)
                    v.tensor_reduce(mx[b][:, 0:2], v3(S[b][:, :], 2), AX.X, ALU.max)
                    dve.drain()
                    v.tensor_scalar(nmx[b][:, 0:2], mx[b][:, 0:2], -1.0 / 16.0, None, ALU.mult).then_inc(xa_max, 1)
                    dve.wait_ge(xa_exp, XH * lay + i + 1)
                    v.reciprocal(rs[b][:, 0:2], sm[b][:, 0:2])
                    dve.drain()
                    for t in range(NT):
                        q = sc[b][:, T * t:T * (t + 1)]
                        v.tensor_scalar(q, q, rs[b][:, t:t + 1], None, ALU.mult)
                    dve.drain().then_inc(xa_p, 1)
                elif kind == "xa_values":
                    dve.wait_ge(xa_h, XH * lay + i + 1)
                    q = slice(XA_A + 2 * i, XA_A + 2 * i + 2)
                    low(actL[:, q, :], v3(S[2][:, :], 2), actH[:, q, :]).then_inc(side_free[2], 1)
                    dve.drain().then_inc(xa_y, 1)
                elif kind == "da_scores":
                    b = i % 2
                    dve.wait_ge(da_sc, HEADS * lay + i + 1)
                    if i >= 2:
                        dve.wait_ge(da_turned, HEADS * lay + i - 1)
                    else:
                        dve.wait_ge(xa_turned, XH * lay + XH)
                    for m in range(2):
                        v.scalar_tensor_tensor(sc[b][:, 512 * m:512 * (m + 1)], dist[:, :], -8.0 * slope(i),
                                               S[m][:, :], ALU.mult, ALU.add).then_inc(side_free[m], 1)
                    dve.drain()
                    v.tensor_reduce(mx[b], v3(sc[b], 4), AX.X, ALU.max)
                    dve.drain()
                    v.tensor_scalar(nmx[b], mx[b], -0.125, None, ALU.mult).then_inc(da_max, 1)
                elif kind == "da_combine":
                    b = i % 2
                    dve.wait_ge(da_exp, HEADS * lay + i + 1)
                    v.reciprocal(rs[b], sm[b])
                    dve.drain()
                    v.tensor_scalar(nl[b], rs[b][:, 2:4], p_nlam, None, ALU.mult)
                    dve.drain()
                    for t in range(NT):
                        q = sc[b][:, 512 + T * t:512 + T * (t + 1)]
                        v.tensor_scalar(q, q, nl[b][:, t:t + 1], None, ALU.mult)
                    dve.drain()
                    for t in range(NT):
                        v.scalar_tensor_tensor(sc[b][:, T * t:T * (t + 1)], sc[b][:, T * t:T * (t + 1)],
                                               rs[b][:, t:t + 1], sc[b][:, 512 + T * t:512 + T * (t + 1)],
                                               ALU.mult, ALU.add)
                    dve.drain().then_inc(da_att, 1)
                elif kind == "da_norm":
                    dve.wait_ge(da_sd, 2 * lay + i + 1)
                    v.reciprocal(sr, sr)
                    dve.drain()
                    v.tensor_tensor(yN, yN, gains(sr, HALF * NT, P), ALU.mult)
                    dve.drain().then_inc(da_n, 1)
                elif kind == "da_out":
                    for r in range(2):
                        dve.wait_ge(da_h, 4 * lay + 2 * i + r + 1)
                        q = slice(DA_A + HALF * i + 2 * r, DA_A + HALF * i + 2 * r + 2)
                        low(actL[:, q, :], v3(S[3][:, :], 2), actH[:, q, :], p_sub).then_inc(side_free[3], 1)
                        dve.drain().then_inc(da_y, 1)
                elif kind == "dt_sums":
                    dve.wait_ge(cs_done, lay + 1)
                    v.tensor_copy(cs, S[0][:, 0:P])
                    dve.drain()
                    v.tensor_tensor(wgt, S[0][:, P:2 * P], cs, ALU.subtract).then_inc(side_free[0], 1)
                    dve.drain().then_inc(cs_sub, 1)
                    dve.wait_ge(cs_exp, lay + 1)
                    v.tensor_tensor(wgt, wgt, dtv, ALU.mult).then_inc(dt_ready, 1)
                elif kind == "cb":
                    dve.wait_ge(cb_done, SG * lay + i + 1)
                    if i > 0:
                        dve.wait_ge(off_done, 8 * lay + 2 * i)
                    for c in range(NT):
                        blk = S[0][:, (T + P) * c:(T + P) * c + P]
                        v.tensor_tensor(cbf[:, c, :], blk, up, ALU.mult)
                        v.tensor_tensor(cbb[:, c, :], blk, lo, ALU.mult)
                    v.tensor_copy(cboff, v3(S[0][:, P:P + T], 2)).then_inc(side_free[0], 1)
                    dve.drain().then_inc(cb_ready, 1)
                elif kind == "bc":
                    job, d, hf = i // 4, i // 2 % 2, i % 2
                    g, c = job // 2, job % 2
                    dve.wait_ge(bc_done, 32 * lay + i + 1)
                    for j in range(4):
                        q = 64 * c + SH * d + HPG * g + 4 * hf + j
                        ins = v.tensor_scalar(E[i % 2][:, P * j:P * (j + 1)], S[i % 2][:, P * j:P * (j + 1)],
                                        cs[:, q:q + 1], 0.0, ALU.subtract, ALU.min)
                    ins.then_inc(side_free[i % 2], 1)
                    dve.drain().then_inc(diff_done, 1)
                elif kind == "decay":
                    job, d, hf = i // 4, i // 2 % 2, i % 2
                    g, c = job // 2, job % 2
                    dve.wait_ge(exp_done, 32 * lay + i + 1)
                    if i >= 2:
                        dve.wait_ge(diag_done, 32 * lay + i - 1)
                    for j in range(4):
                        q = 64 * c + SH * d + HPG * g + 4 * hf + j
                        v.scalar_tensor_tensor(M[i % 2][:, P * j:P * (j + 1)], E[i % 2][:, P * j:P * (j + 1)],
                                               dtv[:, q:q + 1], (cbf, cbb)[d][:, c, :], ALU.mult, ALU.mult)
                    dve.drain().then_inc(m_done, 1)
                elif kind == "assemble":
                    g, c = i // 2, i % 2
                    d = 1 - c
                    dve.wait_ge(off_done, 8 * lay + i + 1)
                    q = 64 * c + SH * d + HPG * g
                    v.tensor_tensor(v3(ytmp, HPG), v3(S[3][:, :], HPG), gains(eo[:, q:q + HPG], HPG, DH), ALU.mult)
                    dve.drain().then_inc(side_free[3], 1)
                    dve.wait_ge(diag_done, 32 * lay + 4 * i + 4)
                    v.tensor_tensor(ytmp, ytmp, S[2][:, :], ALU.add)
                    dve.drain().then_inc(side_free[2], 1)
                    dve.wait_ge(xsd_done, 8 * lay + i + 1)
                    v.tensor_tensor(ytmp, ytmp, xsd, ALU.add)
                    dve.drain()
                    if i % 2 == 0:
                        wait_evacuated(dve, lay, "z", g)
                    zq = zN[:, c, UC * g:UC * (g + 1)]
                    v.tensor_tensor(zq, zq, ytmp, ALU.mult)
                    dve.drain().then_inc(y_done, 1)
                elif kind == "ssm_norm":
                    dve.wait_ge(sd_done, 2 * lay + i + 1)
                    v.reciprocal(r4, r4)
                    dve.drain()
                    for q in range(4):
                        g, c = 2 * i + q // 2, q % 2
                        zq = zN[:, c, UC * g:UC * (g + 1)]
                        v.tensor_scalar(zq, zq, r4[:, q:q + 1], None, ALU.mult)
                    dve.drain().then_inc(n_done, 1)
                elif kind == "ssm_out":
                    for q in range(4):
                        g, c = 2 * i + q // 2, q % 2
                        dve.wait_ge(yt_done, 8 * lay + 4 * i + q + 1)
                        v.tensor_tensor(v3(gtmp, 4), v3(S[3][:, :], 4), gains(p_ssm[:, 4 * g:4 * g + 4], 4, P),
                                        ALU.mult).then_inc(side_free[3], 1)
                        dve.drain().then_inc(g_done, 1)
                        dve.wait_ge(gh_done, 8 * lay + 4 * i + q + 1)
                        t0 = SSM_A + 4 * g
                        low(actL[:, t0:t0 + 4, P * c:P * (c + 1)], v3(gtmp, 4),
                            actH[:, t0:t0 + 4, P * c:P * (c + 1)])
                        dve.drain().then_inc(ssm_y, 1)

            with dve.Fori(0, DEPTH) as lay:
                params(lay)
                mem_part(lay)
                norm_gain(2 * lay + 1, p_mix)
                dve.wait_ge(mem_h, lay + 1)
                low(actL[:, MEM_A:MEM_A + KT, :], v3(mtmp, KT), actH[:, MEM_A:MEM_A + KT, :]
                    ).then_inc(mem_ready, 1)
                for u in range(LOOKAHEAD):
                    split_l(lay, u)
                v.memset(cin[:, :, 0:2], 0.0)
                v.memset(cin[:, :, 2 + T:4 + T], 0.0)

                def unit(u, g, c):
                    if u + LOOKAHEAD < UNITS:
                        split_l(lay, u + LOOKAHEAD)

                def group_end(g):
                    kind, b = GROUPS[g][:2]
                    if kind == "ffn":
                        hidden(lay, g, slice(2 * b * T, (2 * b + 2) * T))
                    else:
                        evac(lay, g)

                def ffn_loop(g):
                    u0 = FIRST_UNIT[g]
                    with dve.Fori(0, FFN_LOOP) as i:
                        for c in range(8):
                            split_l(lay, u0 + c + LOOKAHEAD, 2 * i)
                            if c % 4 == 3:
                                hidden(lay, g + c // 4, bass.ds((4 * i + 2 * (c // 4)) * T, 2 * T), i)

                each_step(unit, group_end, lambda *s: step(lay, *s), ffn_loop)
            norm_gain(2 * DEPTH + 1, par[:, 368:376])
            norm_scale(2 * DEPTH + 1)
            for b in range(4):
                dve.wait_ge(fin_turned, b + 1)
                v.tensor_copy(xload[:, :, T * b:T * (b + 1)], v3(S[b][:, :], 2)).then_inc(fin_copied, 1)


_INS = ["x", "mem", "mix_norm_g", "w_in", "da_lambda_q1", "da_lambda_k1", "da_lambda_q2", "da_lambda_k2",
        "da_subln_g", "ssm_conv_w", "ssm_conv_b", "ssm_dt_bias", "ssm_A_log", "ssm_D", "ssm_norm_g", "mem_norm_g",
        "w_mem_kv", "w_branch", "w_out", "ffn_norm_g", "w_ffn_in", "w_ffn_out", "final_norm_g"]


def kernel(**inputs):
    import numpy as _np
    import concourse.bacc as _bacc
    from concourse import mybir as _mybir
    from concourse.bass_utils import run_bass_kernel_spmd as _run

    nc = _bacc.Bacc("TRN2", target_bir_lowering=False, num_devices=1, dynamic_dma_scratch_size=1024)
    arrays, args = {}, []
    for name in _INS:
        a = _np.ascontiguousarray(inputs[name])
        arrays[f"in_{name}_dram"] = a
        args.append(nc.dram_tensor(f"in_{name}_dram", a.shape, _mybir.dt.from_np(a.dtype), kind="ExternalInput").ap())
    o = nc.dram_tensor("out_0_dram", (1, T, D), _mybir.dt.float32, kind="ExternalOutput").ap()
    build(nc, *args, o, SIDE_USES)
    r = _run(nc, [arrays], core_ids=[0])
    return r.results[0]["out_0_dram"]
```

```python
import math
from contextlib import ExitStack

import concourse.bass as bass
from concourse import mybir

F32 = mybir.dt.float32
F32R = mybir.dt.float32r
ACT = mybir.ActivationFunctionType
ALU = mybir.AluOpType
AX = mybir.AxisListType
BF16 = mybir.dt.bfloat16

P = 128
D = 1024
T = 256
NT = T // P
KT = D // P
DEPTH = 2
EPS = 1e-6
HEADS, HALF = 8, 4
DH = 64
XH = 4
SH, SG = 32, 4
HPG = SH // SG
INNER = 2 * D
CONV = 5
FFN = 2816
FT = FFN // P
DA_Q, DA_K, DA_V = 0, D, 2 * D
Z0 = 3 * D
XBC0 = Z0 + INNER
DT0 = XBC0 + INNER + 2 * SG * P
XQ0 = DT0 + 2 * SH
GATE0 = XQ0 + D
CONV_T = (INNER + 2 * SG * P) // P

RING = 4
LOOKAHEAD = 3
UT = 2
UC = 512


def lambda_init(layer):
    return 0.8 - 0.6 * math.exp(-0.3 * layer)


def slope(head):
    return 2.0 ** (-(head + 1))


def layer_groups():
    g = [("mk", b, 4, "T") for b in range(2)] + [("mv", b, 4, "N") for b in range(2)]
    g += [("xq", b, 4, "T") for b in range(2)]
    for half in range(2):
        g += [("q", half, 4, "T"), ("k", half, 4, "T"), ("v", half, 4, "N")]
    g += [("xbc", b, 4, "T") for b in range(CONV_T // 4)]
    g += [("dt", 0, 2, "D")]
    g += [("z", b, 4, "N") for b in range(4)]
    for branch, units in ((0, 4), (2, 4)):
        for nb in range(2):
            g += [(f"gate{branch}", nb, 4, "T"), (f"br{branch}", nb, units, "T")]
    for nb in range(2):
        g += [("gate1", nb, 4, "T"), ("br1", nb, 8, "T")]
    g += [("out", nb, 4, "T") for nb in range(2)]
    g += [("ffn", b, 4, "T") for b in range(FT // 2)]
    g += [("down", nb, FT // UT, "T") for nb in range(2)]
    return g


GROUPS = layer_groups()
FIRST_UNIT = [sum(x[2] for x in GROUPS[:i]) for i in range(len(GROUPS))]
UNITS = sum(x[2] for x in GROUPS)
NGROUPS = len(GROUPS)
UNIT_GROUP = [i for i, x in enumerate(GROUPS) for _ in range(x[2])]
assert UNITS % RING == 0 and NGROUPS % 2 == 0
GI = {(x[0], x[1]): i for i, x in enumerate(GROUPS)}
N_FFN = FT // 2
FFN_LOOP = N_FFN // 2


def layer_plan():
    after = {}

    def put(u, *step):
        after.setdefault(u, []).append(step)

    put(1, "norm_sum", 0)
    u = FIRST_UNIT[GI["q", 0]]
    for h in range(XH):
        put(u + 3 * h, "xa_scores", h)
        put(u + 3 * h + 2, "xa_turn", h)
        put(u + 3 * h + 3, "xa_values", h)
    u = FIRST_UNIT[GI["q", 1]]
    for h in range(HEADS):
        at = u + (1 + 3 * h if h < HALF else 4 * h)
        put(at, "da_scores", h)
        put(at + 2, "da_combine", h)
        put(at + 4, "da_turn", h)
        put(at + 5, "da_values", h)
    put(u + 16, "da_norm", 0)
    put(u + 17, "da_out", 0)
    put(u + 18, "da_out", 1)
    put(u + 34, "da_norm", 1)
    put(u + 36, "da_out", 2)
    put(u + 38, "da_out", 3)
    u = FIRST_UNIT[GI["xbc", 0]]
    for b in range(CONV_T // 4):
        put(u + 4 * b + 4, "conv", 2 * b)
        put(u + 4 * b + 5, "conv", 2 * b + 1)
        put(u + 4 * b + 6, "conv_silu", b)
        if b < INNER // P // 4:
            put(u + 4 * b + 9, "xs_turn", 2 * b)
            put(u + 4 * b + 10, "xs_turn", 2 * b + 1)
    u = FIRST_UNIT[GI["z", 0]]
    put(u + 3, "dt_sums", 0)
    quads = SG * NT * 4
    start, per = u + 5, 1.25
    for q in range(quads + 2):
        at = start + int(per * q)
        if q % 4 == 0 and q > 0:
            put(at, "off", q // 4 - 1)
        if q < quads:
            if q % 2 == 0:
                put(at, "scale", q // 2)
            put(at, "bc", q)
            if q % 8 == 1:
                put(at, "cb", q // 8)
        if 1 <= q <= quads:
            put(at, "decay", q - 1)
        if q >= 2:
            put(at, "diag", q - 2)
            if q % 4 == 1:
                put(at, "assemble", (q - 2) // 4)
            if q in (17, 33):
                put(at + 1, "ssm_norm", q // 32)
            if q in (22, 23, 26, 27):
                put(at, "ssm_out", (22, 23, 26, 27).index(q))
    for r in range(4):
        put(at + 3 + r, "ssm_out", 4 + r)
    put(FIRST_UNIT[GI["out", 1]] + 3, "norm_sum", 1)
    return after


AFTER = layer_plan()


def pool_splits(u):
    u %= UNITS
    return u % 2 == 1 or (FIRST_UNIT[GI["q", 1]] + 4 <= u < FIRST_UNIT[GI["dt", 0]] + 4 and u % 4 == 2)


SIDE_USES = [34, 27, 33, 29]
CONST_LOADS = 20


def build(nc, x, mem, mix_norm_g, w_in, lq1, lk1, lq2, lk2, subln_g, conv_w, conv_b, dt_bias, A_log, D_skip,
          ssm_norm_g, mem_norm_g, w_mem_kv, w_branch, w_out, ffn_norm_g, w_ffn_in, w_ffn_out, final_norm_g, out,
          side_uses):
    ctx = ExitStack()
    with ctx:
        def sb(name, cols, dtype=F32):
            return ctx.enter_context(nc.sbuf_tensor(name, [P, cols], dtype))

        def sem(name):
            return ctx.enter_context(nc.semaphore(name))

        xT_t = sb("xT", KT * T)
        hH_t, hL_t = sb("hH", KT * T, F32R), sb("hL", KT * T, F32R)
        actH_t, actL_t = sb("actH", 32 * T, F32R), sb("actL", 32 * T, F32R)
        raw_t = sb("w_raw", RING * UT * UC)
        wH_t, wL_t = sb("wH", RING * UT * UC, F32R), sb("wL", RING * UT * UC, F32R)
        regA, regB, scr = sb("regA", 6144), sb("regB", 6144), sb("scr", 6144)
        dts = sb("dts", 5 * P)
        aH_t, aL_t = sb("aH", P, F32R), sb("aL", P, F32R)
        par, lp = sb("par", 3 * P), sb("lp", 192)
        rows, lrow = sb("rows", 2 * 160), sb("lrow", 160)
        dist = sb("dist", NT * T, BF16)
        ident, identB = sb("ident", P), sb("identB", P, BF16)
        mask_t = sb("mask", 2 * P, BF16)
        upR, loR, onesR = sb("upR", P, F32R), sb("loR", P, F32R), sb("onesR", P, F32R)
        small = sb("small", 96)
        junk = sb("junk", UC, BF16)

        def v3(ap, n):
            return ap.rearrange("p (a b) -> p a b", a=n)

        xT = v3(xT_t[:, :], KT)
        hH, hL = v3(hH_t[:, :], KT), v3(hL_t[:, :], KT)
        actH, actL = v3(actH_t[:, :], 32), v3(actL_t[:, :], 32)
        raw = raw_t[:, :].rearrange("p (s k c) -> p s k c", s=RING, k=UT)
        wH = wH_t[:, :].rearrange("p (s k c) -> p s k c", s=RING, k=UT)
        wL = wL_t[:, :].rearrange("p (s k c) -> p s k c", s=RING, k=UT)
        DA_A, SSM_A, XA_A, MEM_A, MRG_A = 0, 8, 24, 22, 0
        mkT, mvN, xqT = v3(regA[:, 0:2048], KT), v3(regA[:, 2048:4096], NT), v3(regA[:, 4096:6144], KT)
        BT, CT, xsN = v3(regA[:, 0:1024], SG), v3(regA[:, 1024:2048], SG), v3(regA[:, 2048:6144], NT)
        memN, sqT, htmp = v3(regB[:, 0:2048], NT), v3(regB[:, 2048:4096], KT), v3(regB[:, 4096:6144], KT)
        qT = [v3(regB[:, 3072 * i:3072 * i + 1024], HALF) for i in range(2)]
        kT = [v3(regB[:, 3072 * i + 1024:3072 * i + 2048], HALF) for i in range(2)]
        vN = [v3(regB[:, 3072 * i + 2048:3072 * i + 3072], NT) for i in range(2)]
        zN, mrg = v3(regB[:, 0:4096], NT), v3(regB[:, 4096:6144], KT)
        std, rstd = regB[:, 2048:2304], regB[:, 2304:2560]
        sc = [scr[:, 1024 * i:1024 * (i + 1)] for i in range(2)]
        attT = v3(scr[:, 2048:2560], NT)
        yN = v3(scr[:, 2560:3584], HALF * NT)
        cin = v3(scr[:, 3584:4624], 4)
        cacc = [BT, CT]
        M = [scr[:, 512 * i:512 * (i + 1)] for i in range(3)]
        cb = scr[:, 1536:2048]
        ytmp, xsd, xw, gtmp, xd0, xd1 = (scr[:, 2048 + 512 * i:2560 + 512 * i] for i in range(6))
        xd = [xd0, xd1]
        sg = scr[:, 5120:6144]
        hid = scr[:, 0:512]
        mtmp = scr[:, 0:2048]
        xload = v3(scr[:, 0:2048], NT)
        mask = v3(mask_t[:, :], 2)
        dtv, aN, cs, eo, wgt = (dts[:, P * i:P * (i + 1)] for i in range(5))
        dt_e, dt_u, dt_x, dt_l, dt_c = (scr[:, P * i:P * (i + 1)] for i in range(5))
        ncs = aN
        ones = onesR[:, :].bitcast(F32)
        p_cw, p_mem, p_cb = lp[:, 0:120], lp[:, 120:128], lp[:, 128:152]
        p_mix, p_ffn, p_ssm = lp[:, 152:160], lp[:, 160:168], lp[:, 168:184]
        p_sub, p_nlam = lp[:, 184:185], lp[:, 185:186]
        r_dtb, r_A, r_D = lrow[:, 0:64], lrow[:, 64:128], lrow[:, 128:160]
        eps = small[:, 0:1]
        lam4, nlam2, sub2 = small[:, 2:6], small[:, 6:8], small[:, 8:10]
        ms, mr = small[:, 10:12], small[:, 12:14]
        mx = [small[:, 16 + 4 * i:20 + 4 * i] for i in range(2)]
        nmx = [small[:, 24 + 4 * i:28 + 4 * i] for i in range(2)]
        sm = [small[:, 32 + 4 * i:36 + 4 * i] for i in range(2)]
        rs = [small[:, 40 + 4 * i:44 + 4 * i] for i in range(2)]
        nl = [small[:, 48 + 2 * i:50 + 2 * i] for i in range(2)]
        ss, sr = small[:, 56:64], small[:, 64:72]
        s4, r4 = small[:, 72:76], small[:, 76:80]
        cstat = small[:, 80:88]

        PS = [ctx.enter_context(nc.psum_tensor(f"PS{i}", [P, 1024], F32)) for i in range(2)]
        S = [ctx.enter_context(nc.psum_tensor(f"S{i}", [P, 512], F32)) for i in range(4)]

        const_in, const_out, x_in, mem_in, stored = (sem(n) for n in (
            "const_in", "const_out", "x_in", "mem_in", "stored"))
        raw_in = [sem(f"raw_in{s}") for s in range(RING)]
        h_done = [sem(f"h_done{s}") for s in range(RING)]
        l_done = [sem(f"l_done{s}") for s in range(RING)]
        unit_used = [sem(f"unit_used{s}") for s in range(RING)]
        psum_free = [sem(f"psum_free{i}") for i in range(2)]
        side_free = [sem(f"side_free{i}") for i in range(4)]
        pool_ready, ident_ready, par_ready = sem("pool_ready"), sem("ident_ready"), sem("par_ready")
        setup_a, setup_v, setup_t = sem("setup_a"), sem("setup_v"), sem("setup_t")
        lp_ready = sem("lp_ready")
        mem_sq, mem_scaled, mem_turned, mem_g, mem_h, mem_ready, mem_std = (sem(n) for n in (
            "mem_sq", "mem_scaled", "mem_turned", "mem_g", "mem_h", "mem_ready", "mem_std"))
        x_ready, sq_done, sum_done, std_done, hn_done, hh_done, h_ready = (sem(n) for n in (
            "x_ready", "sq_done", "sum_done", "std_done", "hn_done", "hh_done", "h_ready"))
        regb_free = sem("regb_free")
        sp_pace = sem("sp_pace")
        xa_sc, xa_max, xa_exp, xa_p, xa_turned, xa_copied, xa_pv, xa_h, xa_y = (sem("xa_" + n) for n in (
            "sc", "max", "exp", "p", "turned", "copied", "pv", "h", "y"))
        da_sc, da_max, da_exp, da_att, da_turned, da_copied, da_pv, da_yc, da_st, da_sd, da_n, da_yt, da_h, da_y = (
            sem("da_" + n) for n in ("sc", "max", "exp", "att", "turned", "copied", "pv", "yc", "st", "sd", "n",
                                     "yt", "h", "y"))
        conv_done, silu_done, xs_turned, xs_ready = (sem(n) for n in (
            "conv_done", "silu_done", "xs_turned", "xs_ready"))
        dt_abs, dt_exp, dt_u1, dt_ln, a_ready, cs_done, cs_sub, cs_exp, dt_ready = (sem(n) for n in (
            "dt_abs", "dt_exp", "dt_u1", "dt_ln", "a_ready", "cs_done", "cs_sub", "cs_exp", "dt_ready"))
        cb_done, cb_ready, bc_done, exp_done, m_done, diag_done = (sem("ssm_" + n) for n in (
            "cb", "cb_ready", "bc", "exp", "m", "diag"))
        xw_done, xd_done, off_done, xsd_done, y_done, st_done, sd_done, n_done, yt_done, g_done, gh_done, ssm_y = (
            sem("ssm_" + n) for n in ("xw", "xd", "off", "xsd", "y", "st", "sd", "n", "yt", "g", "gh", "out"))
        mrg_sum, mrg_h, mrg_ready = sem("mrg_sum"), sem("mrg_h"), sem("mrg_ready")
        gate_done, up_done, hid_h, hid_ready = sem("gate_done"), sem("up_done"), sem("hid_h"), sem("hid_ready")
        fin_turned, fin_copied = sem("fin_turned"), sem("fin_copied")

        w_in_v = w_in.rearrange("l (k p) c -> l p k c", p=P)
        w_kv_v = w_mem_kv.rearrange("l (k p) c -> l p k c", p=P)
        w_br_v = w_branch.rearrange("l (k p) c -> l p k c", p=P)
        w_out_v = w_out.rearrange("l (k p) c -> l p k c", p=P)
        w_fi_v = w_ffn_in.rearrange("l (k p) (s c) -> l p k s c", p=P, s=2)
        w_fo_v = w_ffn_out.rearrange("l (k p) c -> l p k c", p=P)

        def cols(view, lay, k, col, n=UC):
            return view[lay, :, k:k + UT, col:col + n]

        def unit_loads(lay, g, c):
            kind, b, _, _ = GROUPS[g]
            k = UT * c
            if kind == "mk":
                return [cols(w_kv_v, lay, k, UC * b)]
            if kind == "mv":
                return [cols(w_kv_v, lay, k, D + UC * b)]
            if kind == "down":
                return [cols(w_fo_v, lay, k, UC * b)]
            if kind == "out":
                return [cols(w_out_v, lay, k, UC * b)]
            if kind.startswith("br"):
                first = {"br0": 0, "br1": 8, "br2": 24}[kind]
                return [cols(w_br_v, lay, first + k, UC * b)]
            col = {"xq": XQ0, "q": DA_Q, "k": DA_K, "v": DA_V, "xbc": XBC0, "z": Z0, "gate0": GATE0,
                   "gate1": GATE0 + D, "gate2": GATE0 + 2 * D}[kind]
            return [cols(w_in_v, lay, k, col + UC * b)]

        def use(lay, u):
            return lay * (UNITS // RING) + u // RING

        def used_after(lay, g):
            return lay * (NGROUPS // 2) + g // 2 + 2

        def wait_full(eng, lay, g, extra=0):
            u = FIRST_UNIT[g] + GROUPS[g][2] - 1
            eng.wait_ge(unit_used[u % RING], use(lay, u) + extra + 2)

        def wait_evacuated(eng, lay, kind, b):
            g = GI[kind, b]
            eng.wait_ge(psum_free[g % 2], used_after(lay, g))

        def each_step(unit_fn, evac_fn, step_fn, ffn_fn):
            u = 0
            while u < UNITS:
                g = UNIT_GROUP[u]
                if GROUPS[g][:2] == ("ffn", 0):
                    ffn_fn(g)
                    u += 8 * FFN_LOOP
                    continue
                c = u - FIRST_UNIT[g]
                unit_fn(u, g, c)
                if c == GROUPS[g][2] - 1:
                    evac_fn(g)
                for step in AFTER.get(u, []):
                    step_fn(*step)
                u += 1

        block = ctx.enter_context(nc.Block())

        @block.sync
        def _(sp):
            sp.dma_start(xload, x.rearrange("b (t p) d -> p (b t) d", p=P)).then_inc(x_in, 16)
            prm = v3(sqT.rearrange("p a b -> p (a b)")[:, 0:384], 3)
            for lay in range(DEPTH):
                sp.dma_start(prm[0:120, lay, :], conv_w[lay].rearrange("t (c q) -> (t c) q", q=P)
                             ).then_inc(const_in, 16)
                sp.dma_start(prm[120:128, lay, :], mem_norm_g[lay].rearrange("(c q) -> c q", q=P)
                             ).then_inc(const_in, 16)
            at = 0
            for v in (conv_b, mix_norm_g, ffn_norm_g, ssm_norm_g):
                src = v.rearrange("l (c q) -> (l c) q", q=P)
                sp.dma_start(prm[at:at + src.shape[0], 2, :], src).then_inc(const_in, 16)
                at += src.shape[0]
            sp.dma_start(prm[112:120, 2, :], final_norm_g.rearrange("(c q) -> c q", q=P)).then_inc(const_in, 16)
            sp.dma_start(prm[120:122, 2, :], subln_g).then_inc(const_in, 16)
            for lay in range(DEPTH):
                r = rows[:, 160 * lay:160 * (lay + 1)]
                sp.dma_start(r[:, 0:64], dt_bias[lay].rearrange("a b -> (a b)").partition_broadcast(P)
                             ).then_inc(const_in, 16)
                sp.dma_start(r[:, 64:128], A_log[lay].rearrange("a b -> (a b)").partition_broadcast(P)
                             ).then_inc(const_in, 16)
                sp.dma_start(r[:, 128:160], D_skip[lay].partition_broadcast(P)).then_inc(const_in, 16)
            for i, v in enumerate((lq1, lk1, lq2, lk2)):
                sp.dma_start(scr[:, 2048 + P * i:2048 + P * (i + 1)],
                             v.rearrange("l d -> (l d)").partition_broadcast(P)).then_inc(const_in, 16)

            def load(lay, u, extra=0, col=None):
                slot = u % RING
                n = use(lay, u) + extra
                g = UNIT_GROUP[u]
                c = u - FIRST_UNIT[g]
                kind, b = GROUPS[g][:2]
                sp.wait_ge(l_done[slot], n + 1)
                sp.sem_inc(sp_pace, 1)
                if kind == "ffn":
                    b = col if col is not None else b
                    dst = raw[:, slot].rearrange("p k (s c) -> p k s c", s=2)
                    for k in range(UT):
                        sp.dma_start(dst[:, k], w_fi_v[lay, :, UT * c + k, :, bass.ds(b * T, T)]
                                     ).then_inc(raw_in[slot], 16)
                elif kind == "dt":
                    dst = raw[:, slot].rearrange("p k c -> p (k c)")[:, 0:256].rearrange("p (k c) -> p k c", k=4)
                    sp.dma_start(dst, w_in_v[lay, :, 4 * c:4 * c + 4, DT0:DT0 + 64]).then_inc(raw_in[slot], 32)
                else:
                    src, = unit_loads(lay, g, c)
                    sp.dma_start(raw[:, slot], src).then_inc(raw_in[slot], 32)

            with sp.Fori(0, DEPTH) as lay:
                sp.wait_ge(regb_free, lay + 1)
                sp.dma_start(memN, mem.rearrange("b (t p) d -> p (b t) d", p=P)).then_inc(mem_in, 16)

                def ffn_loads(g):
                    u0 = FIRST_UNIT[g]
                    with sp.Fori(0, FFN_LOOP) as i:
                        for c in range(8):
                            load(lay, u0 + c, 2 * i, 2 * i + c // 4)

                each_step(lambda u, g, c: load(lay, u), lambda g: None, lambda *s: None, ffn_loads)
            sp.wait_ge(fin_copied, 4)
            sp.dma_start(out.rearrange("b (t p) d -> p (b t) d", p=P), xload).then_inc(stored, 16)
            sp.wait_ge(stored, 16)

        @block.tensor
        def _(pe):
            side = [0, 0, 0, 0]

            def take(lay, bank):
                pe.wait_ge(side_free[bank], lay * side_uses[bank] + side[bank] + 1)
                side[bank] += 1

            def mm(o, l, r, first, last):
                return nc.tensor.matmul(o, l, r, start=first, stop=last, skip_group_check=True)

            pe.wait_ge(pool_ready, 1)
            pe.wait_ge(const_in, 16 * CONST_LOADS)
            prm = v3(sqT.rearrange("p a b -> p (a b)")[:, 0:384], 3)
            for i in range(3):
                n = 122 if i == 2 else P
                ins = nc.tensor.transpose(PS[0][:, P * i:P * i + n], prm[0:n, i, :], ident[0:n, 0:n])
            ins.then_inc(setup_t, 1)
            pe.wait_ge(x_in, 16)
            for b in range(4):
                for k in range(2):
                    for t in range(NT):
                        ins = nc.tensor.transpose(S[b][:, T * k + P * t:T * k + P * (t + 1)],
                                                  xload[:, t, P * (2 * b + k):P * (2 * b + k + 1)], ident[:, :])
                ins.then_inc(setup_t, 1)
            pe.wait_ge(setup_v, 2)

            def operand(kind):
                if kind in ("mk", "mv"):
                    return actH, actL, MEM_A
                if kind.startswith("br"):
                    return actH, actL, {"br0": DA_A, "br1": SSM_A, "br2": XA_A}[kind]
                if kind == "out":
                    return actH, actL, MRG_A
                if kind == "down":
                    return actH, actL, 0
                return hH, hL, 0

            def wait_operand(lay, kind, b, c):
                if kind == "mk" and b == 0 and c == 0:
                    pe.wait_ge(mem_ready, lay + 1)
                elif kind == "xq" and b == 0 and c == 0:
                    pe.wait_ge(h_ready, 2 * lay + 1)
                elif kind == "ffn" and b == 0 and c == 0:
                    pe.wait_ge(h_ready, 2 * lay + 2)
                elif kind == "br0" and b == 0 and c == 0:
                    pe.wait_ge(da_y, 4 * lay + 4)
                elif kind == "br2" and b == 0 and c == 0:
                    pe.wait_ge(xa_y, XH * lay + XH)
                elif kind == "br1" and b == 0 and c in (0, 4):
                    pe.wait_ge(ssm_y, 8 * lay + (4 if c == 0 else 8))
                elif kind == "out" and b == 0 and c in (0, 2):
                    pe.wait_ge(mrg_ready, 2 * lay + (1 if c == 0 else 2))
                elif kind == "down" and b == 0:
                    pe.wait_ge(hid_ready, N_FFN * lay + c + 1)

            def unit(lay, u, g, c, extra_u=0, extra_g=0):
                kind, b, units, layout = GROUPS[g]
                slot, pair = u % RING, g % 2
                dst = PS[pair]
                if c == 0:
                    pe.wait_ge(psum_free[pair], lay * (NGROUPS // 2) + g // 2 + extra_g + 1)
                wait_operand(lay, kind, b, c)
                pe.wait_ge(l_done[slot], use(lay, u) + extra_u + 2)
                aH_, aL_, a0 = operand(kind)
                last_unit = c == units - 1
                if layout == "T":
                    for m in range(4):
                        for kk in range(UT):
                            k = a0 + UT * c + kk
                            w_h, w_l = wH[:, slot, kk, P * m:P * (m + 1)], wL[:, slot, kk, P * m:P * (m + 1)]
                            o = dst[:, T * m:T * (m + 1)]
                            new = c == 0 and kk == 0
                            mm(o, w_h, aH_[:, k, :], new and m % 2 == 0, False)
                            mm(o, w_h, aL_[:, k, :], False, False)
                            ins = mm(o, w_l, aH_[:, k, :], False, last_unit and kk == UT - 1)
                elif layout == "N":
                    for t in range(NT):
                        for kk in range(UT):
                            k = a0 + UT * c + kk
                            a_h, a_l = aH_[:, k, P * t:P * (t + 1)], aL_[:, k, P * t:P * (t + 1)]
                            o = dst[:, UC * t:UC * (t + 1)]
                            new = c == 0 and kk == 0
                            mm(o, a_h, wH[:, slot, kk, :], new, False)
                            mm(o, a_l, wH[:, slot, kk, :], False, False)
                            ins = mm(o, a_h, wL[:, slot, kk, :], False, last_unit and kk == UT - 1)
                else:
                    w_h = wH[:, slot].rearrange("p k c -> p (k c)")
                    w_l = wL[:, slot].rearrange("p k c -> p (k c)")
                    for t in range(NT):
                        for kk in range(4):
                            k = 4 * c + kk
                            a_h, a_l = aH_[:, k, P * t:P * (t + 1)], aL_[:, k, P * t:P * (t + 1)]
                            o = dst[:, 64 * t:64 * (t + 1)]
                            q = slice(64 * kk, 64 * (kk + 1))
                            mm(o, a_h, w_h[:, q], c == 0 and kk == 0 and t == 0, False)
                            mm(o, a_l, w_h[:, q], False, False)
                            ins = mm(o, a_h, w_l[:, q], False, last_unit and kk == 3)
                ins.then_inc(unit_used[slot], 1)

            def norm_sum(lay, which):
                take(lay, 0)
                pe.wait_ge(sq_done, which)
                for k in range(KT):
                    ins = mm(S[0][:, 0:T], ones, sqT[:, k, :], k == 0, k == KT - 1)
                ins.then_inc(sum_done, 1)

            def mem_turn(lay):
                pe.wait_ge(mem_scaled, lay + 1)
                for b in range(4):
                    take(lay, b)
                    for k in range(2):
                        for t in range(NT):
                            ins = nc.tensor.transpose(S[b][:, T * k + P * t:T * k + P * (t + 1)],
                                                      memN[:, t, P * (2 * b + k):P * (2 * b + k + 1)], ident[:, :])
                    ins.then_inc(mem_turned, 1)

            def step(lay, kind, i):
                if kind == "norm_sum":
                    norm_sum(lay, 2 * lay + i + 1)
                elif kind == "xa_scores":
                    if i == 0:
                        wait_evacuated(pe, lay, "xq", 1)
                        wait_evacuated(pe, lay, "mk", 1)
                    take(lay, i % 2)
                    for t in range(NT):
                        for k in range(2):
                            ins = mm(S[i % 2][:, T * t:T * (t + 1)], xqT[:, 2 * i + k, P * t:P * (t + 1)],
                                     mkT[:, 2 * i + k, :], k == 0, k == 1)
                    ins.then_inc(xa_sc, 1)
                elif kind == "xa_turn":
                    take(lay, 2)
                    pe.wait_ge(xa_p, XH * lay + i + 1)
                    for k in range(2):
                        for t in range(NT):
                            ins = nc.tensor.transpose(S[2][:, T * k + P * t:T * k + P * (t + 1)],
                                                      sc[i % 2][:, T * t + P * k:T * t + P * (k + 1)], ident[:, :])
                    ins.then_inc(xa_turned, 1)
                elif kind == "xa_values":
                    take(lay, 2)
                    pe.wait_ge(xa_copied, XH * lay + i + 1)
                    for e in range(2):
                        for k in range(2):
                            ins = mm(S[2][:, T * e:T * (e + 1)],
                                     mvN[:, k, T * i + P * e:T * i + P * (e + 1)], attT[:, k, :], k == 0, k == 1)
                    ins.then_inc(xa_pv, 1)
                elif kind == "da_scores":
                    half, j = i // HALF, i % HALF
                    if j == 0:
                        wait_evacuated(pe, lay, "k", half)
                        wait_evacuated(pe, lay, "v", half)
                    for m in range(2):
                        take(lay, m)
                        r = slice(DH * m, DH * (m + 1))
                        for t in range(NT):
                            ins = mm(S[m][:, T * t:T * (t + 1)], qT[half][r, j, P * t:P * (t + 1)],
                                     kT[half][r, j, :], True, True)
                    ins.then_inc(da_sc, 1)
                elif kind == "da_turn":
                    take(lay, 2)
                    pe.wait_ge(da_att, HEADS * lay + i + 1)
                    for k in range(2):
                        for t in range(NT):
                            ins = nc.tensor.transpose(S[2][:, T * k + P * t:T * k + P * (t + 1)],
                                                      sc[i % 2][:, T * t + P * k:T * t + P * (k + 1)], ident[:, :])
                    ins.then_inc(da_turned, 1)
                elif kind == "da_values":
                    half, j = i // HALF, i % HALF
                    take(lay, 2)
                    pe.wait_ge(da_copied, HEADS * lay + i + 1)
                    for t in range(NT):
                        for k in range(2):
                            ins = mm(S[2][:, P * t:P * (t + 1)], attT[:, k, P * t:P * (t + 1)],
                                     vN[half][:, k, P * j:P * (j + 1)], k == 0, k == 1)
                    ins.then_inc(da_pv, 1)
                elif kind == "da_out":
                    take(lay, 3)
                    pe.wait_ge(da_n, 2 * lay + i // 2 + 1)
                    for j in range(2):
                        for t in range(NT):
                            ins = nc.tensor.transpose(S[3][:, T * j + P * t:T * j + P * (t + 1)],
                                                      yN[:, NT * (2 * (i % 2) + j) + t, :], ident[:, :])
                    ins.then_inc(da_yt, 1)
                elif kind == "xs_turn":
                    take(lay, 3)
                    pe.wait_ge(silu_done, 6 * lay + i // 2 + 1)
                    t = i % 2
                    for j in range(4):
                        ins = nc.tensor.transpose(S[3][:, P * j:P * (j + 1)], cacc[i // 2 % 2][:, j, P * t:P * (t + 1)],
                                                  ident[:, :])
                    ins.then_inc(xs_turned, 1)
                elif kind == "dt_sums":
                    take(lay, 0)
                    pe.wait_ge(a_ready, lay + 1)
                    c3 = S[0][:, 0:P].rearrange("p (c j) -> p c j", c=NT)
                    aHv = aH_t[:, :].rearrange("p (c j) -> p c j", c=NT)
                    aLv = aL_t[:, :].rearrange("p (c j) -> p c j", c=NT)
                    for tri, q in ((upR, slice(0, SH)), (loR, slice(SH, 2 * SH))):
                        mm(c3[:, :, q], tri[:, :], aHv[:, :, q], True, False)
                        mm(c3[:, :, q], tri[:, :], aLv[:, :, q], False, True)
                    mm(S[0][:, P:2 * P], onesR[:, :], aH_t[:, :], True, False)
                    mm(S[0][:, P:2 * P], onesR[:, :], aL_t[:, :], False, True).then_inc(cs_done, 1)
                elif kind == "cb":
                    take(lay, 0)
                    if i == 0:
                        pe.wait_ge(silu_done, 6 * lay + 6)
                    for c in range(NT):
                        ins = mm(S[0][:, T * c:T * (c + 1)], BT[:, i, P * c:P * (c + 1)], CT[:, i, :], True, True)
                    ins.then_inc(cb_done, 1)
                elif kind == "off":
                    take(lay, 3)
                    c = i % 2
                    pe.wait_ge(xw_done, 8 * lay + i + 1)
                    pe.wait_ge(cb_ready, SG * lay + i // 2 + 1)
                    mm(S[3][:, :], cb[:, T * (1 - c) + P * c:T * (1 - c) + P * (c + 1)], xw, True, True
                       ).then_inc(off_done, 1)
                elif kind == "bc":
                    job, d, hf = i // 4, i // 2 % 2, i % 2
                    g, c = job // 2, job % 2
                    take(lay, i % 2)
                    mm(v3(S[i % 2][:, :], 4), identB[:, :], mask[:, d, :].unsqueeze(1).broadcast_to([P, 4, P]),
                       True, False)
                    for j in range(4):
                        q = 64 * c + SH * d + HPG * g + 4 * hf + j
                        o = S[i % 2][:, P * j:P * (j + 1)]
                        tri = (upR, loR)[d][:, :]
                        mm(o, aH_t[:, q:q + 1].broadcast_to([P, P]), tri, False, False)
                        ins = mm(o, aL_t[:, q:q + 1].broadcast_to([P, P]), tri, False, j == 3)
                    ins.then_inc(bc_done, 1)
                elif kind == "diag":
                    job, d, hf = i // 4, i // 2 % 2, i % 2
                    g, c = job // 2, job % 2
                    if i % 4 == 0:
                        take(lay, 2)
                    if i % 2 == 0:
                        pe.wait_ge(xd_done, 16 * lay + i // 2 + 1)
                    pe.wait_ge(m_done, 32 * lay + i + 1)
                    for j in range(4):
                        h = 4 * hf + j
                        ins = mm(S[2][:, DH * h:DH * (h + 1)], M[i % 3][:, P * j:P * (j + 1)],
                                 xd[d][:, DH * h:DH * (h + 1)], i % 4 == 0 and j == 0,
                                 d == 1)
                    ins.then_inc(diag_done, 1)
                elif kind == "ssm_out":
                    g, c = i // 2, i % 2
                    take(lay, 3)
                    pe.wait_ge(n_done, 2 * lay + i // 4 + 1)
                    for j in range(4):
                        ins = nc.tensor.transpose(S[3][:, P * j:P * (j + 1)],
                                                  zN[:, c, P * (4 * g + j):P * (4 * g + j + 1)], ident[:, :])
                    ins.then_inc(yt_done, 1)

            def ffn_units(lay, g):
                u0 = FIRST_UNIT[g]
                with pe.Fori(0, FFN_LOOP) as i:
                    for c in range(8):
                        unit(lay, u0 + c, g + c // 4, c % 4, 2 * i, i)

            with pe.Fori(0, DEPTH) as lay:
                side[:] = [0, 0, 0, 0]
                mem_turn(lay)
                each_step(lambda u, g, c: unit(lay, u, g, c), lambda g: None, lambda *s: step(lay, *s),
                          lambda g: ffn_units(lay, g))
                counted = list(side)
            side[:] = [0, 0, 0, 0]
            norm_sum(DEPTH, 2 * DEPTH + 1)
            pe.wait_ge(hn_done, 2 * DEPTH + 1)
            for b in range(4):
                take(DEPTH, b)
                for t in range(NT):
                    for k in range(2):
                        ins = nc.tensor.transpose(S[b][:, T * t + P * k:T * t + P * (k + 1)],
                                                  htmp[:, 2 * b + k, P * t:P * (t + 1)], ident[:, :])
                ins.then_inc(fin_turned, 1)
            build.counted = counted

        @block.scalar
        def _(act):
            for s in range(RING):
                act.sem_inc(unit_used[s], 1)
            act.wait_ge(const_in, 16 * CONST_LOADS)
            act.wait_ge(setup_v, 1)
            nc.scalar.activation(lam4, lam4, ACT.Exp)
            r = rows[:, :].rearrange("p (l c) -> p l c", l=DEPTH)[:, :, 64:128]
            nc.scalar.activation(r, r, ACT.Exp)
            act.drain().then_inc(setup_a, 1)

            def split_h(lay, u, extra=0):
                slot = u % RING
                n = use(lay, u) + extra
                act.wait_ge(raw_in[slot], 32 * (n + 1))
                act.wait_ge(unit_used[slot], n + 1)
                if GROUPS[UNIT_GROUP[u]][0] == "dt":
                    q = slice(0, 256)
                else:
                    q = slice(0, UT * UC)
                nc.scalar.copy(wH[:, slot].rearrange("p k c -> p (k c)")[:, q],
                               raw[:, slot].rearrange("p k c -> p (k c)")[:, q]).then_inc(h_done[slot], 1)

            def evac(lay, g, extra=0):
                kind, b = GROUPS[g][:2]
                pair = g % 2
                src = PS[pair]
                if kind in ("mk", "xq", "q", "k", "mv", "v"):
                    wait_full(act, lay, g)
                    if layout_of(kind) == "T":
                        dst = {"mk": mkT, "xq": xqT}[kind][:, 4 * b:4 * b + 4, :] if kind in ("mk", "xq") else (
                            qT if kind == "q" else kT)[b]
                        nc.scalar.copy(dst, v3(src[:, :], 4)).then_inc(psum_free[pair], 1)
                    else:
                        dst = mvN[:, :, UC * b:UC * (b + 1)] if kind == "mv" else vN[b]
                        nc.scalar.copy(dst, v3(src[:, :], NT)).then_inc(psum_free[pair], 1)
                elif kind == "xbc":
                    wait_full(act, lay, g)
                    if b == 0:
                        act.wait_ge(da_copied, HEADS * lay + 1)
                    else:
                        act.wait_ge(conv_done, 6 * lay + b)
                    nc.scalar.copy(cin[:, :, 2:2 + T], v3(src[:, :], 4)).then_inc(psum_free[pair], 1)
                elif kind == "z":
                    wait_full(act, lay, g)
                    nc.scalar.activation(zN[:, :, UC * b:UC * (b + 1)], v3(src[:, :], NT),
                                         ACT.Silu).then_inc(psum_free[pair], 1)
                elif kind.startswith("gate"):
                    wait_full(act, lay, g)
                    last = [x for x in range(g) if GROUPS[x][0].startswith("br")]
                    if last:
                        act.wait_ge(psum_free[last[-1] % 2], used_after(lay, last[-1]))
                    nc.scalar.activation(sg, src[:, :], ACT.Tanh, scale=0.5).then_inc(psum_free[pair], 1)

            def layout_of(kind):
                return "N" if kind in ("mv", "v") else "T"

            def hidden_gate(lay, g, extra=0, first=False):
                pair = g % 2
                wait_full(act, lay, g, 2 * extra)
                act.wait_ge(up_done, N_FFN * lay + (g - GI["ffn", 0]) + 2 * extra + 1)
                nc.scalar.activation(sg[:, 0:512], PS[pair][:, 0:512], ACT.Silu).then_inc(gate_done, 1)

            def hidden_h(lay, g, tile, extra=0):
                act.wait_ge(up_done, N_FFN * lay + (g - GI["ffn", 0]) + 2 * extra + 2)
                nc.scalar.copy(actH_t[:, tile], hid).then_inc(hid_h, 1)

            def norm_act(lay, which):
                act.wait_ge(x_ready, which)
                nc.scalar.activation(sqT, xT, ACT.Square).then_inc(sq_done, 1)

            def norm_root(which):
                act.wait_ge(sum_done, which)
                nc.scalar.activation(std, S[0][:, 0:T], ACT.Sqrt, bias=eps, scale=1.0 / D
                                     ).then_inc(side_free[0], 1)
                act.drain().then_inc(std_done, 1)

            def norm_h(which):
                act.wait_ge(hn_done, which)
                nc.scalar.copy(hH, htmp).then_inc(hh_done, 1)

            def mem_act(lay):
                act.wait_ge(mem_in, 16 * (lay + 1))
                act.wait_ge(lp_ready, lay + 1)
                for t in range(NT):
                    nc.scalar.activation(sqT.rearrange("p a b -> p (a b)")[:, D * t:D * (t + 1)], memN[:, t, :],
                                         ACT.Square, accum_out=ms[:, t:t + 1])
                act.drain()
                nc.scalar.activation(mr, ms, ACT.Sqrt, bias=eps, scale=1.0 / D).then_inc(mem_std, 1)

            def step(lay, kind, i):
                if kind == "norm_sum":
                    if i == 1:
                        norm_act(lay, 2 * lay + 2)
                    norm_root(2 * lay + i + 1)
                    norm_h(2 * lay + i + 1)
                elif kind == "xa_scores":
                    b = i % 2
                    act.wait_ge(xa_max, XH * lay + i + 1)
                    for t in range(NT):
                        ins = nc.scalar.activation(sc[b][:, T * t:T * (t + 1)], S[b][:, T * t:T * (t + 1)], ACT.Exp,
                                                   bias=nmx[b][:, t:t + 1], scale=1.0 / 16.0,
                                                   accum_out=sm[b][:, t:t + 1])
                    ins.then_inc(side_free[b], 1)
                    act.drain().then_inc(xa_exp, 1)
                elif kind == "xa_turn":
                    act.wait_ge(xa_turned, XH * lay + i + 1)
                    nc.scalar.copy(attT, v3(S[2][:, :], 2)).then_inc(side_free[2], 1)
                    act.drain().then_inc(xa_copied, 1)
                elif kind == "xa_values":
                    act.wait_ge(xa_pv, XH * lay + i + 1)
                    nc.scalar.copy(actH[:, XA_A + 2 * i:XA_A + 2 * i + 2, :], v3(S[2][:, :], 2)).then_inc(xa_h, 1)
                elif kind == "da_scores":
                    b = i % 2
                    act.wait_ge(da_max, HEADS * lay + i + 1)
                    for q in range(4):
                        v = sc[b][:, T * q:T * (q + 1)]
                        nc.scalar.activation(v, v, ACT.Exp, bias=nmx[b][:, q:q + 1], scale=0.125,
                                             accum_out=sm[b][:, q:q + 1])
                    act.drain().then_inc(da_exp, 1)
                elif kind == "da_turn":
                    act.wait_ge(da_turned, HEADS * lay + i + 1)
                    nc.scalar.copy(attT, v3(S[2][:, :], 2)).then_inc(side_free[2], 1)
                    act.drain().then_inc(da_copied, 1)
                elif kind == "da_values":
                    j = i % HALF
                    act.wait_ge(da_pv, HEADS * lay + i + 1)
                    if j == 0 and i > 0:
                        act.wait_ge(da_yt, 4 * lay + 2)
                    nc.scalar.copy(yN[:, NT * j:NT * (j + 1), :], v3(S[2][:, 0:T], 2)).then_inc(side_free[2], 1)
                    act.drain()
                    for t in range(NT):
                        nc.scalar.activation(junk[:, P * t:P * (t + 1)], yN[:, NT * j + t, :], ACT.Square,
                                             accum_out=ss[:, NT * j + t:NT * j + t + 1])
                    act.drain().then_inc(da_st, 1)
                elif kind == "da_norm":
                    nc.scalar.activation(sr, ss, ACT.Sqrt, bias=eps, scale=1.0 / P).then_inc(da_sd, 1)
                elif kind == "da_out":
                    act.wait_ge(da_yt, 4 * lay + i + 1)
                    t0 = DA_A + 2 * i
                    nc.scalar.activation(actH[:, t0:t0 + 2, :], v3(S[3][:, :], 2), ACT.Copy,
                                         scale=p_sub).then_inc(da_h, 1)
                elif kind == "conv_silu":
                    act.wait_ge(conv_done, 6 * lay + i + 1)
                    nc.scalar.activation(cacc[i % 2], cacc[i % 2], ACT.Silu)
                    act.drain().then_inc(silu_done, 1)
                elif kind == "xs_turn":
                    b, t = i // 2, i % 2
                    act.wait_ge(xs_turned, 8 * lay + i + 1)
                    nc.scalar.copy(xsN[:, t, UC * b:UC * (b + 1)], S[3][:, :]).then_inc(side_free[3], 1)
                    act.drain().then_inc(xs_ready, 1)
                elif kind == "dt":
                    act.wait_ge(dt_abs, lay + 1)
                    nc.scalar.activation(dt_e, dt_e, ACT.Exp, scale=-1.0).then_inc(dt_exp, 1)
                    act.wait_ge(dt_u1, lay + 1)
                    nc.scalar.activation(dt_l, dt_u, ACT.Ln).then_inc(dt_ln, 1)
                elif kind == "dt_sums":
                    act.wait_ge(cs_sub, lay + 1)
                    nc.scalar.activation(eo, cs, ACT.Exp)
                    nc.scalar.activation(wgt, wgt, ACT.Exp).then_inc(cs_exp, 1)
                elif kind == "decay":
                    job, d, hf = i // 4, i // 2 % 2, i % 2
                    g, c = job // 2, job % 2
                    act.wait_ge(bc_done, 32 * lay + i + 1)
                    if i >= 3:
                        act.wait_ge(diag_done, 32 * lay + i - 2)
                    for j in range(4):
                        q = 64 * c + SH * d + HPG * g + 4 * hf + j
                        ins = nc.scalar.activation(M[i % 3][:, P * j:P * (j + 1)], S[i % 2][:, P * j:P * (j + 1)],
                                                   ACT.Exp, bias=ncs[:, q:q + 1])
                    ins.then_inc(side_free[i % 2], 1)
                    act.drain().then_inc(exp_done, 1)
                elif kind == "assemble":
                    g, c = i // 2, i % 2
                    act.wait_ge(y_done, 8 * lay + i + 1)
                    nc.scalar.activation(junk[:, :], zN[:, c, UC * g:UC * (g + 1)], ACT.Square,
                                         accum_out=s4[:, i % 4:i % 4 + 1])
                    act.drain().then_inc(st_done, 1)
                elif kind == "ssm_norm":
                    nc.scalar.activation(r4, s4, ACT.Sqrt, bias=eps, scale=1.0 / 512).then_inc(sd_done, 1)
                elif kind == "ssm_out":
                    g, c = i // 2, i % 2
                    act.wait_ge(g_done, 8 * lay + i + 1)
                    t0 = SSM_A + 4 * g
                    nc.scalar.copy(actH[:, t0:t0 + 4, P * c:P * (c + 1)], v3(gtmp, 4)).then_inc(gh_done, 1)
                elif kind == "merged":
                    act.wait_ge(mrg_sum, 2 * lay + i + 1)
                    nc.scalar.activation(actH[:, MRG_A + 4 * i:MRG_A + 4 * i + 4, :], mrg[:, 4 * i:4 * i + 4, :],
                                         ACT.Copy, scale=0.5).then_inc(mrg_h, 1)

            with act.Fori(0, DEPTH) as lay:
                mem_act(lay)
                norm_act(lay, 2 * lay + 1)
                act.wait_ge(mem_g, lay + 1)
                nc.scalar.copy(actH[:, MEM_A:MEM_A + KT, :], v3(mtmp, KT)).then_inc(mem_h, 1)
                for u in range(LOOKAHEAD):
                    split_h(lay, u)

                def unit(u, g, c):
                    if u + LOOKAHEAD < UNITS:
                        split_h(lay, u + LOOKAHEAD)

                def group_end(g):
                    kind, b = GROUPS[g][:2]
                    if kind == "ffn":
                        hidden_gate(lay, g)
                        hidden_h(lay, g, slice(2 * b * T, (2 * b + 2) * T))
                    else:
                        evac(lay, g)
                    if kind == "dt":
                        step(lay, "dt", b)
                    if kind == "br1":
                        step(lay, "merged", b)

                def ffn_loop(g):
                    u0 = FIRST_UNIT[g]
                    with act.Fori(0, FFN_LOOP) as i:
                        for c in range(8):
                            split_h(lay, u0 + c + LOOKAHEAD, 2 * i)
                            if c % 4 == 3:
                                hidden_gate(lay, g + c // 4, i)
                                hidden_h(lay, g + c // 4, bass.ds((4 * i + 2 * (c // 4)) * T, 2 * T), i)

                each_step(unit, group_end, lambda *s: step(lay, *s), ffn_loop)
            norm_act(DEPTH, 2 * DEPTH + 1)
            norm_root(2 * DEPTH + 1)

        @block.gpsimd
        def _(pool):
            nc.gpsimd.iota(xT_t[:, 256:768], pattern=[[P, NT], [-1, T]], base=0, channel_multiplier=1,
                           allow_small_or_imprecise_dtypes=True)
            tmp = [scr[:, 2560 + P * i:2560 + P * (i + 1)] for i in range(3)]
            nc.gpsimd.memset(ident[:, :], 0.0)
            for i in range(3):
                nc.gpsimd.memset(tmp[i], 1.0)
            pool.drain()
            nc.gpsimd.affine_select(out=ident[:, :], in_=ident[:, :], compare_op=ALU.not_equal, fill=1.0, base=0,
                                    pattern=[[-1, P]], channel_multiplier=1)
            nc.gpsimd.affine_select(out=tmp[0], in_=tmp[0], compare_op=ALU.is_ge, fill=0.0, base=0,
                                    pattern=[[1, P]], channel_multiplier=-1)
            nc.gpsimd.affine_select(out=tmp[1], in_=tmp[1], compare_op=ALU.is_ge, fill=0.0, base=0,
                                    pattern=[[-1, P]], channel_multiplier=1)
            pool.drain().then_inc(pool_ready, 1)

            def split_l(lay, u, extra=0):
                slot = u % RING
                if not pool_splits(u):
                    return
                n = use(lay, u) + extra
                q = slice(0, 256 if GROUPS[UNIT_GROUP[u]][0] == "dt" else UT * UC)
                pool.wait_ge(h_done[slot], n + 1)
                nc.gpsimd.tensor_tensor(wL[:, slot].rearrange("p k c -> p (k c)")[:, q],
                                        raw[:, slot].rearrange("p k c -> p (k c)")[:, q],
                                        wH[:, slot].rearrange("p k c -> p (k c)")[:, q].bitcast(F32),
                                        ALU.subtract).then_inc(l_done[slot], 1)

            def step(lay, kind, i):
                if kind == "scale":
                    job, d = i // 2, i % 2
                    g, c = job // 2, job % 2

                    def scaled(dst, chunk, weights, q):
                        q += 64 * chunk + HPG * g
                        return nc.gpsimd.tensor_tensor(v3(dst, HPG), v3(xsN[:, chunk, UC * g:UC * (g + 1)], HPG),
                                                       weights[:, q:q + HPG].unsqueeze(2).broadcast_to([P, HPG, DH]),
                                                       ALU.mult)

                    if i == 0:
                        pool.wait_ge(xs_ready, 8 * lay + 8)
                        pool.wait_ge(dt_ready, lay + 1)
                    if job > 0:
                        pool.wait_ge(diag_done, 32 * lay + 4 * job - 2 + 2 * d)
                    scaled(xd[d], c, dtv, SH * d).then_inc(xd_done, 1)
                    if d == 0:
                        if job > 0:
                            pool.wait_ge(off_done, 8 * lay + job)
                        scaled(xw, 1 - c, wgt, SH * (1 - c)).then_inc(xw_done, 1)
                elif kind == "off":
                    g, c = i // 2, i % 2
                    if i > 0:
                        pool.wait_ge(y_done, 8 * lay + i)
                    nc.gpsimd.tensor_tensor(v3(xsd, HPG), v3(xsN[:, c, UC * g:UC * (g + 1)], HPG),
                                            r_D[:, HPG * g:HPG * (g + 1)].unsqueeze(2).broadcast_to([P, HPG, DH]),
                                            ALU.mult).then_inc(xsd_done, 1)

            with pool.Fori(0, DEPTH) as lay:
                for u in range(LOOKAHEAD):
                    split_l(lay, u)

                def ffn_loop(g):
                    u0 = FIRST_UNIT[g]
                    with pool.Fori(0, FFN_LOOP) as i:
                        for c in range(8):
                            split_l(lay, u0 + c + LOOKAHEAD, 2 * i)

                each_step(lambda u, g, c: split_l(lay, u + LOOKAHEAD) if u + LOOKAHEAD < UNITS else None,
                          lambda g: None, lambda *s: step(lay, *s), ffn_loop)

        @block.vector
        def _(dve):
            v = nc.vector
            for s in range(RING):
                dve.sem_inc(l_done[s], 1)
            for i in range(2):
                dve.sem_inc(psum_free[i], 1)
            for i in range(4):
                dve.sem_inc(side_free[i], 1)
            dve.sem_inc(regb_free, 1)
            dve.sem_inc(up_done, 1)
            v.memset(eps, EPS)
            dve.wait_ge(const_in, 16 * CONST_LOADS)
            lam = scr[:, 2048:2560].rearrange("p (a q c) -> p a q c", a=2, q=2)
            lprod = v3(xT_t[:, 0:256], 2)
            v.tensor_tensor(lprod, lam[:, :, 0, :], lam[:, :, 1, :], ALU.mult)
            dve.drain()
            v.tensor_reduce(lam4, xT_t[:, 0:256].rearrange("p (a c) -> p a c", a=4), AX.X, ALU.add)
            dve.drain().then_inc(setup_v, 1)
            dve.wait_ge(pool_ready, 1)
            for i, t in enumerate((upR, loR, onesR)):
                v.tensor_copy(t[:, :], scr[:, 2560 + P * i:2560 + P * (i + 1)])
            for i in range(2):
                v.tensor_scalar(mask[:, i, :], scr[:, 2560 + P * i:2560 + P * (i + 1)], -1.0, 1e30, ALU.add, ALU.mult)
            v.tensor_copy(identB[:, :], ident[:, :])
            v.tensor_scalar(xT_t[:, 768:1280], xT_t[:, 256:768], -1.0, None, ALU.mult)
            dve.drain()
            v.tensor_tensor(dist[:, :], xT_t[:, 256:768], xT_t[:, 768:1280], ALU.max)
            dve.wait_ge(setup_a, 1)
            v.tensor_tensor(nlam2, lam4[:, 2:4], lam4[:, 0:2], ALU.subtract)
            dve.drain()
            for lay in range(DEPTH):
                v.tensor_scalar(nlam2[:, lay:lay + 1], nlam2[:, lay:lay + 1], -lambda_init(lay), None, ALU.add)
            dve.wait_ge(setup_t, 1)
            v.tensor_copy(par[:, 0:378], PS[0][:, 0:378])
            dve.drain()
            for lay in range(DEPTH):
                v.tensor_scalar(sub2[:, lay:lay + 1], par[:, 376 + lay:377 + lay], 1.0 - lambda_init(lay), None,
                                ALU.mult)
            for b in range(4):
                dve.wait_ge(setup_t, 2 + b)
                v.tensor_copy(xT[:, 2 * b:2 * b + 2, :], v3(S[b][:, :], 2))
            dve.drain().then_inc(setup_v, 1)
            dve.sem_inc(x_ready, 1)

            def split_l(lay, u, extra=0):
                slot = u % RING
                if pool_splits(u):
                    return
                n = use(lay, u) + extra
                q = slice(0, 256 if GROUPS[UNIT_GROUP[u]][0] == "dt" else UT * UC)
                dve.wait_ge(h_done[slot], n + 1)
                v.tensor_tensor(wL[:, slot].rearrange("p k c -> p (k c)")[:, q],
                                raw[:, slot].rearrange("p k c -> p (k c)")[:, q],
                                wH[:, slot].rearrange("p k c -> p (k c)")[:, q].bitcast(F32),
                                ALU.subtract).then_inc(l_done[slot], 1)

            def low(out_l, full, high, scale=None):
                if scale is None:
                    return v.tensor_tensor(out_l, full, high.bitcast(F32), ALU.subtract)
                return v.scalar_tensor_tensor(out_l, full, scale, high.bitcast(F32), ALU.mult, ALU.subtract)

            def gains(g, n, width):
                return g.unsqueeze(2).broadcast_to([P, n, width])

            def norm_gain(which, g):
                dve.wait_ge(x_ready, which)
                v.tensor_tensor(htmp, xT, gains(g, KT, T), ALU.mult)

            def norm_scale(which):
                dve.wait_ge(std_done, which)
                v.reciprocal(rstd, std)
                dve.drain()
                v.tensor_tensor(htmp, htmp, rstd.unsqueeze(1).broadcast_to([P, KT, T]), ALU.mult)
                dve.drain().then_inc(hn_done, 1)

            def norm_low(which):
                dve.wait_ge(hh_done, which)
                low(hL, htmp, hH).then_inc(h_ready, 1)

            def params(lay):
                v.tensor_copy(lp[:, 0:128], par[:, bass.ds(lay * 128, 128)])
                v.tensor_copy(p_cb, par[:, bass.ds(lay * 24 + 256, 24)])
                v.tensor_copy(p_mix, par[:, bass.ds(lay * 8 + 304, 8)])
                v.tensor_copy(p_ffn, par[:, bass.ds(lay * 8 + 320, 8)])
                v.tensor_copy(p_ssm, par[:, bass.ds(lay * 16 + 336, 16)])
                v.tensor_copy(p_sub, sub2[:, bass.ds(lay, 1)])
                v.tensor_copy(p_nlam, nlam2[:, bass.ds(lay, 1)])
                v.tensor_copy(lrow[:, :], rows[:, bass.ds(lay * 160, 160)])
                dve.drain().then_inc(lp_ready, 1)

            def mem_part(lay):
                dve.wait_ge(mem_std, lay + 1)
                v.reciprocal(mr, mr)
                dve.drain()
                for t in range(NT):
                    v.tensor_scalar(memN[:, t, :], memN[:, t, :], mr[:, t:t + 1], None, ALU.mult)
                dve.drain().then_inc(mem_scaled, 1)
                for b in range(4):
                    dve.wait_ge(mem_turned, 4 * lay + b + 1)
                    v.tensor_tensor(v3(mtmp[:, 512 * b:512 * (b + 1)], 2), v3(S[b][:, :], 2),
                                    gains(p_mem[:, 2 * b:2 * b + 2], 2, T), ALU.mult).then_inc(side_free[b], 1)
                dve.drain().then_inc(mem_g, 1)

            def evac(lay, g, extra=0):
                kind, b = GROUPS[g][:2]
                pair = g % 2
                src = PS[pair]
                tiles = slice(4 * b, 4 * b + 4) if kind != "ffn" else None
                if kind == "dt":
                    wait_full(dve, lay, g)
                    bias = r_dtb.unsqueeze(1).broadcast_to([P, NT, 64])
                    v.tensor_tensor(v3(dt_x, NT), v3(src[:, 0:P], NT), bias, ALU.add)
                    dve.drain().then_inc(psum_free[pair], 1)
                    v.scalar_tensor_tensor(dt_e, dt_x, -1.0, dt_x, ALU.mult, ALU.max)
                    dve.drain().then_inc(dt_abs, 1)
                    dve.wait_ge(dt_exp, lay + 1)
                    v.tensor_scalar(dt_u, dt_e, 1.0, None, ALU.add)
                    dve.drain().then_inc(dt_u1, 1)
                    v.scalar_tensor_tensor(dt_c, dt_u, -1.0, dt_e, ALU.add, ALU.subtract)
                    v.reciprocal(aN, dt_u)
                    dve.drain()
                    v.tensor_tensor(dt_c, dt_c, aN, ALU.mult)
                    dve.drain()
                    dve.wait_ge(dt_ln, lay + 1)
                    v.tensor_tensor(dt_c, dt_l, dt_c, ALU.subtract)
                    dve.drain()
                    v.scalar_tensor_tensor(dtv, dt_x, 0.0, dt_c, ALU.max, ALU.add)
                    dve.drain()
                    v.scalar_tensor_tensor(v3(aN, NT), v3(dtv, NT), -1.0,
                                           r_A.unsqueeze(1).broadcast_to([P, NT, 64]), ALU.mult, ALU.mult)
                    dve.drain()
                    v.tensor_copy(aH_t[:, :], aN)
                    dve.drain()
                    low(aL_t[:, :], aN, aH_t[:, :]).then_inc(a_ready, 1)
                elif kind.startswith("br"):
                    gate = g - 1
                    dve.wait_ge(psum_free[gate % 2], used_after(lay, gate))
                    wait_full(dve, lay, g)
                    if kind == "br0":
                        v.scalar_tensor_tensor(mrg[:, tiles, :], v3(sg, 4), 1.0, v3(src[:, :], 4), ALU.add,
                                               ALU.mult)
                        dve.drain().then_inc(psum_free[pair], 1)
                    else:
                        v.scalar_tensor_tensor(v3(sg, 4), v3(sg, 4), 1.0, v3(src[:, :], 4), ALU.add, ALU.mult)
                        dve.drain()
                        v.tensor_tensor(mrg[:, tiles, :], mrg[:, tiles, :], v3(sg, 4), ALU.add)
                        dve.drain().then_inc(psum_free[pair], 1)
                    if kind == "br1":
                        dve.drain().then_inc(mrg_sum, 1)
                        dve.wait_ge(mrg_h, 2 * lay + b + 1)
                        low(actL[:, MRG_A + 4 * b:MRG_A + 4 * b + 4, :], mrg[:, tiles, :],
                            actH[:, MRG_A + 4 * b:MRG_A + 4 * b + 4, :], 0.5).then_inc(mrg_ready, 1)
                elif kind in ("out", "down"):
                    wait_full(dve, lay, g)
                    v.tensor_tensor(xT[:, tiles, :], xT[:, tiles, :], v3(src[:, :], 4), ALU.add
                                    ).then_inc(psum_free[pair], 1)
                    if b == 1:
                        dve.drain().then_inc(x_ready, 1)
                        if kind == "out":
                            dve.drain().then_inc(regb_free, 1)

            def hidden(lay, g, tile, extra=0):
                pair = g % 2
                n = N_FFN * lay + (g - GI["ffn", 0]) + 2 * extra
                dve.wait_ge(gate_done, n + 1)
                v.tensor_tensor(hid, sg[:, 0:512], PS[pair][:, 512:1024], ALU.mult).then_inc(psum_free[pair], 1)
                dve.drain().then_inc(up_done, 1)
                dve.wait_ge(hid_h, n + 1)
                low(actL_t[:, tile], hid, actH_t[:, tile]).then_inc(hid_ready, 1)
                dve.drain()

            def step(lay, kind, i):
                if kind == "norm_sum":
                    if i == 1:
                        norm_gain(2 * lay + 2, p_ffn)
                    norm_scale(2 * lay + i + 1)
                    norm_low(2 * lay + i + 1)
                elif kind == "xa_scores":
                    b = i % 2
                    dve.wait_ge(xa_sc, XH * lay + i + 1)
                    v.tensor_reduce(mx[b][:, 0:2], v3(S[b][:, :], 2), AX.X, ALU.max)
                    dve.drain()
                    v.tensor_scalar(nmx[b][:, 0:2], mx[b][:, 0:2], -1.0 / 16.0, None, ALU.mult).then_inc(xa_max, 1)
                    dve.wait_ge(xa_exp, XH * lay + i + 1)
                    v.reciprocal(rs[b][:, 0:2], sm[b][:, 0:2])
                    dve.drain()
                    for t in range(NT):
                        q = sc[b][:, T * t:T * (t + 1)]
                        v.tensor_scalar(q, q, rs[b][:, t:t + 1], None, ALU.mult)
                    dve.drain().then_inc(xa_p, 1)
                elif kind == "xa_values":
                    dve.wait_ge(xa_h, XH * lay + i + 1)
                    q = slice(XA_A + 2 * i, XA_A + 2 * i + 2)
                    low(actL[:, q, :], v3(S[2][:, :], 2), actH[:, q, :]).then_inc(side_free[2], 1)
                    dve.drain().then_inc(xa_y, 1)
                elif kind == "da_scores":
                    b = i % 2
                    dve.wait_ge(da_sc, HEADS * lay + i + 1)
                    if i >= 2:
                        dve.wait_ge(da_turned, HEADS * lay + i - 1)
                    else:
                        dve.wait_ge(xa_turned, XH * lay + XH)
                    for m in range(2):
                        v.scalar_tensor_tensor(sc[b][:, 512 * m:512 * (m + 1)], dist[:, :], -8.0 * slope(i),
                                               S[m][:, :], ALU.mult, ALU.add).then_inc(side_free[m], 1)
                    dve.drain()
                    v.tensor_reduce(mx[b], v3(sc[b], 4), AX.X, ALU.max)
                    dve.drain()
                    v.tensor_scalar(nmx[b], mx[b], -0.125, None, ALU.mult).then_inc(da_max, 1)
                elif kind == "da_combine":
                    b = i % 2
                    dve.wait_ge(da_exp, HEADS * lay + i + 1)
                    v.reciprocal(rs[b], sm[b])
                    dve.drain()
                    v.tensor_scalar(nl[b], rs[b][:, 2:4], p_nlam, None, ALU.mult)
                    dve.drain()
                    for t in range(NT):
                        q = sc[b][:, 512 + T * t:512 + T * (t + 1)]
                        v.tensor_scalar(q, q, nl[b][:, t:t + 1], None, ALU.mult)
                    dve.drain()
                    for t in range(NT):
                        v.scalar_tensor_tensor(sc[b][:, T * t:T * (t + 1)], sc[b][:, T * t:T * (t + 1)],
                                               rs[b][:, t:t + 1], sc[b][:, 512 + T * t:512 + T * (t + 1)],
                                               ALU.mult, ALU.add)
                    dve.drain().then_inc(da_att, 1)
                elif kind == "da_norm":
                    dve.wait_ge(da_sd, 2 * lay + i + 1)
                    v.reciprocal(sr, sr)
                    dve.drain()
                    v.tensor_tensor(yN, yN, gains(sr, HALF * NT, P), ALU.mult)
                    dve.drain().then_inc(da_n, 1)
                elif kind == "da_out":
                    dve.wait_ge(da_h, 4 * lay + i + 1)
                    q = slice(DA_A + 2 * i, DA_A + 2 * i + 2)
                    low(actL[:, q, :], v3(S[3][:, :], 2), actH[:, q, :], p_sub).then_inc(side_free[3], 1)
                    dve.drain().then_inc(da_y, 1)
                elif kind == "conv":
                    b, g = i // 2, GI["xbc", i // 2]
                    if i % 2 == 0:
                        dve.wait_ge(psum_free[g % 2], used_after(lay, g))
                        if b >= 2:
                            dve.wait_ge(xs_turned, 8 * lay + 2 * b - 2)
                    js = range(2 * (i % 2), 2 * (i % 2) + 2)
                    for j in js:
                        t = 4 * b + j
                        v.tensor_scalar(cacc[b % 2][:, j, :], cin[:, j, 0:T], p_cw[:, t:t + 1], p_cb[:, t:t + 1],
                                        ALU.mult, ALU.add)
                    for k in range(1, CONV):
                        dve.drain()
                        for j in js:
                            q = CONV_T * k + 4 * b + j
                            v.scalar_tensor_tensor(cacc[b % 2][:, j, :], cin[:, j, k:k + T], p_cw[:, q:q + 1],
                                                   cacc[b % 2][:, j, :], ALU.mult, ALU.add)
                    done = dve.drain()
                    if i % 2 == 1:
                        done.then_inc(conv_done, 1)
                elif kind == "dt_sums":
                    dve.wait_ge(cs_done, lay + 1)
                    v.tensor_copy(cs, S[0][:, 0:P])
                    v.tensor_scalar(ncs, S[0][:, 0:P], -1.0, None, ALU.mult)
                    dve.drain()
                    v.tensor_tensor(wgt, S[0][:, P:2 * P], cs, ALU.subtract).then_inc(side_free[0], 1)
                    dve.drain().then_inc(cs_sub, 1)
                    dve.wait_ge(cs_exp, lay + 1)
                    v.tensor_tensor(wgt, wgt, dtv, ALU.mult).then_inc(dt_ready, 1)
                elif kind == "cb":
                    dve.wait_ge(cb_done, SG * lay + i + 1)
                    if i > 0:
                        dve.wait_ge(off_done, 8 * lay + 2 * i)
                    v.tensor_copy(cb, S[0][:, :]).then_inc(side_free[0], 1)
                    dve.drain().then_inc(cb_ready, 1)
                elif kind == "decay":
                    c = i // 4 % 2
                    dve.wait_ge(exp_done, 32 * lay + i + 1)
                    blk = cb[:, (T + P) * c:(T + P) * c + P]
                    v.tensor_tensor(v3(M[i % 3], 4), v3(M[i % 3], 4), blk.unsqueeze(1).broadcast_to([P, 4, P]),
                                    ALU.mult)
                    dve.drain().then_inc(m_done, 1)
                elif kind == "assemble":
                    g, c = i // 2, i % 2
                    d = 1 - c
                    dve.wait_ge(off_done, 8 * lay + i + 1)
                    q = 64 * c + SH * d + HPG * g
                    v.tensor_tensor(v3(ytmp, HPG), v3(S[3][:, :], HPG), gains(eo[:, q:q + HPG], HPG, DH), ALU.mult)
                    dve.drain().then_inc(side_free[3], 1)
                    dve.wait_ge(diag_done, 32 * lay + 4 * i + 4)
                    v.tensor_tensor(ytmp, ytmp, S[2][:, :], ALU.add)
                    dve.drain().then_inc(side_free[2], 1)
                    dve.wait_ge(xsd_done, 8 * lay + i + 1)
                    v.tensor_tensor(ytmp, ytmp, xsd, ALU.add)
                    dve.drain()
                    if i % 2 == 0:
                        wait_evacuated(dve, lay, "z", g)
                    zq = zN[:, c, UC * g:UC * (g + 1)]
                    v.tensor_tensor(zq, zq, ytmp, ALU.mult)
                    dve.drain().then_inc(y_done, 1)
                elif kind == "ssm_norm":
                    dve.wait_ge(sd_done, 2 * lay + i + 1)
                    v.reciprocal(r4, r4)
                    dve.drain()
                    for q in range(4):
                        g, c = 2 * i + q // 2, q % 2
                        zq = zN[:, c, UC * g:UC * (g + 1)]
                        v.tensor_scalar(zq, zq, r4[:, q:q + 1], None, ALU.mult)
                    dve.drain().then_inc(n_done, 1)
                elif kind == "ssm_out":
                    g, c = i // 2, i % 2
                    dve.wait_ge(yt_done, 8 * lay + i + 1)
                    v.tensor_tensor(v3(gtmp, 4), v3(S[3][:, :], 4), gains(p_ssm[:, 4 * g:4 * g + 4], 4, P),
                                    ALU.mult).then_inc(side_free[3], 1)
                    dve.drain().then_inc(g_done, 1)
                    dve.wait_ge(gh_done, 8 * lay + i + 1)
                    t0 = SSM_A + 4 * g
                    low(actL[:, t0:t0 + 4, P * c:P * (c + 1)], v3(gtmp, 4),
                        actH[:, t0:t0 + 4, P * c:P * (c + 1)])
                    dve.drain().then_inc(ssm_y, 1)

            with dve.Fori(0, DEPTH) as lay:
                params(lay)
                mem_part(lay)
                norm_gain(2 * lay + 1, p_mix)
                dve.wait_ge(mem_h, lay + 1)
                low(actL[:, MEM_A:MEM_A + KT, :], v3(mtmp, KT), actH[:, MEM_A:MEM_A + KT, :]
                    ).then_inc(mem_ready, 1)
                for u in range(LOOKAHEAD):
                    split_l(lay, u)
                v.memset(cin[:, :, 0:2], 0.0)
                v.memset(cin[:, :, 2 + T:4 + T], 0.0)

                def unit(u, g, c):
                    if u + LOOKAHEAD < UNITS:
                        split_l(lay, u + LOOKAHEAD)

                def group_end(g):
                    kind, b = GROUPS[g][:2]
                    if kind == "ffn":
                        hidden(lay, g, slice(2 * b * T, (2 * b + 2) * T))
                    else:
                        evac(lay, g)

                def ffn_loop(g):
                    u0 = FIRST_UNIT[g]
                    with dve.Fori(0, FFN_LOOP) as i:
                        for c in range(8):
                            split_l(lay, u0 + c + LOOKAHEAD, 2 * i)
                            if c % 4 == 3:
                                hidden(lay, g + c // 4, bass.ds((4 * i + 2 * (c // 4)) * T, 2 * T), i)

                each_step(unit, group_end, lambda *s: step(lay, *s), ffn_loop)
            norm_gain(2 * DEPTH + 1, par[:, 368:376])
            norm_scale(2 * DEPTH + 1)
            for b in range(4):
                dve.wait_ge(fin_turned, b + 1)
                v.tensor_copy(xload[:, :, T * b:T * (b + 1)], v3(S[b][:, :], 2)).then_inc(fin_copied, 1)


_INS = ["x", "mem", "mix_norm_g", "w_in", "da_lambda_q1", "da_lambda_k1", "da_lambda_q2", "da_lambda_k2",
        "da_subln_g", "ssm_conv_w", "ssm_conv_b", "ssm_dt_bias", "ssm_A_log", "ssm_D", "ssm_norm_g", "mem_norm_g",
        "w_mem_kv", "w_branch", "w_out", "ffn_norm_g", "w_ffn_in", "w_ffn_out", "final_norm_g"]


def kernel(**inputs):
    import numpy as _np
    import concourse.bacc as _bacc
    from concourse import mybir as _mybir
    from concourse.bass_utils import run_bass_kernel_spmd as _run

    nc = _bacc.Bacc("TRN2", target_bir_lowering=False, num_devices=1, dynamic_dma_scratch_size=1024)
    arrays, args = {}, []
    for name in _INS:
        a = _np.ascontiguousarray(inputs[name])
        arrays[f"in_{name}_dram"] = a
        args.append(nc.dram_tensor(f"in_{name}_dram", a.shape, _mybir.dt.from_np(a.dtype), kind="ExternalInput").ap())
    o = nc.dram_tensor("out_0_dram", (1, T, D), _mybir.dt.float32, kind="ExternalOutput").ap()
    build(nc, *args, o, SIDE_USES)
    r = _run(nc, [arrays], core_ids=[0])
    return r.results[0]["out_0_dram"]
```

```python
import math
from contextlib import ExitStack

import concourse.bass as bass
from concourse import mybir

F32 = mybir.dt.float32
F32R = mybir.dt.float32r
BF16 = mybir.dt.bfloat16
ACT = mybir.ActivationFunctionType
ALU = mybir.AluOpType
AX = mybir.AxisListType

P = 128
D = 1024
T = 256
NT = T // P
KT = D // P
DEPTH = 2
EPS = 1e-6
HEADS, HALF = 8, 4
DH = 64
XH = 4
SH, SG = 32, 4
HPG = SH // SG
INNER = 2 * D
CONV = 5
FFN = 2816
FT = FFN // P
DA_Q, DA_K, DA_V = 0, D, 2 * D
Z0 = 3 * D
XBC0 = Z0 + INNER
DT0 = XBC0 + INNER + 2 * SG * P
XQ0 = DT0 + 2 * SH
GATE0 = XQ0 + D
CONV_T = (INNER + 2 * SG * P) // P

RING = 4
LOOKAHEAD = 3
UT = 2
UC = 512


def lambda_init(layer):
    return 0.8 - 0.6 * math.exp(-0.3 * layer)


def slope(head):
    return 2.0 ** (-(head + 1))


def layer_groups():
    g = [("mk", b, 4, "T") for b in range(2)] + [("mv", b, 4, "N") for b in range(2)]
    g += [("xq", b, 4, "T") for b in range(2)]
    g += [("dt", 0, 2, "D")]
    for half in range(2):
        g += [("q", half, 4, "T"), ("k", half, 4, "T"), ("v", half, 4, "N")]
    g += [("xbc", b, 4, "T") for b in range(CONV_T // 4)]
    g += [("z", b, 4, "N") for b in range(4)]
    for branch, units in ((0, 4), (2, 4)):
        for nb in range(2):
            g += [(f"gate{branch}", nb, 4, "T"), (f"br{branch}", nb, units, "T")]
    for nb in range(2):
        g += [("gate1", nb, 4, "T"), ("br1", nb, 8, "T")]
    g += [("out", nb, 4, "T") for nb in range(2)]
    g += [("ffn", b, 4, "T") for b in range(FT // 2)]
    g += [("down", nb, FT // UT, "T") for nb in range(2)]
    return g


GROUPS = layer_groups()
FIRST_UNIT = [sum(x[2] for x in GROUPS[:i]) for i in range(len(GROUPS))]
UNITS = sum(x[2] for x in GROUPS)
NGROUPS = len(GROUPS)
UNIT_GROUP = [i for i, x in enumerate(GROUPS) for _ in range(x[2])]
assert UNITS % RING == 0 and NGROUPS % 2 == 0
GI = {(x[0], x[1]): i for i, x in enumerate(GROUPS)}
N_FFN = FT // 2
FFN_FIRST = 1
FFN_LOOP = (N_FFN - 2) // 2


def layer_plan():
    after = {}

    def put(u, *step):
        after.setdefault(u, []).append(step)

    put(1, "norm_square", 0)
    put(4, "norm_sum", 0)
    put(5, "norm_root", 0)
    put(7, "norm_split", 0)
    u = FIRST_UNIT[GI["q", 0]]
    for h in range(XH):
        put(u + 1 + 3 * h, "xa_scores", h)
        put(u + 3 + 3 * h, "xa_turn", h)
        put(u + 4 + 3 * h, "xa_values", h)
    put(u + 6, "dt_sums", 0)
    u = FIRST_UNIT[GI["q", 1]]
    for h in range(HEADS):
        at = u + (1 + 3 * h if h < HALF else 4 * h)
        put(at, "da_scores", h)
        put(at + 2, "da_combine", h)
        put(at + 3 + (h >= HALF), "da_turn", h)
        put(at + 4 + (h >= HALF), "da_values", h)
    put(u + 15, "da_norm", 0)
    put(u + 17, "da_out", 0)
    put(u + 19, "da_out", 1)
    put(u + 34, "da_norm", 1)
    put(u + 37, "da_out", 2)
    put(u + 39, "da_out", 3)
    u = FIRST_UNIT[GI["xbc", 0]]
    for b in range(CONV_T // 4):
        put(u + 4 * b + 4, "conv", 2 * b)
        put(u + 4 * b + 5, "conv", 2 * b + 1)
        put(u + 4 * b + 6, "conv_silu", b)
        if b < INNER // P // 4:
            put(u + 4 * b + 9, "xs_turn", 2 * b)
            put(u + 4 * b + 10, "xs_turn", 2 * b + 1)
    u = FIRST_UNIT[GI["z", 0]]
    quads = SG * NT * 4
    start, per = u + 5, 1.28
    for q in range(quads):
        put(start + int(per * q) - 3, "spread", q)
    for q in range(quads + 3):
        at = start + int(per * q)
        if q % 4 == 1 and q > 1:
            put(at, "off", q // 4 - 1)
        if q < quads:
            if q % 4 == 2:
                put(at, "scale", q // 4)
            put(at, "decay_sums", q)
            if q % 8 == 1:
                put(at, "cb", q // 8)
        if 1 <= q <= quads:
            put(at, "decay", q - 1)
        if q >= 4 and q % 2 == 0:
            put(at, "diag", q // 2 - 2)
        if q >= 6 and q % 4 == 2:
            put(at, "assemble", q // 4 - 1)
            if q in (18, 34):
                put(at + 1, "ssm_norm", q // 32)
        if q in (23, 24, 27, 28):
            put(at, "ssm_out", (23, 24, 27, 28).index(q))
    for r in range(4):
        put(at + 3 + r, "ssm_out", 4 + r)
    put(FIRST_UNIT[GI["out", 1]], "ffn_input", 0)
    put(FIRST_UNIT[GI["out", 1]] + 2, "ffn_sum", 0)
    put(FIRST_UNIT[GI["out", 1]] + 3, "ffn_input", 1)
    put(FIRST_UNIT[GI["ffn", 0]] + 2, "ffn_sum", 1)
    u = FIRST_UNIT[GI["down", 0]]
    put(u, "mem_load", 0)
    put(u + 6, "mem_scale", 0)
    for b in range(4):
        put(u + 8 + 2 * b, "mem_turn", b)
        put(u + 9 + 2 * b, "mem_split", b)
    return after


AFTER = layer_plan()


def pool_splits(u):
    u %= UNITS
    busy = FIRST_UNIT[GI["q", 1]] + 4 <= u < FIRST_UNIT[GI["z", 0]] + 48
    return u % 2 == 1 or busy


SIDE_USES = [34, 27, 29, 33]
PAR_LOADS, ROW_LOADS = 8, 7


def build(nc, x, mem, mix_norm_g, w_in, lq1, lk1, lq2, lk2, subln_g, conv_w, conv_b, dt_bias, A_log, D_skip,
          ssm_norm_g, mem_norm_g, w_mem_kv, w_branch, w_out, ffn_norm_g, w_ffn_in, w_ffn_out, final_norm_g, out,
          side_uses):
    ctx = ExitStack()
    with ctx:
        def sb(name, cols, dtype=F32):
            return ctx.enter_context(nc.sbuf_tensor(name, [P, cols], dtype))

        def sem(name):
            return ctx.enter_context(nc.semaphore(name))

        xT_t = sb("xT", KT * T)
        hH_t, hL_t = sb("hH", KT * T, F32R), sb("hL", KT * T, F32R)
        actH_t, actL_t = sb("actH", 32 * T, F32R), sb("actL", 32 * T, F32R)
        raw_t = sb("w_raw", RING * UT * UC)
        wH_t, wL_t = sb("wH", RING * UT * UC, F32R), sb("wL", RING * UT * UC, F32R)
        regA, regB, scr = sb("regA", 6144), sb("regB", 6144), sb("scr", 6400)
        dts = sb("dts", 5 * P)
        aH_t, aL_t = sb("aH", P, F32R), sb("aL", P, F32R)
        par, lp = sb("par", 3 * P), sb("lp", 192)
        rows, lrow = sb("rows", 2 * 160), sb("lrow", 160)
        dist = sb("dist", NT * T, BF16)
        ident = sb("ident", P)
        upR, loR, onesR, afterR, beforeR = (sb(n, P, F32R) for n in ("upR", "loR", "onesR", "afterR", "beforeR"))
        small = sb("small", 96)
        junk = sb("junk", UC, BF16)

        def v3(ap, n):
            return ap.rearrange("p (a b) -> p a b", a=n)

        xT = v3(xT_t[:, :], KT)
        hH, hL = v3(hH_t[:, :], KT), v3(hL_t[:, :], KT)
        actH, actL = v3(actH_t[:, :], 32), v3(actL_t[:, :], 32)
        raw = raw_t[:, :].rearrange("p (s k c) -> p s k c", s=RING, k=UT)
        wH = wH_t[:, :].rearrange("p (s k c) -> p s k c", s=RING, k=UT)
        wL = wL_t[:, :].rearrange("p (s k c) -> p s k c", s=RING, k=UT)
        DA_A, SSM_A, XA_A, MEM_A, MRG_A = 0, 8, 24, 22, 0
        mkT, mvN, xqT = v3(regA[:, 0:2048], KT), v3(regA[:, 2048:4096], NT), v3(regA[:, 4096:6144], KT)
        BT, CT, xsN = v3(regA[:, 0:1024], SG), v3(regA[:, 1024:2048], SG), v3(regA[:, 2048:6144], NT)
        memN, mtmp = v3(regA[:, 0:2048], NT), regA[:, 2048:4096]
        sqT, htmp = v3(regB[:, 2048:4096], KT), v3(regB[:, 4096:6144], KT)
        qT = [v3(regB[:, 3072 * i:3072 * i + 1024], HALF) for i in range(2)]
        kT = [v3(regB[:, 3072 * i + 1024:3072 * i + 2048], HALF) for i in range(2)]
        vN = [v3(regB[:, 3072 * i + 2048:3072 * i + 3072], NT) for i in range(2)]
        zN, mrg = v3(regB[:, 0:4096], NT), v3(regB[:, 4096:6144], KT)
        std, rstd = regB[:, 2048:2304], regB[:, 2304:2560]
        sc = [scr[:, 1024 * i:1024 * (i + 1)] for i in range(2)]
        attT = v3(scr[:, 2048:2560], NT)
        yN = v3(scr[:, 2560:3584], HALF * NT)
        cin = v3(scr[:, 3584:4624], 4)
        cacc = [BT, CT]
        M = [scr[:, 512 * i:512 * (i + 1)] for i in range(4)]
        cbm = scr[:, 2048:2560].rearrange("p (d c l) -> p d c l", d=2, c=NT)
        cboff = v3(scr[:, 6144:6400], NT)
        ytmp, xsd, xw, gtmp = (scr[:, 2560 + 512 * i:3072 + 512 * i] for i in range(4))
        spH, spL = ([t[:, 16 + 2 * i:18 + 2 * i, :].rearrange("p a b -> p (a b)") for i in range(4)]
                    for t in (actH, actL))
        sg = scr[:, 5120:6144]
        hid = scr[:, 0:512]
        xload = v3(scr[:, 0:2048], NT)
        dtv, aN, cs, eo, wgt = (dts[:, P * i:P * (i + 1)] for i in range(5))
        dt_e, dt_u, dt_x, dt_l, dt_c = (scr[:, P * i:P * (i + 1)] for i in range(5))
        ones = onesR[:, :].bitcast(F32)
        p_cw, p_cb = lp[:, 0:120], lp[:, 128:152]
        p_mix, p_ffn, p_ssm = lp[:, 152:160], lp[:, 160:168], lp[:, 168:184]
        p_sub, p_nlam = lp[:, 184:185], lp[:, 185:186]
        r_dtb, r_A, r_D = lrow[:, 0:64], lrow[:, 64:128], lrow[:, 128:160]
        eps = small[:, 0:1]
        lam4, nlam2, sub2 = small[:, 2:6], small[:, 6:8], small[:, 8:10]
        ms, mr = small[:, 10:12], small[:, 12:14]
        mx = [small[:, 16 + 4 * i:20 + 4 * i] for i in range(2)]
        nmx = [small[:, 24 + 4 * i:28 + 4 * i] for i in range(2)]
        sm = [small[:, 32 + 4 * i:36 + 4 * i] for i in range(2)]
        rs = [small[:, 40 + 4 * i:44 + 4 * i] for i in range(2)]
        nl = [small[:, 48 + 2 * i:50 + 2 * i] for i in range(2)]
        ss, sr = small[:, 56:64], small[:, 64:72]
        s4, r4 = small[:, 72:76], small[:, 76:80]
        fstd, frs = small[:, 80:82], small[:, 82:84]
        p_mem = small[:, 88:96]

        PS = [ctx.enter_context(nc.psum_tensor(f"PS{i}", [P, 1024], F32)) for i in range(2)]
        S = [ctx.enter_context(nc.psum_tensor(f"S{i}", [P, 512], F32)) for i in range(4)]

        par_in, row_in, x_in, stored = (sem(n) for n in ("par_in", "row_in", "x_in", "stored"))
        mem_in = [sem(f"mem_in{t}") for t in range(NT)]
        raw_in = [sem(f"raw_in{s}") for s in range(RING)]
        h_done = [sem(f"h_done{s}") for s in range(RING)]
        l_done = [sem(f"l_done{s}") for s in range(RING)]
        unit_used = [sem(f"unit_used{s}") for s in range(RING)]
        psum_free = [sem(f"psum_free{i}") for i in range(2)]
        side_free = [sem(f"side_free{i}") for i in range(4)]
        tri_ready, ident_ready, ones_ready = sem("tri_ready"), sem("ident_ready"), sem("ones_ready")
        par_turned, par_copied, x_turned, lam_sum, lam_exp = (sem(n) for n in (
            "par_turned", "par_copied", "x_turned", "lam_sum", "lam_exp"))
        mem_scaled, mem_turned, mem_g, mem_h, mem_ready, mem_std = (sem(n) for n in (
            "mem_scaled", "mem_turned", "mem_g", "mem_h", "mem_ready", "mem_std"))
        x_half = sem("x_half")
        sq_done, sum_done, std_done, hn_done, hh_done, h_ready = (sem("norm_" + n) for n in (
            "sq", "sum", "std", "scaled", "h", "ready"))
        f_gain, f_high, f_ready, f_sq, f_sum, f_std = (sem("ffn_" + n) for n in (
            "gain", "h", "ready", "sq", "sum", "std"))
        sp_pace = sem("sp_pace")
        xa_sc, xa_max, xa_exp, xa_p, xa_turned, xa_copied, xa_pv, xa_h, xa_y = (sem("xa_" + n) for n in (
            "sc", "max", "exp", "p", "turned", "copied", "pv", "h", "y"))
        da_sc, da_max, da_exp, da_att, da_turned, da_copied, da_pv, da_st, da_sd, da_n, da_yt, da_h, da_y = (
            sem("da_" + n) for n in ("sc", "max", "exp", "att", "turned", "copied", "pv", "st", "sd", "n",
                                     "yt", "h", "y"))
        conv_done, silu_done, xs_turned, xs_ready = (sem(n) for n in (
            "conv_done", "silu_done", "xs_turned", "xs_ready"))
        dt_abs, dt_exp, dt_u1, dt_ln, a_ready, cs_done, cs_sub, cs_exp, dt_ready = (sem(n) for n in (
            "dt_abs", "dt_exp", "dt_u1", "dt_ln", "a_ready", "cs_done", "cs_sub", "cs_exp", "dt_ready"))
        cb_done, cb_ready, spread_done, bc_done, exp_done, m_done, diag_done = (sem("ssm_" + n) for n in (
            "cb", "cb_ready", "spread", "decay", "exp", "m", "diag"))
        pair_done = sem("ssm_pair")
        xw_done, off_done, xsd_done, y_done, st_done, sd_done, n_done, yt_done, g_done, gh_done, ssm_y = (
            sem("ssm_" + n) for n in ("xw", "off", "xsd", "y", "st", "sd", "n", "yt", "g", "gh", "out"))
        sg_used, br_done = sem("sg_used"), sem("br_done")
        mrg_sum, mrg_h, mrg_ready = sem("mrg_sum"), sem("mrg_h"), sem("mrg_ready")
        gate_scaled, gate_done, up_done, hid_h, hid_ready = (sem(n) for n in (
            "gate_scaled", "gate_done", "up_done", "hid_h", "hid_ready"))
        fin_gain, fin_copied = [sem("fin_gain0"), sem("fin_gain1")], [sem("fin_copied_a"), sem("fin_copied_v")]
        fin_sq, fin_sum, fin_std, fin_rstd, fin_turned = (sem("fin_" + n) for n in (
            "sq", "sum", "std", "rstd", "turned"))

        w_in_v = w_in.rearrange("l (k p) c -> l p k c", p=P)
        w_kv_v = w_mem_kv.rearrange("l (k p) c -> l p k c", p=P)
        w_br_v = w_branch.rearrange("l (k p) c -> l p k c", p=P)
        w_out_v = w_out.rearrange("l (k p) c -> l p k c", p=P)
        w_fi_v = w_ffn_in.rearrange("l (k p) (s c) -> l p k s c", p=P, s=2)
        w_fo_v = w_ffn_out.rearrange("l (k p) c -> l p k c", p=P)

        def cols(view, lay, k, col, n=UC):
            return view[lay, :, k:k + UT, col:col + n]

        def unit_source(lay, g, c):
            kind, b, _, _ = GROUPS[g]
            k = UT * c
            if kind == "mk":
                return cols(w_kv_v, lay, k, UC * b)
            if kind == "mv":
                return cols(w_kv_v, lay, k, D + UC * b)
            if kind == "down":
                return cols(w_fo_v, lay, k, UC * b)
            if kind == "out":
                return cols(w_out_v, lay, k, UC * b)
            if kind.startswith("br"):
                first = {"br0": 0, "br1": 8, "br2": 24}[kind]
                return cols(w_br_v, lay, first + k, UC * b)
            col = {"xq": XQ0, "q": DA_Q, "k": DA_K, "v": DA_V, "xbc": XBC0, "z": Z0, "gate0": GATE0,
                   "gate1": GATE0 + D, "gate2": GATE0 + 2 * D}[kind]
            return cols(w_in_v, lay, k, col + UC * b)

        def use(lay, u):
            return lay * (UNITS // RING) + u // RING

        def used_after(lay, g):
            return lay * (NGROUPS // 2) + g // 2 + 2

        def wait_full(eng, lay, g, extra=0):
            u = FIRST_UNIT[g] + GROUPS[g][2] - 1
            eng.wait_ge(unit_used[u % RING], use(lay, u) + extra + 2)

        def wait_evacuated(eng, lay, kind, b):
            g = GI[kind, b]
            eng.wait_ge(psum_free[g % 2], used_after(lay, g))

        def each_step(unit_fn, evac_fn, step_fn, ffn_fn):
            u = 0
            while u < UNITS:
                g = UNIT_GROUP[u]
                if GROUPS[g][:2] == ("ffn", FFN_FIRST):
                    ffn_fn(g)
                    u += 8 * FFN_LOOP
                    continue
                c = u - FIRST_UNIT[g]
                unit_fn(u, g, c)
                if c == GROUPS[g][2] - 1:
                    evac_fn(g)
                for step in AFTER.get(u, []):
                    step_fn(*step)
                u += 1

        def hidden_tiles(i, c):
            return bass.ds((4 * i + 2 * (FFN_FIRST + c // 4)) * T, 2 * T)

        def quad_heads(i):
            job, hf, d = i // 4, i // 2 % 2, i % 2
            return 64 * (job % 2) + SH * d + HPG * (job // 2) + 4 * hf

        block = ctx.enter_context(nc.Block())

        @block.sync
        def _(sp):
            def load_mem():
                for t in range(NT):
                    sp.dma_start(memN[:, t, :], mem[0, P * t:P * (t + 1), :]).then_inc(mem_in[t], 16)

            load_mem()
            prm = v3(sqT.rearrange("p a b -> p (a b)")[:, 0:384], 3)
            sp.dma_start(prm[0:120, 0:DEPTH, :], conv_w.rearrange("l t (c q) -> (t c) l q", q=P)).then_inc(par_in, 16)
            sp.dma_start(prm[120:128, 0:DEPTH, :], mem_norm_g.rearrange("l (c q) -> c l q", q=P)
                         ).then_inc(par_in, 16)
            at = 0
            for v in (conv_b, mix_norm_g, ffn_norm_g, ssm_norm_g):
                src = v.rearrange("l (c q) -> (l c) q", q=P)
                sp.dma_start(prm[at:at + src.shape[0], 2, :], src).then_inc(par_in, 16)
                at += src.shape[0]
            sp.dma_start(prm[112:120, 2, :], final_norm_g.rearrange("(c q) -> c q", q=P)).then_inc(par_in, 16)
            sp.dma_start(prm[120:122, 2, :], subln_g).then_inc(par_in, 16)

            def load(lay, u, extra=0, col=None):
                slot = u % RING
                n = use(lay, u) + extra
                g = UNIT_GROUP[u % UNITS]
                c = u % UNITS - FIRST_UNIT[g]
                kind, b = GROUPS[g][:2]
                sp.wait_ge(l_done[slot], n + 1)
                sp.sem_inc(sp_pace, 1)
                if kind == "ffn":
                    b = col if col is not None else b
                    dst = raw[:, slot].rearrange("p k (s c) -> p k s c", s=2)
                    for k in range(UT):
                        sp.dma_start(dst[:, k], w_fi_v[lay, :, UT * c + k, :, bass.ds(b * T, T)]
                                     ).then_inc(raw_in[slot], 16)
                elif kind == "dt":
                    dst = raw[:, slot].rearrange("p k c -> p (k c)")[:, 0:256].rearrange("p (k c) -> p k c", k=4)
                    sp.dma_start(dst, w_in_v[lay, :, 4 * c:4 * c + 4, DT0:DT0 + 64]).then_inc(raw_in[slot], 32)
                else:
                    src = unit_source(1 - lay if u >= UNITS else lay, g, c)
                    sp.dma_start(raw[:, slot], src).then_inc(raw_in[slot], 32)

            for u in range(LOOKAHEAD):
                load(0, u)

            with sp.Fori(0, DEPTH) as lay:
                def ffn_loads(g):
                    u0 = FIRST_UNIT[g]
                    with sp.Fori(0, FFN_LOOP) as i:
                        for c in range(8):
                            load(lay, u0 + c + LOOKAHEAD, 2 * i, FFN_FIRST + 2 * i + (c + LOOKAHEAD) // 4)

                def step(kind, i):
                    if kind == "mem_load":
                        sp.wait_ge(y_done, 8 * lay + 8)
                        sp.sem_inc(sp_pace, 1)
                        load_mem()

                each_step(lambda u, g, c: load(lay, u + LOOKAHEAD), lambda g: None, step, ffn_loads)
            out_v = out.rearrange("b (t p) d -> p (b t) d", p=P)
            for h in range(2):
                for q in range(2):
                    sp.wait_ge(fin_copied[q], h + 1)
                sp.dma_start(out_v[:, :, UC * h:UC * (h + 1)], xload[:, :, UC * h:UC * (h + 1)]).then_inc(stored, 16)
            sp.wait_ge(stored, 32)

        @block.tensor
        def _(pe):
            side = [0, 0, 0, 0]

            def take(lay, bank):
                pe.wait_ge(side_free[bank], lay * side_uses[bank] + side[bank] + 1)
                side[bank] += 1

            def mm(o, l, r, first, last):
                return nc.tensor.matmul(o, l, r, start=first, stop=last, skip_group_check=True)

            def turn(dst, src, swap=False):
                for k in range(2):
                    for t in range(NT):
                        at = T * t + P * k if swap else T * k + P * t
                        ins = nc.tensor.transpose(dst[:, at:at + P], src(t, k), ident[:, :])
                return ins

            def mem_turn(n, b):
                take(0 if n is None else n, b)
                pe.wait_ge(mem_scaled, 1 if n is None else n + 2)
                turn(S[b], lambda t, k: memN[:, t, P * (2 * b + k):P * (2 * b + k + 1)]).then_inc(mem_turned, 1)

            def x_turn(b, dst):
                turn(dst, lambda t, k: xload[:, t, P * (2 * b + k):P * (2 * b + k + 1)]).then_inc(x_turned, 1)

            pe.wait_ge(ident_ready, 1)
            pe.wait_ge(par_in, 16 * PAR_LOADS)
            prm = v3(sqT.rearrange("p a b -> p (a b)")[:, 0:384], 3)
            for i in range(3):
                n = 122 if i == 2 else P
                ins = nc.tensor.transpose(PS[1][:, P * i:P * i + n], prm[0:n, i, :], ident[0:n, 0:n])
            ins.then_inc(par_turned, 1)
            for b in range(4):
                mem_turn(None, b)
            pe.wait_ge(x_in, 16)
            pe.wait_ge(par_copied, 1)
            for b in range(2):
                x_turn(b, PS[1][:, 512 * b:512 * (b + 1)])
            for b in range(2, 4):
                take(0, b - 2)
                x_turn(b, S[b - 2])
            setup_side = list(side)

            def operand(kind):
                if kind in ("mk", "mv"):
                    return actH, actL, MEM_A
                if kind.startswith("br"):
                    return actH, actL, {"br0": DA_A, "br1": SSM_A, "br2": XA_A}[kind]
                if kind == "out":
                    return actH, actL, MRG_A
                if kind == "down":
                    return actH, actL, 0
                return hH, hL, 0

            def wait_operand(lay, kind, b, c):
                if kind == "mk" and b == 0:
                    pe.wait_ge(mem_ready, 4 * lay + c + 1)
                elif kind == "xq" and b == 0 and c == 0:
                    pe.wait_ge(h_ready, lay + 1)
                elif kind == "ffn" and b == 0 and c in (0, 2):
                    pe.wait_ge(f_ready, 2 * lay + (1 if c == 0 else 2))
                elif kind == "br0" and b == 0 and c == 0:
                    pe.wait_ge(da_y, 4 * lay + 4)
                elif kind == "br2" and b == 0 and c == 0:
                    pe.wait_ge(xa_y, XH * lay + XH)
                elif kind == "br1" and b == 0 and c in (0, 4):
                    pe.wait_ge(ssm_y, 8 * lay + (4 if c == 0 else 8))
                elif kind == "out" and b == 0 and c in (0, 2):
                    pe.wait_ge(mrg_ready, 2 * lay + (1 if c == 0 else 2))
                elif kind == "down" and b == 0:
                    pe.wait_ge(hid_ready, N_FFN * lay + c + 1)

            def unit(lay, u, g, c, extra_u=0, extra_g=0):
                kind, b, units, layout = GROUPS[g]
                slot, pair = u % RING, g % 2
                dst = PS[pair]
                if c == 0:
                    pe.wait_ge(psum_free[pair], lay * (NGROUPS // 2) + g // 2 + extra_g + 1)
                wait_operand(lay, kind, b, c)
                pe.wait_ge(l_done[slot], use(lay, u) + extra_u + 2)
                aH_, aL_, a0 = operand(kind)
                last_unit = c == units - 1
                if layout == "T":
                    for m in range(4):
                        for kk in range(UT):
                            k = a0 + UT * c + kk
                            w_h, w_l = wH[:, slot, kk, P * m:P * (m + 1)], wL[:, slot, kk, P * m:P * (m + 1)]
                            o = dst[:, T * m:T * (m + 1)]
                            new = c == 0 and kk == 0
                            mm(o, w_h, aH_[:, k, :], new and m % 2 == 0, False)
                            mm(o, w_h, aL_[:, k, :], False, False)
                            ins = mm(o, w_l, aH_[:, k, :], False, last_unit and kk == UT - 1)
                elif layout == "N":
                    for t in range(NT):
                        for kk in range(UT):
                            k = a0 + UT * c + kk
                            a_h, a_l = aH_[:, k, P * t:P * (t + 1)], aL_[:, k, P * t:P * (t + 1)]
                            o = dst[:, UC * t:UC * (t + 1)]
                            new = c == 0 and kk == 0
                            mm(o, a_h, wH[:, slot, kk, :], new, False)
                            mm(o, a_l, wH[:, slot, kk, :], False, False)
                            ins = mm(o, a_h, wL[:, slot, kk, :], False, last_unit and kk == UT - 1)
                else:
                    w_h = wH[:, slot].rearrange("p k c -> p (k c)")
                    w_l = wL[:, slot].rearrange("p k c -> p (k c)")
                    for t in range(NT):
                        for kk in range(4):
                            k = 4 * c + kk
                            a_h, a_l = aH_[:, k, P * t:P * (t + 1)], aL_[:, k, P * t:P * (t + 1)]
                            o = dst[:, 64 * t:64 * (t + 1)]
                            q = slice(64 * kk, 64 * (kk + 1))
                            mm(o, a_h, w_h[:, q], c == 0 and kk == 0 and t == 0, False)
                            mm(o, a_l, w_h[:, q], False, False)
                            ins = mm(o, a_h, w_l[:, q], False, last_unit and kk == 3)
                ins.then_inc(unit_used[slot], 1)

            def step(lay, kind, i):
                if kind == "norm_sum":
                    take(lay, 0)
                    pe.wait_ge(ones_ready, 1)
                    pe.wait_ge(sq_done, lay + 1)
                    for k in range(KT):
                        ins = mm(S[0][:, 0:T], ones, sqT[:, k, :], k == 0, k == KT - 1)
                    ins.then_inc(sum_done, 1)
                elif kind == "ffn_sum":
                    if i == 0:
                        take(lay, 0)
                    pe.wait_ge(f_sq, 2 * lay + i + 1)
                    for k in range(4 * i, 4 * i + 4):
                        ins = mm(S[0][:, 0:T], ones, sqT[:, k, :], k == 0, k == KT - 1)
                    if i == 1:
                        ins.then_inc(f_sum, 1)
                elif kind == "mem_turn":
                    mem_turn(lay, i)
                elif kind == "xa_scores":
                    if i == 0:
                        wait_evacuated(pe, lay, "xq", 1)
                        wait_evacuated(pe, lay, "mk", 1)
                    take(lay, i % 2)
                    for t in range(NT):
                        for k in range(2):
                            ins = mm(S[i % 2][:, T * t:T * (t + 1)], xqT[:, 2 * i + k, P * t:P * (t + 1)],
                                     mkT[:, 2 * i + k, :], k == 0, k == 1)
                    ins.then_inc(xa_sc, 1)
                elif kind == "xa_turn":
                    take(lay, 2)
                    pe.wait_ge(xa_p, XH * lay + i + 1)
                    for k in range(2):
                        for t in range(NT):
                            ins = nc.tensor.transpose(S[2][:, T * k + P * t:T * k + P * (t + 1)],
                                                      sc[i % 2][:, T * t + P * k:T * t + P * (k + 1)], ident[:, :])
                    ins.then_inc(xa_turned, 1)
                elif kind == "xa_values":
                    take(lay, 3)
                    pe.wait_ge(xa_copied, XH * lay + i + 1)
                    for e in range(2):
                        for k in range(2):
                            ins = mm(S[3][:, T * e:T * (e + 1)],
                                     mvN[:, k, T * i + P * e:T * i + P * (e + 1)], attT[:, k, :], k == 0, k == 1)
                    ins.then_inc(xa_pv, 1)
                elif kind == "da_scores":
                    half, j = i // HALF, i % HALF
                    if j == 0:
                        wait_evacuated(pe, lay, "k", half)
                        wait_evacuated(pe, lay, "v", half)
                    for m in range(2):
                        take(lay, m)
                        r = slice(DH * m, DH * (m + 1))
                        for t in range(NT):
                            ins = mm(S[m][:, T * t:T * (t + 1)], qT[half][r, j, P * t:P * (t + 1)],
                                     kT[half][r, j, :], True, True)
                    ins.then_inc(da_sc, 1)
                elif kind == "da_turn":
                    take(lay, 2)
                    pe.wait_ge(da_att, HEADS * lay + i + 1)
                    for k in range(2):
                        for t in range(NT):
                            ins = nc.tensor.transpose(S[2][:, T * k + P * t:T * k + P * (t + 1)],
                                                      sc[i % 2][:, T * t + P * k:T * t + P * (k + 1)], ident[:, :])
                    ins.then_inc(da_turned, 1)
                elif kind == "da_values":
                    half, j = i // HALF, i % HALF
                    take(lay, 2)
                    pe.wait_ge(da_copied, HEADS * lay + i + 1)
                    for t in range(NT):
                        for k in range(2):
                            ins = mm(S[2][:, P * t:P * (t + 1)], attT[:, k, P * t:P * (t + 1)],
                                     vN[half][:, k, P * j:P * (j + 1)], k == 0, k == 1)
                    ins.then_inc(da_pv, 1)
                elif kind == "da_out":
                    take(lay, 3)
                    pe.wait_ge(da_n, 2 * lay + i // 2 + 1)
                    for j in range(2):
                        for t in range(NT):
                            ins = nc.tensor.transpose(S[3][:, T * j + P * t:T * j + P * (t + 1)],
                                                      yN[:, NT * (2 * (i % 2) + j) + t, :], ident[:, :])
                    ins.then_inc(da_yt, 1)
                elif kind == "xs_turn":
                    take(lay, 3)
                    pe.wait_ge(silu_done, 6 * lay + i // 2 + 1)
                    t = i % 2
                    for j in range(4):
                        ins = nc.tensor.transpose(S[3][:, P * j:P * (j + 1)], cacc[i // 2 % 2][:, j, P * t:P * (t + 1)],
                                                  ident[:, :])
                    ins.then_inc(xs_turned, 1)
                elif kind == "dt_sums":
                    take(lay, 0)
                    pe.wait_ge(a_ready, lay + 1)
                    c3 = S[0][:, 0:P].rearrange("p (c j) -> p c j", c=NT)
                    aHv = aH_t[:, :].rearrange("p (c j) -> p c j", c=NT)
                    aLv = aL_t[:, :].rearrange("p (c j) -> p c j", c=NT)
                    for tri, q in ((upR, slice(0, SH)), (loR, slice(SH, 2 * SH))):
                        mm(c3[:, :, q], tri[:, :], aHv[:, :, q], True, False)
                        mm(c3[:, :, q], tri[:, :], aLv[:, :, q], False, True)
                    mm(S[0][:, P:2 * P], onesR[:, :], aH_t[:, :], True, False)
                    mm(S[0][:, P:2 * P], onesR[:, :], aL_t[:, :], False, True).then_inc(cs_done, 1)
                elif kind == "cb":
                    take(lay, 0)
                    if i == 0:
                        pe.wait_ge(silu_done, 6 * lay + 6)
                    for c in range(NT):
                        ins = mm(S[0][:, T * c:T * (c + 1)], BT[:, i, P * c:P * (c + 1)], CT[:, i, :], True, True)
                    ins.then_inc(cb_done, 1)
                elif kind == "off":
                    take(lay, 3)
                    c = i % 2
                    pe.wait_ge(xw_done, 8 * lay + i + 1)
                    pe.wait_ge(cb_ready, SG * lay + i // 2 + 1)
                    mm(S[3][:, :], cboff[:, 1 - c, :], xw, True, True).then_inc(off_done, 1)
                elif kind == "decay_sums":
                    strict = (afterR, beforeR)[i % 2][:, :]
                    take(lay, i % 2)
                    pe.wait_ge(spread_done, 32 * lay + i + 1)
                    mm(S[i % 2][:, :], strict, spH[i % 4], True, False)
                    mm(S[i % 2][:, :], strict, spL[i % 4], False, True).then_inc(bc_done, 1)
                elif kind == "diag":
                    job, hf = i // 2, i % 2
                    g, c = job // 2, job % 2
                    if hf == 0:
                        take(lay, 2)
                    if i == 0:
                        pe.wait_ge(xs_ready, 8 * lay + 8)
                    pe.wait_ge(pair_done, 16 * lay + i + 1)
                    for j in range(4):
                        h = 4 * hf + j
                        ins = mm(S[2][:, DH * h:DH * (h + 1)], M[2 * i % 4][:, P * j:P * (j + 1)],
                                 xsN[:, c, DH * (HPG * g + h):DH * (HPG * g + h + 1)], h == 0, True)
                    ins.then_inc(diag_done, 1)
                elif kind == "ssm_out":
                    g, c = i // 2, i % 2
                    take(lay, 3)
                    pe.wait_ge(n_done, 2 * lay + i // 4 + 1)
                    for j in range(4):
                        ins = nc.tensor.transpose(S[3][:, P * j:P * (j + 1)],
                                                  zN[:, c, P * (4 * g + j):P * (4 * g + j + 1)], ident[:, :])
                    ins.then_inc(yt_done, 1)

            def ffn_units(lay, g):
                u0 = FIRST_UNIT[g]
                with pe.Fori(0, FFN_LOOP) as i:
                    for c in range(8):
                        unit(lay, u0 + c, g + c // 4, c % 4, 2 * i, i)

            with pe.Fori(0, DEPTH) as lay:
                side[:] = setup_side
                each_step(lambda u, g, c: unit(lay, u, g, c), lambda g: None, lambda *s: step(lay, *s),
                          lambda g: ffn_units(lay, g))
                counted = [n - m for n, m in zip(side, setup_side)]
            side[:] = setup_side
            for b in range(4):
                if b % 2 == 0:
                    pe.wait_ge(fin_gain[b // 2], 1)
                take(DEPTH, b)
                turn(S[b], lambda t, k: htmp[:, 2 * b + k, P * t:P * (t + 1)], True).then_inc(fin_turned, 1)
            pe.wait_ge(fin_sq, 2)
            for t in range(NT):
                for k in range(KT):
                    ins = mm(PS[0][:, t:t + 1], sqT[:, k, P * t:P * (t + 1)], ones[:, 0:1], t == 0 and k == 0,
                             k == KT - 1)
            ins.then_inc(fin_sum, 1)
            build.counted = counted

        @block.scalar
        def _(act):
            for s in range(RING):
                act.sem_inc(unit_used[s], 1)
            for i, v in enumerate((lq1, lk1, lq2, lk2)):
                act.dma_start(scr[:, 2048 + P * i:2048 + P * (i + 1)],
                              v.rearrange("l d -> (l d)").partition_broadcast(P)).then_inc(row_in, 16)
            rows3 = v3(rows[:, :], DEPTH)
            for at, n, v in ((0, 64, dt_bias.rearrange("l a b -> l (a b)")),
                             (64, 64, A_log.rearrange("l a b -> l (a b)")), (128, SH, D_skip)):
                act.dma_start(rows3[:, :, at:at + n], v.partition_broadcast(P)).then_inc(row_in, 16)
            act.dma_start(xload, x.rearrange("b (t p) d -> p (b t) d", p=P)).then_inc(x_in, 16)

            def split_h(lay, u, extra=0):
                slot = u % RING
                n = use(lay, u) + extra
                act.wait_ge(raw_in[slot], 32 * (n + 1))
                act.wait_ge(unit_used[slot], n + 1)
                if GROUPS[UNIT_GROUP[u % UNITS]][0] == "dt":
                    q = slice(0, 256)
                else:
                    q = slice(0, UT * UC)
                nc.scalar.copy(wH[:, slot].rearrange("p k c -> p (k c)")[:, q],
                               raw[:, slot].rearrange("p k c -> p (k c)")[:, q]).then_inc(h_done[slot], 1)

            def evac(lay, g, extra=0):
                kind, b = GROUPS[g][:2]
                pair = g % 2
                src = PS[pair]
                if kind in ("mk", "xq", "q", "k", "mv", "v"):
                    wait_full(act, lay, g)
                    if layout_of(kind) == "T":
                        dst = {"mk": mkT, "xq": xqT}[kind][:, 4 * b:4 * b + 4, :] if kind in ("mk", "xq") else (
                            qT if kind == "q" else kT)[b]
                        nc.scalar.copy(dst, v3(src[:, :], 4)).then_inc(psum_free[pair], 1)
                    else:
                        dst = mvN[:, :, UC * b:UC * (b + 1)] if kind == "mv" else vN[b]
                        nc.scalar.copy(dst, v3(src[:, :], NT)).then_inc(psum_free[pair], 1)
                elif kind == "xbc":
                    wait_full(act, lay, g)
                    if b == 0:
                        act.wait_ge(da_copied, HEADS * lay + 1)
                    else:
                        act.wait_ge(conv_done, 6 * lay + b)
                    nc.scalar.copy(cin[:, :, 2:2 + T], v3(src[:, :], 4)).then_inc(psum_free[pair], 1)
                elif kind == "z":
                    wait_full(act, lay, g)
                    nc.scalar.activation(zN[:, :, UC * b:UC * (b + 1)], v3(src[:, :], NT),
                                         ACT.Silu).then_inc(psum_free[pair], 1)
                elif kind.startswith("gate"):
                    wait_full(act, lay, g)
                    before = sum(x[0].startswith("br") for x in GROUPS[:g])
                    if before:
                        act.wait_ge(sg_used, 6 * lay + before)
                    nc.scalar.activation(sg, src[:, :], ACT.Tanh, scale=0.5).then_inc(psum_free[pair], 1)

            def layout_of(kind):
                return "N" if kind in ("mv", "v") else "T"

            def hidden(lay, g, tile, extra=0):
                n = N_FFN * lay + (g - GI["ffn", 0]) + 2 * extra
                act.wait_ge(gate_scaled, n + 1)
                nc.scalar.activation(sg[:, 0:512], sg[:, 0:512], ACT.Silu).then_inc(gate_done, 1)
                act.wait_ge(up_done, n + 1)
                nc.scalar.copy(actH_t[:, tile], hid).then_inc(hid_h, 1)

            def mem_stats(n):
                if n is None:
                    act.wait_ge(ident_ready, 1)
                for t in range(NT):
                    act.wait_ge(mem_in[t], 16 if n is None else 16 * (n + 2))
                    nc.scalar.activation(mtmp[:, D * t:D * (t + 1)], memN[:, t, :], ACT.Square,
                                         accum_out=ms[:, t:t + 1])
                if n is None:
                    act.wait_ge(row_in, 16 * ROW_LOADS)
                    nc.scalar.activation(rows3[:, :, 64:128], rows3[:, :, 64:128], ACT.Exp)
                    act.wait_ge(lam_sum, 1)
                    nc.scalar.activation(lam4, lam4, ACT.Exp)
                    act.drain().then_inc(lam_exp, 1)
                else:
                    act.drain()
                nc.scalar.activation(mr, ms, ACT.Sqrt, bias=eps, scale=1.0 / D).then_inc(mem_std, 1)

            def mem_high(n, b):
                act.wait_ge(mem_g, b + 1 if n is None else 4 * n + 4 + b + 1)
                nc.scalar.copy(actH[:, MEM_A + 2 * b:MEM_A + 2 * b + 2, :], v3(mtmp[:, 512 * b:512 * (b + 1)], 2)
                               ).then_inc(mem_h, 1)

            def step(lay, kind, i):
                if kind == "norm_square":
                    act.wait_ge(x_half, 4 * lay + 2)
                    nc.scalar.activation(sqT, xT, ACT.Square).then_inc(sq_done, 1)
                elif kind == "norm_root":
                    act.wait_ge(sum_done, lay + 1)
                    nc.scalar.activation(std, S[0][:, 0:T], ACT.Sqrt, bias=eps, scale=1.0 / D
                                         ).then_inc(side_free[0], 1)
                    act.drain().then_inc(std_done, 1)
                elif kind == "norm_split":
                    act.wait_ge(hn_done, lay + 1)
                    nc.scalar.copy(hH, htmp).then_inc(hh_done, 1)
                elif kind == "ffn_input":
                    q = slice(4 * i, 4 * i + 4)
                    act.wait_ge(f_gain, 2 * lay + i + 1)
                    nc.scalar.copy(hH[:, q, :], htmp[:, q, :]).then_inc(f_high, 1)
                    nc.scalar.activation(sqT[:, q, :], xT[:, q, :], ACT.Square).then_inc(f_sq, 1)
                elif kind == "ffn_sum" and i == 1:
                    act.wait_ge(f_sum, lay + 1)
                    nc.scalar.activation(std, S[0][:, 0:T], ACT.Sqrt, bias=eps, scale=1.0 / D
                                         ).then_inc(side_free[0], 1)
                    act.drain().then_inc(f_std, 1)
                elif kind == "mem_scale":
                    mem_stats(lay)
                elif kind == "mem_split":
                    mem_high(lay, i)
                elif kind == "xa_scores":
                    b = i % 2
                    act.wait_ge(xa_max, XH * lay + i + 1)
                    for t in range(NT):
                        ins = nc.scalar.activation(sc[b][:, T * t:T * (t + 1)], S[b][:, T * t:T * (t + 1)], ACT.Exp,
                                                   bias=nmx[b][:, t:t + 1], scale=1.0 / 16.0,
                                                   accum_out=sm[b][:, t:t + 1])
                    ins.then_inc(side_free[b], 1)
                    act.drain().then_inc(xa_exp, 1)
                elif kind == "xa_turn":
                    act.wait_ge(xa_turned, XH * lay + i + 1)
                    nc.scalar.copy(attT, v3(S[2][:, :], 2)).then_inc(side_free[2], 1)
                    act.drain().then_inc(xa_copied, 1)
                elif kind == "xa_values":
                    act.wait_ge(xa_pv, XH * lay + i + 1)
                    nc.scalar.copy(actH[:, XA_A + 2 * i:XA_A + 2 * i + 2, :], v3(S[3][:, :], 2)).then_inc(xa_h, 1)
                elif kind == "da_scores":
                    b = i % 2
                    act.wait_ge(da_max, HEADS * lay + i + 1)
                    for q in range(4):
                        v = sc[b][:, T * q:T * (q + 1)]
                        nc.scalar.activation(v, v, ACT.Exp, bias=nmx[b][:, q:q + 1], scale=0.125,
                                             accum_out=sm[b][:, q:q + 1])
                    act.drain().then_inc(da_exp, 1)
                elif kind == "da_turn":
                    act.wait_ge(da_turned, HEADS * lay + i + 1)
                    nc.scalar.copy(attT, v3(S[2][:, :], 2)).then_inc(side_free[2], 1)
                    act.drain().then_inc(da_copied, 1)
                elif kind == "da_values":
                    j = i % HALF
                    act.wait_ge(da_pv, HEADS * lay + i + 1)
                    if j == 0 and i > 0:
                        act.wait_ge(da_yt, 4 * lay + 2)
                    for t in range(NT):
                        ins = nc.scalar.activation(yN[:, NT * j + t, :], S[2][:, P * t:P * (t + 1)], ACT.Copy,
                                                   scale=rs[i % 2][:, t:t + 1])
                    ins.then_inc(side_free[2], 1)
                    act.drain()
                    for t in range(NT):
                        nc.scalar.activation(junk[:, P * t:P * (t + 1)], yN[:, NT * j + t, :], ACT.Square,
                                             accum_out=ss[:, NT * j + t:NT * j + t + 1])
                    act.drain().then_inc(da_st, 1)
                elif kind == "da_norm":
                    nc.scalar.activation(sr, ss, ACT.Sqrt, bias=eps, scale=1.0 / P).then_inc(da_sd, 1)
                elif kind == "da_out":
                    act.wait_ge(da_yt, 4 * lay + i + 1)
                    t0 = DA_A + 2 * i
                    nc.scalar.activation(actH[:, t0:t0 + 2, :], v3(S[3][:, :], 2), ACT.Copy,
                                         scale=p_sub).then_inc(da_h, 1)
                elif kind == "conv_silu":
                    act.wait_ge(conv_done, 6 * lay + i + 1)
                    nc.scalar.activation(cacc[i % 2], cacc[i % 2], ACT.Silu)
                    act.drain().then_inc(silu_done, 1)
                elif kind == "xs_turn":
                    b, t = i // 2, i % 2
                    act.wait_ge(xs_turned, 8 * lay + i + 1)
                    nc.scalar.copy(xsN[:, t, UC * b:UC * (b + 1)], S[3][:, :]).then_inc(side_free[3], 1)
                    act.drain().then_inc(xs_ready, 1)
                elif kind == "dt":
                    act.wait_ge(dt_abs, lay + 1)
                    nc.scalar.activation(dt_e, dt_e, ACT.Exp, scale=-1.0).then_inc(dt_exp, 1)
                    act.wait_ge(dt_u1, lay + 1)
                    nc.scalar.activation(dt_l, dt_u, ACT.Ln).then_inc(dt_ln, 1)
                elif kind == "dt_sums":
                    act.wait_ge(cs_sub, lay + 1)
                    nc.scalar.activation(eo, cs, ACT.Exp)
                    nc.scalar.activation(wgt, wgt, ACT.Exp).then_inc(cs_exp, 1)
                elif kind == "decay":
                    act.wait_ge(bc_done, 32 * lay + i + 1)
                    if i >= 4:
                        act.wait_ge(diag_done, 16 * lay + i // 2 - 1)
                    nc.scalar.activation(M[i % 4], S[i % 2][:, :], ACT.Exp).then_inc(side_free[i % 2], 1)
                    act.drain().then_inc(exp_done, 1)
                elif kind == "assemble":
                    g, c = i // 2, i % 2
                    act.wait_ge(y_done, 8 * lay + i + 1)
                    nc.scalar.activation(junk[:, :], zN[:, c, UC * g:UC * (g + 1)], ACT.Square,
                                         accum_out=s4[:, i % 4:i % 4 + 1])
                    act.drain().then_inc(st_done, 1)
                elif kind == "ssm_norm":
                    nc.scalar.activation(r4, s4, ACT.Sqrt, bias=eps, scale=1.0 / 512).then_inc(sd_done, 1)
                elif kind == "ssm_out":
                    g, c = i // 2, i % 2
                    act.wait_ge(g_done, 8 * lay + i + 1)
                    t0 = SSM_A + 4 * g
                    nc.scalar.copy(actH[:, t0:t0 + 4, P * c:P * (c + 1)], v3(gtmp, 4)).then_inc(gh_done, 1)
                elif kind == "merged":
                    act.wait_ge(mrg_sum, 2 * lay + i + 1)
                    nc.scalar.activation(actH[:, MRG_A + 4 * i:MRG_A + 4 * i + 4, :], mrg[:, 4 * i:4 * i + 4, :],
                                         ACT.Copy, scale=0.5).then_inc(mrg_h, 1)

            mem_stats(None)
            for b in range(4):
                if b != 1:
                    split_h(0, (b + 1) // 2)
                mem_high(None, b)

            with act.Fori(0, DEPTH) as lay:
                def unit(u, g, c):
                    split_h(lay, u + LOOKAHEAD)

                def group_end(g):
                    kind, b = GROUPS[g][:2]
                    if kind == "ffn":
                        hidden(lay, g, slice(2 * b * T, (2 * b + 2) * T))
                    else:
                        evac(lay, g)
                    if kind == "dt":
                        step(lay, "dt", b)
                    if kind == "br1":
                        step(lay, "merged", b)

                def ffn_loop(g):
                    u0 = FIRST_UNIT[g]
                    with act.Fori(0, FFN_LOOP) as i:
                        for c in range(8):
                            split_h(lay, u0 + c + LOOKAHEAD, 2 * i)
                            if c % 4 == 3:
                                hidden(lay, g + c // 4, hidden_tiles(i, c), i)

                each_step(unit, group_end, lambda *s: step(lay, *s), ffn_loop)
            for h in range(2):
                act.wait_ge(x_half, 4 * DEPTH + 1 + h)
                nc.scalar.activation(sqT[:, 4 * h:4 * h + 4, :], xT[:, 4 * h:4 * h + 4, :], ACT.Square
                                     ).then_inc(fin_sq, 1)
            act.wait_ge(fin_sum, 1)
            nc.scalar.activation(fstd, PS[0][:, 0:NT], ACT.Sqrt, bias=eps, scale=1.0 / D).then_inc(fin_std, 1)
            act.wait_ge(fin_rstd, 1)
            for b in (0, 2):
                act.wait_ge(fin_turned, b + 1)
                for t in range(NT):
                    ins = nc.scalar.activation(xload[:, t, T * b:T * (b + 1)], S[b][:, T * t:T * (t + 1)], ACT.Copy,
                                               scale=frs[:, t:t + 1])
                ins.then_inc(fin_copied[0], 1)

        @block.gpsimd
        def _(pool):
            nc.gpsimd.memset(ident[:, :], 0.0)
            nc.gpsimd.memset(eps, EPS)
            pool.drain()
            nc.gpsimd.affine_select(out=ident[:, :], in_=ident[:, :], compare_op=ALU.not_equal, fill=1.0, base=0,
                                    pattern=[[-1, P]], channel_multiplier=1)
            pool.drain().then_inc(ident_ready, 1)
            tmp = [scr[:, 2560 + P * i:2560 + P * (i + 1)] for i in range(3)]
            for i in range(3):
                nc.gpsimd.memset(tmp[i], 1.0)
            pool.drain()
            nc.gpsimd.affine_select(out=tmp[0], in_=tmp[0], compare_op=ALU.is_ge, fill=0.0, base=0,
                                    pattern=[[1, P]], channel_multiplier=-1)
            nc.gpsimd.affine_select(out=tmp[1], in_=tmp[1], compare_op=ALU.is_ge, fill=0.0, base=0,
                                    pattern=[[-1, P]], channel_multiplier=1)
            nc.gpsimd.iota(scr[:, 3072:3584], pattern=[[P, NT], [-1, T]], base=0, channel_multiplier=1,
                           allow_small_or_imprecise_dtypes=True)
            pool.drain().then_inc(tri_ready, 1)

            def split_l(lay, u, extra=0):
                slot = u % RING
                if not pool_splits(u):
                    return
                n = use(lay, u) + extra
                q = slice(0, 256 if GROUPS[UNIT_GROUP[u % UNITS]][0] == "dt" else UT * UC)
                pool.wait_ge(h_done[slot], n + 1)
                nc.gpsimd.tensor_tensor(wL[:, slot].rearrange("p k c -> p (k c)")[:, q],
                                        raw[:, slot].rearrange("p k c -> p (k c)")[:, q],
                                        wH[:, slot].rearrange("p k c -> p (k c)")[:, q].bitcast(F32),
                                        ALU.subtract).then_inc(l_done[slot], 1)

            def step(lay, kind, i):
                if kind == "scale":
                    g, c = i // 2, i % 2
                    if i == 0:
                        pool.wait_ge(xs_ready, 8 * lay + 8)
                        pool.wait_ge(dt_ready, lay + 1)
                        pool.wait_ge(conv_done, 6 * lay + 6)
                        pool.wait_ge(da_yt, 4 * lay + 4)
                    else:
                        pool.wait_ge(off_done, 8 * lay + i)
                    q = 64 * (1 - c) + SH * (1 - c) + HPG * g
                    nc.gpsimd.tensor_tensor(v3(xw, HPG), v3(xsN[:, 1 - c, UC * g:UC * (g + 1)], HPG),
                                            wgt[:, q:q + HPG].unsqueeze(2).broadcast_to([P, HPG, DH]),
                                            ALU.mult).then_inc(xw_done, 1)
                elif kind == "decay" and i % 2 == 1:
                    pool.wait_ge(m_done, 32 * lay + i + 1)
                    m, other = M[(i - 1) % 4], M[i % 4]
                    nc.gpsimd.tensor_tensor(m, m, other, ALU.add).then_inc(pair_done, 1)
                elif kind == "off":
                    g, c = i // 2, i % 2
                    if i > 0:
                        pool.wait_ge(y_done, 8 * lay + i)
                    nc.gpsimd.tensor_tensor(v3(xsd, HPG), v3(xsN[:, c, UC * g:UC * (g + 1)], HPG),
                                            r_D[:, HPG * g:HPG * (g + 1)].unsqueeze(2).broadcast_to([P, HPG, DH]),
                                            ALU.mult).then_inc(xsd_done, 1)

            for u in range(LOOKAHEAD):
                split_l(0, u)

            with pool.Fori(0, DEPTH) as lay:
                def ffn_loop(g):
                    u0 = FIRST_UNIT[g]
                    with pool.Fori(0, FFN_LOOP) as i:
                        for c in range(8):
                            split_l(lay, u0 + c + LOOKAHEAD, 2 * i)

                def group_end(g):
                    kind, b = GROUPS[g][:2]
                    if kind == "br2":
                        pool.wait_ge(br_done, 2 * lay + b + 1)
                        q = mrg[:, 4 * b:4 * b + 4, :]
                        nc.gpsimd.tensor_tensor(q, q, v3(sg, 4), ALU.add)
                        pool.drain().then_inc(sg_used, 1)

                each_step(lambda u, g, c: split_l(lay, u + LOOKAHEAD), group_end, lambda *s: step(lay, *s), ffn_loop)
            pool.wait_ge(x_half, 4 * DEPTH + 1)
            nc.gpsimd.tensor_tensor(htmp[:, 0:4, :], xT[:, 0:4, :],
                                    par[:, 368:372].unsqueeze(2).broadcast_to([P, 4, T]), ALU.mult
                                    ).then_inc(fin_gain[0], 1)

        @block.vector
        def _(dve):
            v = nc.vector
            for s in range(RING):
                dve.sem_inc(l_done[s], 1)
            for i in range(4):
                dve.sem_inc(side_free[i], 1)
            dve.sem_inc(psum_free[0], 1)

            def split_l(lay, u, extra=0):
                slot = u % RING
                if pool_splits(u):
                    return
                n = use(lay, u) + extra
                q = slice(0, 256 if GROUPS[UNIT_GROUP[u % UNITS]][0] == "dt" else UT * UC)
                dve.wait_ge(h_done[slot], n + 1)
                v.tensor_tensor(wL[:, slot].rearrange("p k c -> p (k c)")[:, q],
                                raw[:, slot].rearrange("p k c -> p (k c)")[:, q],
                                wH[:, slot].rearrange("p k c -> p (k c)")[:, q].bitcast(F32),
                                ALU.subtract).then_inc(l_done[slot], 1)

            def low(out_l, full, high, scale=None):
                if scale is None:
                    return v.tensor_tensor(out_l, full, high.bitcast(F32), ALU.subtract)
                return v.scalar_tensor_tensor(out_l, full, scale, high.bitcast(F32), ALU.mult, ALU.subtract)

            def gains(g, n, width):
                return g.unsqueeze(2).broadcast_to([P, n, width])

            def params(lay):
                v.tensor_copy(p_cw, par[:, bass.ds(lay * 128, 120)])
                v.tensor_copy(p_mem, par[:, bass.ds(248 - lay * 128, 8)])
                v.tensor_copy(p_cb, par[:, bass.ds(lay * 24 + 256, 24)])
                v.tensor_copy(p_mix, par[:, bass.ds(lay * 8 + 304, 8)])
                v.tensor_copy(p_ffn, par[:, bass.ds(lay * 8 + 320, 8)])
                v.tensor_copy(p_ssm, par[:, bass.ds(lay * 16 + 336, 16)])
                v.tensor_copy(p_sub, sub2[:, bass.ds(lay, 1)])
                v.tensor_copy(p_nlam, nlam2[:, bass.ds(lay, 1)])
                v.tensor_copy(lrow[:, :], rows[:, bass.ds(lay * 160, 160)])
                dve.drain()

            def mem_scale(n):
                dve.wait_ge(mem_std, 1 if n is None else n + 2)
                v.reciprocal(mr, mr)
                dve.drain()
                for t in range(NT):
                    v.tensor_scalar(memN[:, t, :], memN[:, t, :], mr[:, t:t + 1], None, ALU.mult)
                dve.drain().then_inc(mem_scaled, 1)

            def mem_split(n, b, g):
                at = b + 1 if n is None else 4 * n + 4 + b + 1
                part = v3(mtmp[:, 512 * b:512 * (b + 1)], 2)
                dve.wait_ge(mem_turned, at)
                v.tensor_tensor(part, v3(S[b][:, :], 2), gains(g[:, 2 * b:2 * b + 2], 2, T), ALU.mult
                                ).then_inc(side_free[b], 1)
                dve.drain().then_inc(mem_g, 1)
                dve.wait_ge(mem_h, at)
                q = slice(MEM_A + 2 * b, MEM_A + 2 * b + 2)
                low(actL[:, q, :], part, actH[:, q, :]).then_inc(mem_ready, 1)

            def evac(lay, g, extra=0):
                kind, b = GROUPS[g][:2]
                pair = g % 2
                src = PS[pair]
                tiles = slice(4 * b, 4 * b + 4) if kind != "ffn" else None
                if kind == "dt":
                    wait_full(dve, lay, g)
                    bias = r_dtb.unsqueeze(1).broadcast_to([P, NT, 64])
                    v.tensor_tensor(v3(dt_x, NT), v3(src[:, 0:P], NT), bias, ALU.add)
                    dve.drain().then_inc(psum_free[pair], 1)
                    v.scalar_tensor_tensor(dt_e, dt_x, -1.0, dt_x, ALU.mult, ALU.max)
                    dve.drain().then_inc(dt_abs, 1)
                    dve.wait_ge(dt_exp, lay + 1)
                    v.tensor_scalar(dt_u, dt_e, 1.0, None, ALU.add)
                    dve.drain().then_inc(dt_u1, 1)
                    v.scalar_tensor_tensor(dt_c, dt_u, -1.0, dt_e, ALU.add, ALU.subtract)
                    v.reciprocal(aN, dt_u)
                    dve.drain()
                    v.tensor_tensor(dt_c, dt_c, aN, ALU.mult)
                    dve.drain()
                    dve.wait_ge(dt_ln, lay + 1)
                    v.tensor_tensor(dt_c, dt_l, dt_c, ALU.subtract)
                    dve.drain()
                    v.scalar_tensor_tensor(dtv, dt_x, 0.0, dt_c, ALU.max, ALU.add)
                    dve.drain()
                    v.scalar_tensor_tensor(v3(aN, NT), v3(dtv, NT), -1.0,
                                           r_A.unsqueeze(1).broadcast_to([P, NT, 64]), ALU.mult, ALU.mult)
                    dve.drain()
                    v.tensor_copy(aH_t[:, :], aN)
                    dve.drain()
                    low(aL_t[:, :], aN, aH_t[:, :]).then_inc(a_ready, 1)
                elif kind.startswith("br"):
                    gate = g - 1
                    dve.wait_ge(psum_free[gate % 2], used_after(lay, gate))
                    wait_full(dve, lay, g)
                    if kind == "br0":
                        v.scalar_tensor_tensor(mrg[:, tiles, :], v3(sg, 4), 1.0, v3(src[:, :], 4), ALU.add,
                                               ALU.mult)
                        dve.drain().then_inc(psum_free[pair], 1)
                        dve.drain().then_inc(sg_used, 1)
                    else:
                        v.scalar_tensor_tensor(v3(sg, 4), v3(sg, 4), 1.0, v3(src[:, :], 4), ALU.add, ALU.mult
                                               ).then_inc(psum_free[pair], 1)
                        if kind == "br2":
                            dve.drain().then_inc(br_done, 1)
                        else:
                            dve.drain()
                            v.tensor_tensor(mrg[:, tiles, :], mrg[:, tiles, :], v3(sg, 4), ALU.add)
                            dve.drain().then_inc(sg_used, 1)
                            dve.drain().then_inc(mrg_sum, 1)
                    if kind == "br1":
                        dve.wait_ge(mrg_h, 2 * lay + b + 1)
                        low(actL[:, MRG_A + 4 * b:MRG_A + 4 * b + 4, :], mrg[:, tiles, :],
                            actH[:, MRG_A + 4 * b:MRG_A + 4 * b + 4, :], 0.5).then_inc(mrg_ready, 1)
                elif kind in ("out", "down"):
                    wait_full(dve, lay, g)
                    v.tensor_tensor(xT[:, tiles, :], xT[:, tiles, :], v3(src[:, :], 4), ALU.add
                                    ).then_inc(psum_free[pair], 1)
                    dve.drain().then_inc(x_half, 1)

            def hidden(lay, g, tile, extra=0):
                pair = g % 2
                n = N_FFN * lay + (g - GI["ffn", 0]) + 2 * extra
                r2 = rstd.unsqueeze(1).broadcast_to([P, 2, T])
                wait_full(dve, lay, g, 2 * extra)
                v.tensor_tensor(v3(sg[:, 0:512], 2), v3(PS[pair][:, 0:512], 2), r2, ALU.mult)
                dve.drain().then_inc(gate_scaled, 1)
                v.tensor_tensor(v3(hid, 2), v3(PS[pair][:, 512:1024], 2), r2, ALU.mult).then_inc(psum_free[pair], 1)
                dve.drain()
                dve.wait_ge(gate_done, n + 1)
                v.tensor_tensor(hid, hid, sg[:, 0:512], ALU.mult)
                dve.drain().then_inc(up_done, 1)
                dve.wait_ge(hid_h, n + 1)
                low(actL_t[:, tile], hid, actH_t[:, tile]).then_inc(hid_ready, 1)
                dve.drain()

            def step(lay, kind, i):
                if kind == "norm_square":
                    v.tensor_tensor(htmp, xT, gains(p_mix, KT, T), ALU.mult)
                elif kind == "norm_root":
                    dve.wait_ge(std_done, lay + 1)
                    v.reciprocal(rstd, std)
                    dve.drain()
                    v.tensor_tensor(htmp, htmp, rstd.unsqueeze(1).broadcast_to([P, KT, T]), ALU.mult)
                    dve.drain().then_inc(hn_done, 1)
                elif kind == "norm_split":
                    dve.wait_ge(hh_done, lay + 1)
                    low(hL, htmp, hH).then_inc(h_ready, 1)
                elif kind == "ffn_input":
                    q = slice(4 * i, 4 * i + 4)
                    v.tensor_tensor(htmp[:, q, :], xT[:, q, :], gains(p_ffn[:, q], 4, T), ALU.mult)
                    dve.drain().then_inc(f_gain, 1)
                    dve.wait_ge(f_high, 2 * lay + i + 1)
                    low(hL[:, q, :], htmp[:, q, :], hH[:, q, :]).then_inc(f_ready, 1)
                elif kind == "ffn_sum" and i == 1:
                    dve.wait_ge(f_std, lay + 1)
                    v.reciprocal(rstd, std)
                    dve.drain()
                elif kind == "mem_scale":
                    mem_scale(lay)
                elif kind == "mem_split":
                    mem_split(lay, i, p_mem)
                elif kind == "xa_scores":
                    b = i % 2
                    dve.wait_ge(xa_sc, XH * lay + i + 1)
                    v.tensor_reduce(mx[b][:, 0:2], v3(S[b][:, :], 2), AX.X, ALU.max)
                    dve.drain()
                    v.tensor_scalar(nmx[b][:, 0:2], mx[b][:, 0:2], -1.0 / 16.0, None, ALU.mult).then_inc(xa_max, 1)
                    dve.wait_ge(xa_exp, XH * lay + i + 1)
                    v.reciprocal(rs[b][:, 0:2], sm[b][:, 0:2])
                    dve.drain()
                    for t in range(NT):
                        q = sc[b][:, T * t:T * (t + 1)]
                        v.tensor_scalar(q, q, rs[b][:, t:t + 1], None, ALU.mult)
                    dve.drain().then_inc(xa_p, 1)
                elif kind == "xa_values":
                    dve.wait_ge(xa_h, XH * lay + i + 1)
                    q = slice(XA_A + 2 * i, XA_A + 2 * i + 2)
                    low(actL[:, q, :], v3(S[3][:, :], 2), actH[:, q, :]).then_inc(side_free[3], 1)
                    dve.drain().then_inc(xa_y, 1)
                elif kind == "da_scores":
                    b = i % 2
                    dve.wait_ge(da_sc, HEADS * lay + i + 1)
                    if i >= 2:
                        dve.wait_ge(da_turned, HEADS * lay + i - 1)
                    else:
                        dve.wait_ge(xa_turned, XH * lay + XH)
                    for m in range(2):
                        v.scalar_tensor_tensor(sc[b][:, 512 * m:512 * (m + 1)], dist[:, :], -8.0 * slope(i),
                                               S[m][:, :], ALU.mult, ALU.add).then_inc(side_free[m], 1)
                    dve.drain()
                    v.tensor_reduce(mx[b], v3(sc[b], 4), AX.X, ALU.max)
                    dve.drain()
                    v.tensor_scalar(nmx[b], mx[b], -0.125, None, ALU.mult).then_inc(da_max, 1)
                elif kind == "da_combine":
                    b = i % 2
                    dve.wait_ge(da_exp, HEADS * lay + i + 1)
                    v.reciprocal(rs[b], sm[b])
                    dve.drain()
                    v.scalar_tensor_tensor(nl[b], rs[b][:, 2:4], p_nlam, sm[b][:, 0:2], ALU.mult, ALU.mult)
                    dve.drain()
                    for t in range(NT):
                        v.scalar_tensor_tensor(sc[b][:, T * t:T * (t + 1)], sc[b][:, 512 + T * t:512 + T * (t + 1)],
                                               nl[b][:, t:t + 1], sc[b][:, T * t:T * (t + 1)], ALU.mult, ALU.add)
                    dve.drain().then_inc(da_att, 1)
                elif kind == "da_norm":
                    dve.wait_ge(da_sd, 2 * lay + i + 1)
                    v.reciprocal(sr, sr)
                    dve.drain()
                    v.tensor_tensor(yN, yN, gains(sr, HALF * NT, P), ALU.mult)
                    dve.drain().then_inc(da_n, 1)
                elif kind == "da_out":
                    dve.wait_ge(da_h, 4 * lay + i + 1)
                    q = slice(DA_A + 2 * i, DA_A + 2 * i + 2)
                    low(actL[:, q, :], v3(S[3][:, :], 2), actH[:, q, :], p_sub).then_inc(side_free[3], 1)
                    dve.drain().then_inc(da_y, 1)
                elif kind == "conv":
                    b, g = i // 2, GI["xbc", i // 2]
                    if i % 2 == 0:
                        dve.wait_ge(psum_free[g % 2], used_after(lay, g))
                        if b >= 2:
                            dve.wait_ge(xs_turned, 8 * lay + 2 * b - 2)
                    js = range(2 * (i % 2), 2 * (i % 2) + 2)
                    for j in js:
                        t = 4 * b + j
                        v.tensor_scalar(cacc[b % 2][:, j, :], cin[:, j, 0:T], p_cw[:, t:t + 1], p_cb[:, t:t + 1],
                                        ALU.mult, ALU.add)
                    for k in range(1, CONV):
                        dve.drain()
                        for j in js:
                            q = CONV_T * k + 4 * b + j
                            v.scalar_tensor_tensor(cacc[b % 2][:, j, :], cin[:, j, k:k + T], p_cw[:, q:q + 1],
                                                   cacc[b % 2][:, j, :], ALU.mult, ALU.add)
                    done = dve.drain()
                    if i % 2 == 1:
                        done.then_inc(conv_done, 1)
                elif kind == "dt_sums":
                    dve.wait_ge(cs_done, lay + 1)
                    v.tensor_copy(cs, S[0][:, 0:P])
                    dve.drain()
                    v.tensor_tensor(wgt, S[0][:, P:2 * P], cs, ALU.subtract).then_inc(side_free[0], 1)
                    dve.drain().then_inc(cs_sub, 1)
                    dve.wait_ge(cs_exp, lay + 1)
                    v.tensor_tensor(wgt, wgt, dtv, ALU.mult).then_inc(dt_ready, 1)
                elif kind == "spread":
                    q, d = quad_heads(i), i % 2
                    if i >= 4:
                        dve.wait_ge(bc_done, 32 * lay + i - 3)
                    for dst, a in ((spH, aH_t), (spL, aL_t)):
                        v.tensor_tensor(v3(dst[i % 4], 4),
                                        (upR, loR)[d][:, :].bitcast(F32).unsqueeze(1).broadcast_to([P, 4, P]),
                                        gains(a[:, q:q + 4].bitcast(F32), 4, P), ALU.mult)
                    dve.drain().then_inc(spread_done, 1)
                elif kind == "cb":
                    dve.wait_ge(cb_done, SG * lay + i + 1)
                    if i > 0:
                        dve.wait_ge(off_done, 8 * lay + 2 * i)
                    for c in range(NT):
                        for d, tri in enumerate((upR, loR)):
                            v.tensor_tensor(cbm[:, d, c, :], S[0][:, (T + P) * c:(T + P) * c + P],
                                            tri[:, :].bitcast(F32), ALU.mult)
                    v.tensor_copy(cboff, v3(S[0][:, P:P + T], 2)).then_inc(side_free[0], 1)
                    dve.drain().then_inc(cb_ready, 1)
                elif kind == "decay":
                    q, c, d = quad_heads(i), i // 4 % 2, i % 2
                    dve.wait_ge(exp_done, 32 * lay + i + 1)
                    for j in range(4):
                        m = M[i % 4][:, P * j:P * (j + 1)]
                        v.scalar_tensor_tensor(m, m, dtv[:, q + j:q + j + 1], cbm[:, d, c, :], ALU.mult, ALU.mult)
                    dve.drain().then_inc(m_done, 1)
                elif kind == "assemble":
                    g, c = i // 2, i % 2
                    d = 1 - c
                    dve.wait_ge(off_done, 8 * lay + i + 1)
                    q = 64 * c + SH * d + HPG * g
                    v.tensor_tensor(v3(ytmp, HPG), v3(S[3][:, :], HPG), gains(eo[:, q:q + HPG], HPG, DH), ALU.mult)
                    dve.drain().then_inc(side_free[3], 1)
                    dve.wait_ge(diag_done, 16 * lay + 2 * i + 2)
                    v.tensor_tensor(ytmp, ytmp, S[2][:, :], ALU.add)
                    dve.drain().then_inc(side_free[2], 1)
                    dve.wait_ge(xsd_done, 8 * lay + i + 1)
                    v.tensor_tensor(ytmp, ytmp, xsd, ALU.add)
                    dve.drain()
                    if i % 2 == 0:
                        wait_evacuated(dve, lay, "z", g)
                    zq = zN[:, c, UC * g:UC * (g + 1)]
                    v.tensor_tensor(zq, zq, ytmp, ALU.mult)
                    dve.drain().then_inc(y_done, 1)
                elif kind == "ssm_norm":
                    dve.wait_ge(sd_done, 2 * lay + i + 1)
                    v.reciprocal(r4, r4)
                    dve.drain()
                    for q in range(4):
                        g, c = 2 * i + q // 2, q % 2
                        zq = zN[:, c, UC * g:UC * (g + 1)]
                        v.tensor_scalar(zq, zq, r4[:, q:q + 1], None, ALU.mult)
                    dve.drain().then_inc(n_done, 1)
                elif kind == "ssm_out":
                    g, c = i // 2, i % 2
                    dve.wait_ge(yt_done, 8 * lay + i + 1)
                    v.tensor_tensor(v3(gtmp, 4), v3(S[3][:, :], 4), gains(p_ssm[:, 4 * g:4 * g + 4], 4, P),
                                    ALU.mult).then_inc(side_free[3], 1)
                    dve.drain().then_inc(g_done, 1)
                    dve.wait_ge(gh_done, 8 * lay + i + 1)
                    t0 = SSM_A + 4 * g
                    low(actL[:, t0:t0 + 4, P * c:P * (c + 1)], v3(gtmp, 4),
                        actH[:, t0:t0 + 4, P * c:P * (c + 1)])
                    dve.drain().then_inc(ssm_y, 1)

            dve.wait_ge(tri_ready, 1)
            for i, t in enumerate((upR, loR, onesR)):
                v.tensor_copy(t[:, :], scr[:, 2560 + P * i:2560 + P * (i + 1)])
            dve.drain().then_inc(ones_ready, 1)
            for i, t in enumerate((afterR, beforeR)):
                v.tensor_tensor(t[:, :], scr[:, 2816:2944], scr[:, 2560 + P * i:2560 + P * (i + 1)], ALU.subtract)
            v.tensor_scalar(scr[:, 3584:4096], scr[:, 3072:3584], -1.0, None, ALU.mult)
            dve.drain()
            v.tensor_tensor(dist[:, :], scr[:, 3072:3584], scr[:, 3584:4096], ALU.max)
            dve.wait_ge(row_in, 16 * ROW_LOADS)
            lam = scr[:, 2048:2560].rearrange("p (a q c) -> p a q c", a=2, q=2)
            v.tensor_tensor(v3(scr[:, 4096:4352], 2), lam[:, :, 0, :], lam[:, :, 1, :], ALU.mult)
            dve.drain()
            v.tensor_reduce(lam4, scr[:, 4096:4352].rearrange("p (a c) -> p a c", a=4), AX.X, ALU.add)
            dve.drain().then_inc(lam_sum, 1)
            mem_scale(None)
            dve.wait_ge(par_turned, 1)
            v.tensor_copy(par[:, 0:378], PS[1][:, 0:378])
            dve.drain().then_inc(par_copied, 1)
            for b in range(4):
                if b != 1:
                    split_l(0, (b + 1) // 2)
                mem_split(None, b, par[:, 120:128])
            for b in range(2):
                dve.wait_ge(x_turned, b + 1)
                ins = v.tensor_copy(xT[:, 2 * b:2 * b + 2, :], v3(PS[1][:, 512 * b:512 * (b + 1)], 2))
            ins.then_inc(psum_free[1], 1)
            for b in range(2, 4):
                dve.wait_ge(x_turned, b + 1)
                v.tensor_copy(xT[:, 2 * b:2 * b + 2, :], v3(S[b - 2][:, :], 2)).then_inc(side_free[b - 2], 1)
            dve.drain().then_inc(x_half, 2)
            dve.wait_ge(lam_exp, 1)
            v.tensor_tensor(nlam2, lam4[:, 2:4], lam4[:, 0:2], ALU.subtract)
            dve.drain()
            for lay in range(DEPTH):
                v.tensor_scalar(nlam2[:, lay:lay + 1], nlam2[:, lay:lay + 1], -lambda_init(lay), None, ALU.add)
                v.tensor_scalar(sub2[:, lay:lay + 1], par[:, 376 + lay:377 + lay], 1.0 - lambda_init(lay), None,
                                ALU.mult)
            dve.drain()

            with dve.Fori(0, DEPTH) as lay:
                params(lay)

                def unit(u, g, c):
                    if u == FIRST_UNIT[GI["q", 0]]:
                        v.memset(cin[:, :, 0:2], 0.0)
                        v.memset(cin[:, :, 2 + T:4 + T], 0.0)
                    split_l(lay, u + LOOKAHEAD)

                def group_end(g):
                    kind, b = GROUPS[g][:2]
                    if kind == "ffn":
                        hidden(lay, g, slice(2 * b * T, (2 * b + 2) * T))
                    else:
                        evac(lay, g)

                def ffn_loop(g):
                    u0 = FIRST_UNIT[g]
                    with dve.Fori(0, FFN_LOOP) as i:
                        for c in range(8):
                            split_l(lay, u0 + c + LOOKAHEAD, 2 * i)
                            if c % 4 == 3:
                                hidden(lay, g + c // 4, hidden_tiles(i, c), i)

                each_step(unit, group_end, lambda *s: step(lay, *s), ffn_loop)
            v.tensor_tensor(htmp[:, 4:8, :], xT[:, 4:8, :], gains(par[:, 372:376], 4, T), ALU.mult
                            ).then_inc(fin_gain[1], 1)
            dve.wait_ge(fin_std, 1)
            v.reciprocal(frs, fstd)
            dve.drain().then_inc(fin_rstd, 1)
            for b in (1, 3):
                dve.wait_ge(fin_turned, b + 1)
                for t in range(NT):
                    ins = v.tensor_scalar(xload[:, t, T * b:T * (b + 1)], S[b][:, T * t:T * (t + 1)], frs[:, t:t + 1],
                                          None, ALU.mult)
                ins.then_inc(fin_copied[1], 1)


_INS = ["x", "mem", "mix_norm_g", "w_in", "da_lambda_q1", "da_lambda_k1", "da_lambda_q2", "da_lambda_k2",
        "da_subln_g", "ssm_conv_w", "ssm_conv_b", "ssm_dt_bias", "ssm_A_log", "ssm_D", "ssm_norm_g", "mem_norm_g",
        "w_mem_kv", "w_branch", "w_out", "ffn_norm_g", "w_ffn_in", "w_ffn_out", "final_norm_g"]


def kernel(**inputs):
    import numpy as _np
    import concourse.bacc as _bacc
    from concourse import mybir as _mybir
    from concourse.bass_utils import run_bass_kernel_spmd as _run

    nc = _bacc.Bacc("TRN2", target_bir_lowering=False, num_devices=1, dynamic_dma_scratch_size=1024)
    arrays, args = {}, []
    for name in _INS:
        a = _np.ascontiguousarray(inputs[name])
        arrays[f"in_{name}_dram"] = a
        args.append(nc.dram_tensor(f"in_{name}_dram", a.shape, _mybir.dt.from_np(a.dtype), kind="ExternalInput").ap())
    o = nc.dram_tensor("out_0_dram", (1, T, D), _mybir.dt.float32, kind="ExternalOutput").ap()
    build(nc, *args, o, SIDE_USES)
    r = _run(nc, [arrays], core_ids=[0])
    return r.results[0]["out_0_dram"]
```
